# Optimizing a Trainium2 kernel written in Bass

```python
import math
import jax, jax.numpy as jnp
from jax import lax
import numpy as np

D_MODEL = 1024
BATCH = 1
SEQ = 512
DEPTH = 1

D_RNN = D_MODEL
RNN_HEADS = 8
RNN_BLOCK = D_RNN // RNN_HEADS
RNN_CONV = 4
RG_C = 8.0
ATT_HEADS = 8
HEAD_DIM = 128
ATT_WIDTH = ATT_HEADS * HEAD_DIM
Q_BLOCK = 128
D_FF = 3 * D_MODEL
FFN_CONV = 3
EPS = 1e-6
IN_SPLITS = (D_RNN, D_RNN, ATT_WIDTH, ATT_WIDTH, ATT_WIDTH, D_MODEL, D_MODEL)
D_IN = sum(IN_SPLITS)


def rmsnorm(x, g):
    x32 = x.astype(jnp.float32)
    y = x32 * lax.rsqrt(jnp.mean(x32 * x32, axis=-1, keepdims=True) + EPS)
    return (y * g.astype(jnp.float32)).astype(x.dtype)

def causal_dwconv(x, w, b):
    k_w = w.shape[0]
    s = x.shape[1]
    xp = jnp.pad(x, ((0, 0), (k_w - 1, 0), (0, 0)))
    out = b + w[0] * xp[:, 0:s]
    for k in range(1, k_w):
        out = out + w[k] * xp[:, k:k + s]
    return out

def rg_lru(x, wa, ba, wx, bx, lam):
    b_, s_, c_ = x.shape
    xh = x.reshape(b_, s_, RNN_HEADS, RNN_BLOCK)
    r = jax.nn.sigmoid(jnp.einsum('bshi,hij->bshj', xh, wa).reshape(b_, s_, c_) + ba)
    i = jax.nn.sigmoid(jnp.einsum('bshi,hij->bshj', xh, wx).reshape(b_, s_, c_) + bx)
    log_a = -RG_C * r.astype(jnp.float32) * jax.nn.softplus(-lam.astype(jnp.float32))
    a = jnp.exp(log_a)
    mult = jnp.sqrt(-jnp.expm1(2.0 * log_a))
    u = mult * (i * x).astype(jnp.float32)

    def step(h, inp):
        a_t, u_t = inp
        h = a_t * h + u_t
        return h, h

    h0 = jnp.zeros((b_, c_), jnp.float32)
    _, hs = lax.scan(step, h0, (jnp.swapaxes(a, 0, 1), jnp.swapaxes(u, 0, 1)))
    return jnp.swapaxes(hs, 0, 1).astype(x.dtype)

def head_rmsnorm(x, g):
    return rmsnorm(x, g)

def stick_breaking_attention(q, k, v):
    b_, s_, h_, d_ = q.shape
    nb = s_ // Q_BLOCK
    scale = 1.0 / math.sqrt(d_)
    kh = jnp.transpose(k, (0, 2, 1, 3))
    vh = jnp.transpose(v, (0, 2, 1, 3))
    qb = jnp.transpose(q.reshape(b_, nb, Q_BLOCK, h_, d_), (1, 0, 3, 2, 4))
    key_pos = jnp.arange(s_)

    def one_block(args):
        q_blk, blk = args
        q_pos = blk * Q_BLOCK + jnp.arange(Q_BLOCK)
        mask = key_pos[None, :] < q_pos[:, None]
        z = jnp.einsum('bhqd,bhkd->bhqk', q_blk, kh).astype(jnp.float32) * scale
        log_beta = jax.nn.log_sigmoid(z)
        log_1mb = jnp.where(mask, log_beta - z, 0.0)
        suffix = lax.cumsum(log_1mb, axis=3, reverse=True) - log_1mb
        attn = jnp.where(mask, jnp.exp(log_beta + suffix), 0.0)
        return jnp.einsum('bhqk,bhkd->bhqd', attn.astype(v.dtype), vh)

    out = lax.map(one_block, (qb, jnp.arange(nb)))
    return jnp.transpose(out, (1, 0, 3, 2, 4)).reshape(b_, s_, h_ * d_)

def first_inputs(seed: int = 0) -> dict:
    key = jax.random.key(seed)
    ks = jax.random.split(key, 24)
    n = jax.random.normal
    L, D = DEPTH, D_MODEL
    u = jax.random.uniform(ks[10], (L, D_RNN), minval=0.9, maxval=0.999)
    a0 = u ** (1.0 / RG_C)
    lam = jnp.log(a0) - jnp.log1p(-a0)
    return {
        "x": n(ks[0], (BATCH, SEQ, D), jnp.float32),
        "c": n(ks[1], (BATCH, D), jnp.float32),
        "ada_w": n(ks[2], (L, D, 6 * D), jnp.float32) * (0.5 * D ** -0.5),
        "ada_b": n(ks[3], (L, 6 * D), jnp.float32) * 0.01,
        "norm1_g": 1.0 + 0.05 * n(ks[4], (L, D), jnp.float32),
        "w_in": n(ks[5], (L, D, D_IN), jnp.float32) * D ** -0.5,
        "conv_w": n(ks[6], (L, RNN_CONV, D_RNN), jnp.float32) * RNN_CONV ** -0.5,
        "conv_b": n(ks[7], (L, D_RNN), jnp.float32) * 0.01,
        "rg_wa": n(ks[8], (L, RNN_HEADS, RNN_BLOCK, RNN_BLOCK), jnp.float32) * RNN_BLOCK ** -0.5,
        "rg_ba": n(ks[9], (L, D_RNN), jnp.float32) * 0.01,
        "rg_wx": n(ks[11], (L, RNN_HEADS, RNN_BLOCK, RNN_BLOCK), jnp.float32) * RNN_BLOCK ** -0.5,
        "rg_bx": n(ks[12], (L, D_RNN), jnp.float32) * 0.01,
        "rg_lambda": lam.astype(jnp.float32),
        "q_norm_g": 1.0 + 0.05 * n(ks[13], (L, HEAD_DIM), jnp.float32),
        "k_norm_g": 1.0 + 0.05 * n(ks[14], (L, HEAD_DIM), jnp.float32),
        "w_out": n(ks[15], (L, D, D), jnp.float32) * D ** -0.5,
        "norm2_g": 1.0 + 0.05 * n(ks[16], (L, D), jnp.float32),
        "ffn_up": n(ks[17], (L, D, 2 * D_FF), jnp.float32) * D ** -0.5,
        "ffn_conv_w": n(ks[18], (L, FFN_CONV, 2 * D_FF), jnp.float32) * FFN_CONV ** -0.5,
        "ffn_conv_b": n(ks[19], (L, 2 * D_FF), jnp.float32) * 0.01,
        "ffn_down": n(ks[20], (L, D_FF, D), jnp.float32) * D_FF ** -0.5,
    }

def first_block(x, c, ada_w, ada_b, norm1_g, w_in, conv_w, conv_b, rg_wa, rg_ba, rg_wx, rg_bx,
              rg_lambda, q_norm_g, k_norm_g, w_out, norm2_g, ffn_up, ffn_conv_w, ffn_conv_b,
              ffn_down):
    b_, s_, d_ = x.shape
    cuts = np.cumsum(IN_SPLITS)[:-1].tolist()
    for l in range(DEPTH):
        mod = c @ ada_w[l] + ada_b[l]
        sh1, sc1, gt1, sh2, sc2, gt2 = [m[:, None, :] for m in jnp.split(mod, 6, axis=-1)]

        h = rmsnorm(x, norm1_g[l]) * (1.0 + sc1) + sh1
        p = h @ w_in[l]
        xr, yr, q, k, v, ga, gb = jnp.split(p, cuts, axis=-1)

        xr = causal_dwconv(xr, conv_w[l], conv_b[l])
        y_a = rg_lru(xr, rg_wa[l], rg_ba[l], rg_wx[l], rg_bx[l], rg_lambda[l]) * jax.nn.gelu(yr)

        q = head_rmsnorm(q.reshape(b_, s_, ATT_HEADS, HEAD_DIM), q_norm_g[l])
        k = head_rmsnorm(k.reshape(b_, s_, ATT_HEADS, HEAD_DIM), k_norm_g[l])
        v = v.reshape(b_, s_, ATT_HEADS, HEAD_DIM)
        y_b = stick_breaking_attention(q, k, v)

        mix = jax.nn.sigmoid(ga) * y_a + jax.nn.sigmoid(gb) * y_b
        x = x + gt1 * (mix @ w_out[l])

        h2 = rmsnorm(x, norm2_g[l]) * (1.0 + sc2) + sh2
        up = causal_dwconv(h2 @ ffn_up[l], ffn_conv_w[l], ffn_conv_b[l])
        g_ff, v_ff = jnp.split(up, 2, axis=-1)
        x = x + gt2 * ((jax.nn.gelu(g_ff) * v_ff) @ ffn_down[l])
    return x


CHUNK = 64
LEFT_CHUNKS = 8
BAND = LEFT_CHUNKS + 1
EPS_2 = 1e-5
D_FF_2 = 2816
SSD_HEADS = 16
SSD_HEAD_DIM = 64
SSD_INNER = SSD_HEADS * SSD_HEAD_DIM
SSD_GROUPS = 2
SSD_STATE = 128
CONV_WIDTH = 4
CONV_DIM = SSD_INNER + 2 * SSD_GROUPS * SSD_STATE
ATT_HEAD_DIM = 64
ATT_INNER = ATT_HEADS * ATT_HEAD_DIM
MAX_REL = 256
MIX_WIDTH = SSD_INNER + ATT_INNER
PROJ_DIM = SSD_INNER + CONV_DIM + SSD_HEADS + 3 * ATT_INNER


def rms_norm(x, w):
    xf = x.astype(jnp.float32)
    y = xf * lax.rsqrt(jnp.mean(xf * xf, axis=-1, keepdims=True) + EPS_2)
    return (y * w.astype(jnp.float32)).astype(x.dtype)

def swiglu(h, w_gate, w_up, w_down):
    return (jax.nn.silu(h @ w_gate) * (h @ w_up)) @ w_down

def causal_depthwise_conv(u, w, b):
    k = w.shape[0]
    out = lax.conv_general_dilated(
        u, w.astype(u.dtype)[:, None, :], window_strides=(1,), padding=[(k - 1, 0)],
        dimension_numbers=('NWC', 'WIO', 'NWC'), feature_group_count=u.shape[-1])
    return out + b.astype(u.dtype)

def ssd_chunked(xs, dt, a, bmat, cmat, d_skip):
    bsz, seqlen, n_heads, hd = xs.shape
    n_groups, n_state = bmat.shape[-2], bmat.shape[-1]
    m = n_heads // n_groups
    nc = seqlen // CHUNK
    xf = xs.astype(jnp.float32)
    xdt = (xf * dt[..., None]).reshape(bsz, nc, CHUNK, n_groups, m, hd)
    a_cs = jnp.cumsum((dt * a).reshape(bsz, nc, CHUNK, n_groups, m), axis=2)
    bc = bmat.astype(jnp.float32).reshape(bsz, nc, CHUNK, n_groups, n_state)
    cc = cmat.astype(jnp.float32).reshape(bsz, nc, CHUNK, n_groups, n_state)
    causal = jnp.tril(jnp.ones((CHUNK, CHUNK), dtype=bool))[:, :, None, None]
    seg = a_cs[:, :, :, None] - a_cs[:, :, None, :]
    decay = jnp.exp(jnp.where(causal, seg, -jnp.inf))
    cb = jnp.einsum('bclgn,bcsgn->bclsg', cc, bc)
    y_diag = jnp.einsum('bclsg,bclsgm,bcsgmp->bclgmp', cb, decay, xdt)
    decay_out = jnp.exp(a_cs[:, :, -1:] - a_cs)
    states = jnp.einsum('bclgn,bclgm,bclgmp->bcgmpn', bc, decay_out, xdt)
    chunk_decay = jnp.exp(a_cs[:, :, -1])

    def step(h, inp):
        s_c, d_c = inp
        return h * d_c[..., None, None] + s_c, h

    h0 = jnp.zeros((bsz, n_groups, m, hd, n_state), jnp.float32)
    _, prev = lax.scan(step, h0, (jnp.moveaxis(states, 1, 0), jnp.moveaxis(chunk_decay, 1, 0)))
    prev = jnp.moveaxis(prev, 0, 1)
    y_off = jnp.einsum('bclgn,bcgmpn,bclgm->bclgmp', cc, prev, jnp.exp(a_cs))
    y = (y_diag + y_off).reshape(bsz, seqlen, n_heads, hd)
    return y + xf * d_skip.astype(jnp.float32)[:, None]

def chunked_rel_attention(q, k, v, rel_bias):
    bsz, seqlen, n_heads, hd = q.shape
    nc = seqlen // CHUNK
    qc = q.reshape(bsz, nc, CHUNK, n_heads, hd)
    pad = ((0, 0), (LEFT_CHUNKS * CHUNK, 0), (0, 0), (0, 0))
    kp = jnp.pad(k, pad).reshape(bsz, nc + LEFT_CHUNKS, CHUNK, n_heads, hd)
    vp = jnp.pad(v, pad).reshape(bsz, nc + LEFT_CHUNKS, CHUNK, n_heads, hd)
    kb = jnp.stack([kp[:, o:o + nc] for o in range(BAND)], axis=2).reshape(bsz, nc, BAND * CHUNK, n_heads, hd)
    vb = jnp.stack([vp[:, o:o + nc] for o in range(BAND)], axis=2).reshape(bsz, nc, BAND * CHUNK, n_heads, hd)
    qpos = LEFT_CHUNKS * CHUNK + jnp.arange(CHUNK)
    kpos = jnp.arange(BAND * CHUNK)
    rel = jnp.clip(qpos[:, None] - kpos[None, :], -MAX_REL, MAX_REL) + MAX_REL
    bias = rel_bias.astype(jnp.float32)[:, rel]
    s = jnp.einsum('bcqhd,bckhd->bhcqk', qc, kb).astype(jnp.float32) * (hd ** -0.5) + bias[None, :, None]
    valid = (jnp.arange(nc)[:, None] - LEFT_CHUNKS + jnp.arange(BAND)[None, :]) >= 0
    valid = jnp.repeat(valid, CHUNK, axis=1)
    s = jnp.where(valid[None, None, :, None, :], s, jnp.finfo(jnp.float32).min)
    p = jax.nn.softmax(s, axis=-1).astype(v.dtype)
    o = jnp.einsum('bhcqk,bckhd->bcqhd', p, vb)
    return o.reshape(bsz, seqlen, n_heads * hd)

def hybrid_mixer(x, mix_norm, w_in, conv_w, conv_b, dt_bias, a_log, d_skip, ssd_norm, rel_bias, w_out):
    bsz, seqlen, _ = x.shape
    h = rms_norm(x, mix_norm)
    proj = h @ w_in
    o1 = SSD_INNER
    o2 = o1 + CONV_DIM
    o3 = o2 + SSD_HEADS
    o4 = o3 + ATT_INNER
    o5 = o4 + ATT_INNER
    z, xbc, dt_raw = proj[..., :o1], proj[..., o1:o2], proj[..., o2:o3]
    q, k, v = proj[..., o3:o4], proj[..., o4:o5], proj[..., o5:]
    xbc = jax.nn.silu(causal_depthwise_conv(xbc, conv_w, conv_b))
    gn = SSD_GROUPS * SSD_STATE
    xs = xbc[..., :SSD_INNER].reshape(bsz, seqlen, SSD_HEADS, SSD_HEAD_DIM)
    bm = xbc[..., SSD_INNER:SSD_INNER + gn].reshape(bsz, seqlen, SSD_GROUPS, SSD_STATE)
    cm = xbc[..., SSD_INNER + gn:].reshape(bsz, seqlen, SSD_GROUPS, SSD_STATE)
    dt = jax.nn.softplus(dt_raw.astype(jnp.float32) + dt_bias.astype(jnp.float32))
    a = -jnp.exp(a_log.astype(jnp.float32))
    y = ssd_chunked(xs, dt, a, bm, cm, d_skip).reshape(bsz, seqlen, SSD_INNER)
    y = rms_norm(y * jax.nn.silu(z.astype(jnp.float32)), ssd_norm).astype(x.dtype)
    att = chunked_rel_attention(
        q.reshape(bsz, seqlen, ATT_HEADS, ATT_HEAD_DIM),
        k.reshape(bsz, seqlen, ATT_HEADS, ATT_HEAD_DIM),
        v.reshape(bsz, seqlen, ATT_HEADS, ATT_HEAD_DIM), rel_bias).astype(x.dtype)
    return jnp.concatenate([y, att], axis=-1) @ w_out

def second_inputs(seed: int = 0) -> dict:
    key = jax.random.key(seed)
    ks = jax.random.split(key, 24)

    def nrm(k, shape, scale):
        return jax.random.normal(k, shape, jnp.float32) * scale

    def gain(k, n):
        return 1.0 + nrm(k, (DEPTH, n), 0.02)

    u = jax.random.uniform(ks[10], (DEPTH, SSD_HEADS), jnp.float32)
    dt0 = jnp.exp(u * (np.log(0.1) - np.log(0.001)) + np.log(0.001))
    dt_bias = dt0 + jnp.log(-jnp.expm1(-dt0))
    a_log = jnp.log(jax.random.uniform(ks[11], (DEPTH, SSD_HEADS), jnp.float32, 1.0, 16.0))
    return {
        "x": nrm(ks[0], (BATCH, SEQ, D_MODEL), 1.0),
        "ffn1_norm": gain(ks[1], D_MODEL),
        "ffn1_w_gate": nrm(ks[2], (DEPTH, D_MODEL, D_FF_2), D_MODEL ** -0.5),
        "ffn1_w_up": nrm(ks[3], (DEPTH, D_MODEL, D_FF_2), D_MODEL ** -0.5),
        "ffn1_w_down": nrm(ks[4], (DEPTH, D_FF_2, D_MODEL), D_FF_2 ** -0.5),
        "mix_norm": gain(ks[5], D_MODEL),
        "w_in": nrm(ks[6], (DEPTH, D_MODEL, PROJ_DIM), D_MODEL ** -0.5),
        "conv_w": nrm(ks[7], (DEPTH, CONV_WIDTH, CONV_DIM), CONV_WIDTH ** -0.5),
        "conv_b": nrm(ks[8], (DEPTH, CONV_DIM), 0.02),
        "dt_bias": dt_bias,
        "a_log": a_log,
        "d_skip": 1.0 + nrm(ks[12], (DEPTH, SSD_HEADS), 0.1),
        "ssd_norm": gain(ks[13], SSD_INNER),
        "rel_bias": nrm(ks[14], (DEPTH, ATT_HEADS, 2 * MAX_REL + 1), 0.1),
        "w_out": nrm(ks[15], (DEPTH, MIX_WIDTH, D_MODEL), MIX_WIDTH ** -0.5),
        "ffn2_norm": gain(ks[16], D_MODEL),
        "ffn2_w_gate": nrm(ks[17], (DEPTH, D_MODEL, D_FF_2), D_MODEL ** -0.5),
        "ffn2_w_up": nrm(ks[18], (DEPTH, D_MODEL, D_FF_2), D_MODEL ** -0.5),
        "ffn2_w_down": nrm(ks[19], (DEPTH, D_FF_2, D_MODEL), D_FF_2 ** -0.5),
        "final_norm": 1.0 + nrm(ks[20], (D_MODEL,), 0.02),
    }

def second_block(x, ffn1_norm, ffn1_w_gate, ffn1_w_up, ffn1_w_down, mix_norm, w_in, conv_w, conv_b,
              dt_bias, a_log, d_skip, ssd_norm, rel_bias, w_out, ffn2_norm, ffn2_w_gate, ffn2_w_up,
              ffn2_w_down, final_norm):
    for i in range(DEPTH):
        x = x + 0.5 * swiglu(rms_norm(x, ffn1_norm[i]), ffn1_w_gate[i], ffn1_w_up[i], ffn1_w_down[i])
        x = x + hybrid_mixer(x, mix_norm[i], w_in[i], conv_w[i], conv_b[i], dt_bias[i], a_log[i],
                             d_skip[i], ssd_norm[i], rel_bias[i], w_out[i])
        x = x + 0.5 * swiglu(rms_norm(x, ffn2_norm[i]), ffn2_w_gate[i], ffn2_w_up[i], ffn2_w_down[i])
    return rms_norm(x, final_norm)


def setup_inputs(seed=0):
    out = dict(first_inputs(seed))
    for name, value in second_inputs(seed + 1).items():
        if name != "x":
            out[name + "_2"] = value
    return out


def reference(
    x, c, ada_w, ada_b, norm1_g, w_in, conv_w, conv_b, rg_wa, rg_ba, rg_wx, rg_bx, rg_lambda,
    q_norm_g, k_norm_g, w_out, norm2_g, ffn_up, ffn_conv_w, ffn_conv_b, ffn_down, ffn1_norm_2,
    ffn1_w_gate_2, ffn1_w_up_2, ffn1_w_down_2, mix_norm_2, w_in_2, conv_w_2, conv_b_2,
    dt_bias_2, a_log_2, d_skip_2, ssd_norm_2, rel_bias_2, w_out_2, ffn2_norm_2, ffn2_w_gate_2,
    ffn2_w_up_2, ffn2_w_down_2, final_norm_2,
):
    x = first_block(
        x, c, ada_w, ada_b, norm1_g, w_in, conv_w, conv_b, rg_wa, rg_ba, rg_wx, rg_bx,
        rg_lambda, q_norm_g, k_norm_g, w_out, norm2_g, ffn_up, ffn_conv_w, ffn_conv_b, ffn_down,
    )
    return second_block(
        x, ffn1_norm_2, ffn1_w_gate_2, ffn1_w_up_2, ffn1_w_down_2, mix_norm_2, w_in_2, conv_w_2,
        conv_b_2, dt_bias_2, a_log_2, d_skip_2, ssd_norm_2, rel_bias_2, w_out_2, ffn2_norm_2,
        ffn2_w_gate_2, ffn2_w_up_2, ffn2_w_down_2, final_norm_2,
    )


_drawn_inputs = setup_inputs


def setup_inputs(seed=0):
    import zlib

    import numpy as np

    out = dict(_drawn_inputs(seed))
    spreads = {}
    factors = {'conv_b': 4.909,
     'rg_ba': 37.598,
     'rg_bx': 8.0,
     'q_norm_g': 8.0,
     'k_norm_g': 8.0,
     'ffn_conv_b': 8.0,
     'ffn1_norm_2': 7.065,
     'mix_norm_2': 11.895,
     'conv_b_2': 29.282,
     'ssd_norm_2': 121.722,
     'rel_bias_2': 36.23,
     'ffn2_norm_2': 30.112,
     'final_norm_2': 22.394,
     'd_skip_2': 64.0}
    for name, (base, spread) in spreads.items():
        noise = np.random.default_rng([zlib.crc32(name.encode()), seed]).standard_normal(out[name].shape)
        drawn = base * np.exp(spread * noise) if base else spread * noise
        out[name] = __import__('jax').numpy.asarray(drawn.astype(out[name].dtype))
    for name, factor in factors.items():
        out[name] = (out[name] * factor).astype(out[name].dtype)
    return out
```

```python
import numpy as np
import concourse.bass as bass
from concourse import mybir
from contextlib import ExitStack

F32 = mybir.dt.float32
BF16 = mybir.dt.bfloat16
ACT = mybir.ActivationFunctionType
ALU = mybir.AluOpType
AX = mybir.AxisListType

P = 128
S = 512
D = 1024
KD = D // P
HEADS = 8
NJ1 = 3 * D // P
NJ2 = 2816 // P
NT = S // P
RING = 4
BLOCKS = 8
UNIT = BLOCKS * P
ARENA_COLS = 36 * S
EPS1 = 1e-6
EPS2 = 1e-5
NEG = -1e30

SEG_OFF = [0, 512, 1024, 896]
SEG_BANK = [(0, 0), (1, 0), (2, 0), (1, 384)]
SEG_W = [S - P * i for i in range(NT)]
BANK_PART = [(0, 512, 0), (1, 512, 512), (2, 256, 1024)]
TRI = 1280

U_ADA = 0
U_HEAD = U_ADA + 16
HEAD_UNITS = 12
U_OUT1 = U_HEAD + HEADS * HEAD_UNITS
U_UP1 = U_OUT1 + 8
U_DN1 = U_UP1 + 2 * NJ1
U_UPA = U_DN1 + 24
U_DNA = U_UPA + 2 * NJ2
U_BC = U_DNA + 24
U_PAIR = U_BC + 5
PAIR_UNITS = 8
U_OUT2 = U_PAIR + 4 * PAIR_UNITS
U_UPB = U_OUT2 + 12
U_DNB = U_UPB + 2 * NJ2
N_UNITS = U_DNB + 24

VEC_SIZES = [("c", 8), ("ada_b", 48), ("norm1_g", 8), ("conv_w", 32), ("conv_b", 8), ("rg_ba", 8),
             ("rg_bx", 8), ("rg_lambda", 8), ("q_norm_g", 1), ("k_norm_g", 1), ("norm2_g", 8),
             ("ffn_conv_w", 3 * 48), ("ffn_conv_b", 48), ("ffn1_norm_2", 8), ("mix_norm_2", 8),
             ("conv_w_2", 48), ("conv_b_2", 12), ("d_skip_2", 8), ("ssd_norm_2", 8),
             ("ffn2_norm_2", 8), ("final_norm_2", 8), ("dt_bias_2", 1), ("a_log_2", 1)]
VEC = {}
_at = 0
for _name, _n in VEC_SIZES:
    VEC[_name] = _at
    _at += _n
N_VEC = _at


def program(nc, xt_in, vec_in, stream, out):
    ctx = ExitStack()
    with ctx:
        def sb(name, shape, dt=F32):
            return ctx.enter_context(nc.sbuf_tensor(name, shape, dt))

        def sem(name):
            return ctx.enter_context(nc.semaphore(name))

        XT = sb("XT", [P, KD * S])
        HT = sb("HT", [P, KD * S])
        MIX = sb("MIX", [P, 12 * S])
        ARENA = sb("ARENA", [P, ARENA_COLS])
        ring = sb("ring", [P, RING, UNIT])
        vec = sb("vec", [P, N_VEC])
        MOD = sb("MOD", [P, 48])
        G1 = sb("G1", [P, KD])
        G2 = sb("G2", [P, KD])
        c8 = sb("c8", [P, HEADS])
        nc8 = sb("nc8", [P, HEADS])
        lam_t = sb("lam_t", [P, 3 * HEADS])
        qg = sb("qg", [P, 1])
        aneg = sb("aneg", [P, 1])
        eps1 = sb("eps1", [P, 1])
        eps2 = sb("eps2", [P, 1])
        one = sb("one", [P, 1])
        zero = sb("zero", [P, 1])
        ones = sb("ones", [P, P])
        negones = sb("negones", [P, P])
        negtri = sb("negtri", [P, P])
        ident = sb("ident", [P, P])
        identb = sb("identb", [P, P], BF16)
        strictb = sb("strictb", [P, P], BF16)
        chunkb = sb("chunkb", [P, P], BF16)
        SS = sb("SS", [P, S])
        SQ = sb("SQ", [P, S])
        RT = sb("RT", [P, S])
        RS = sb("RS", [P, S])
        TG = sb("TG", [P, 2, S])
        CG = sb("CG", [P, 2, S])
        CV = sb("CV", [P, 2, S])

        def arena():
            at = [0]

            def take(n):
                at[0] += n
                assert at[0] <= ARENA_COLS, at[0]
                return ARENA[:, at[0] - n:at[0]]
            return take

        def mixer1_tiles():
            t = arena()
            d = {n: t(S) for n in "QR QSQ KR KSQ RQ RK RSQ RSK QN KN VT GY SGA SGB XC RG IG AD TH A2 M2 ML IX U HS YA YB".split()}
            d["XR"] = t(S + 4)[:, 0:S + 3]
            for n in ("AZ", "PP", "AT"):
                d[n] = t(TRI)
            d["EZ"] = d["LP"] = d["AZ"]
            return d

        def mixer2_tiles():
            t = arena()
            d = {}
            d["BT"] = t(2 * S)
            d["CT"] = t(2 * S)
            d["GS"] = t(2 * TRI)
            d["CS"] = t(S)
            for n in ("ED0", "ED1", "SC"):
                d[n] = t(TRI)
            d["PT"] = t(TRI)
            d["Q2"] = t(S)
            d["K2"] = t(S)
            d["V2"] = t(S)
            d["DTT"] = t(64)
            d["CST"] = t(64)
            d["mx"] = t(4)
            d["nmx"] = t(4)
            d["sm"] = t(4)
            d["rsm"] = t(4)
            d["DT"] = d["Q2"]
            d["DZ"] = d["K2"]
            d["DE"] = d["V2"]
            d["LA"] = d["SC"][:, 0:S]
            d["BC"] = d["ED0"][:, 0:S]
            d["XS"] = [CG[:, 0, :], CG[:, 1, :]]
            d["ZS"] = [TG[:, 0, :], TG[:, 1, :]]
            d["XD"] = [CV[:, 0, :], CV[:, 1, :]]
            d["YY"] = t(S)
            d["SELH"] = t(2 * P)
            return d

        bank = [ctx.enter_context(nc.psum_tensor(f"bank{b}", [P, S], F32)) for b in range(8)]

        def v(name, k=0, n=1):
            return vec[:, VEC[name] + k:VEC[name] + k + n]

        def vd(name, k):
            return vec[:, bass.ds(k + VEC[name], 1)]

        def tile_of(T, m):
            return T[:, m * S:(m + 1) * S] if isinstance(m, int) else T[:, bass.ds(m * S, S)]

        def seg_bank(first, i, lo=0):
            b, c = SEG_BANK[i]
            return bank[first[b]][:, c + lo:c + SEG_W[i]]

        arrived = [sem(f"arrived{s}") for s in range(RING)]
        unit_done = sem("unit_done")
        vec_in_s = sem("vec_in_s")
        x_in_s = sem("x_in_s")
        out_s = sem("out_s")
        consts = sem("consts")
        pool_step = sem("pool_step")
        prep_a = sem("prep_a")
        prep_v = sem("prep_v")
        mod_done = sem("mod_done")
        res_done = sem("res_done")
        sq_done = sem("sq_done")
        ss_done = sem("ss_done")
        ss_clear = sem("ss_clear")
        ms_done = sem("ms_done")
        rt_done = sem("rt_done")
        rs_done = sem("rs_done")
        h_mul = sem("h_mul")
        h_add = sem("h_add")
        up_act = sem("up_act")
        ff_done = sem("ff_done")

        N_RES = 6

        names = ("q_evac k_evac v_evac xr_evac q_ms k_ms rq_done rk_done rsq rsk qn_done kn_done "
                 "gy_done conv_done z_done absz_done ez_done lnp_done p_done s_done att_done pv_done "
                 "sga_done sgb_done r_mm i_mm rg_sig ig_sig a_dec th_dec a2_done m2_done mult_done "
                 "ix_done u_done scan_done ya_done yb_done mix_done").split()
        q = {n: sem("m1_" + n) for n in names}
        cgv_act = sem("cgv_act")
        cg_dve = sem("cg_dve")
        cv_dve = sem("cv_dve")
        names = ("bc_conv bc_tap bc_silu dt_z dt_abs dt_exp dt_ln dt_sp dt_la cs_done tr_dt tr_evac "
                 "g_mm g_evac g_mask xs_conv xs_tap xs_silu xs_tr xd_done sel_done csb_done "
                 "dd_done ed_done mm_done y_mm y_skip z_silu yz_done yss_done qk_evac v_evac "
                 "s_mm s_add s_max s_neg s_exp s_rec s_nrm t_mm t_evac o_evac "
                 "yms yrt yrs ynorm").split()
        r = {n: sem("m2_" + n) for n in names}

        block = ctx.enter_context(nc.Block())

        @block.sync
        def _(sp):
            sp.dma_start(vec[:, :], vec_in).then_inc(vec_in_s, 16)
            sp.dma_start(XT[:, :], xt_in).then_inc(x_in_s, 16)
            for s in range(RING):
                sp.dma_start(ring[:, s, :], stream[s]).then_inc(arrived[s], 16)
            full = N_UNITS // RING
            with sp.Fori(1, full) as i:
                for s in range(RING):
                    sp.wait_ge(unit_done, (i - 1) * RING + s + 1)
                    sp.dma_start(ring[:, s, :], stream[bass.ds(i * RING + s, 1)].rearrange("a p n -> (a p) n")).then_inc(arrived[s], 16)
            for u in range(full * RING, N_UNITS):
                sp.wait_ge(unit_done, u - RING + 1)
                sp.dma_start(ring[:, u % RING, :], stream[u]).then_inc(arrived[u % RING], 16)
            sp.wait_ge(h_mul, 8 * N_RES)
            sp.dma_start(out, HT[:, :]).then_inc(out_s, 16)
            sp.wait_ge(out_s, 16)

        @block.gpsimd
        def _(pool):
            n = [0]

            def step(ins):
                n[0] += 1
                ins.then_inc(pool_step, 1)
                pool.wait_ge(pool_step, n[0])

            def keep(t, cmp, fill, pattern, mult, base=0):
                step(nc.gpsimd.affine_select(out=t, in_=t, compare_op=cmp, fill=fill, base=base,
                                             pattern=pattern, channel_multiplier=mult))

            for t, value in ((ones, 1.0), (negones, -1.0), (negtri, -1.0), (ident, 0.0),
                             (identb, 0.0), (strictb, NEG), (chunkb, NEG)):
                step(nc.gpsimd.memset(t[:, :], value))
            keep(negtri[:, :], ALU.is_ge, 0.0, [[-1, P]], 1)
            keep(strictb[:, :], ALU.is_ge, 0.0, [[-1, P]], 1)
            keep(ident[:, :], ALU.not_equal, 1.0, [[-1, P]], 1)
            keep(identb[:, :], ALU.not_equal, 1.0, [[-1, P]], 1)
            keep(chunkb[:, :], ALU.is_ge, 0.0, [[0, P]], -1, base=63)
            keep(chunkb[:, :], ALU.is_ge, 0.0, [[1, P]], 0, base=-64)
            pool.sem_inc(consts, 1)
            GS = mixer2_tiles()["GS"]
            for g in range(2):
                pool.wait_ge(r["g_evac"], 3 * (g + 1))
                for i in range(NT):
                    at = g * TRI + SEG_OFF[i]
                    ins = nc.gpsimd.affine_select(out=GS[:, at:at + P], in_=GS[:, at:at + P],
                                                  compare_op=ALU.is_ge, fill=0.0, base=0,
                                                  pattern=[[1, P]], channel_multiplier=-1)
                    ins.then_inc(r["g_mask"], 1)

        @block.tensor
        def _(pe):
            mm = nc.tensor.matmul

            def unit_wait(base, loc, i=0, stride=0):
                u = base + loc
                pe.wait_ge(arrived[u % RING], 16 * (u // RING + 1) + i * (16 * (stride // RING)))

            def blk(base, loc, b, n=1):
                return ring[:, (base + loc) % RING, b * P:(b + n) * P]

            def project(out_ap, base, loc, i=0, stride=0, done=True):
                unit_wait(base, loc, i, stride)
                for k in range(KD):
                    last = mm(out_ap, blk(base, loc, k), tile_of(HT, k), start=(k == 0), stop=(k == KD - 1))
                if done:
                    last.then_inc(unit_done, 1)

            def project_tokens(out_bank, base, loc, i=0, stride=0):
                unit_wait(base, loc, i, stride)
                for t in range(NT):
                    for k in range(KD):
                        last = mm(out_bank[:, t * P:(t + 1) * P], HT[:, k * S + t * P:k * S + (t + 1) * P],
                                  blk(base, loc, k), start=(k == 0), stop=(k == KD - 1))
                last.then_inc(unit_done, 1)

            def sum_squares(n):
                pe.wait_ge(ss_done, 8 * (n + 1))
                mm(bank[7][:, :], ones[:, :], SS[:, :], start=True, stop=True).then_inc(ms_done, 1)

            def ada(col, base, loc, i=0, stride=0):
                unit_wait(base, loc, i, stride)
                for k in range(KD):
                    out_ap = bank[6][:, col:col + 1] if isinstance(col, int) else bank[6][:, bass.ds(col, 1)]
                    last = mm(out_ap, blk(base, loc, k), v("c", k), start=(k == 0), stop=(k == KD - 1))
                last.then_inc(unit_done, 1)

            pe.wait_ge(consts, 1)
            sum_squares(0)
            pe.wait_ge(vec_in_s, 16)
            with pe.Fori(0, 4) as i:
                for j in range(4):
                    ada(i * 4 + j, U_ADA, j, i, 4)
            pe.wait_ge(h_add, 8)

            M = mixer1_tiles()
            with pe.Fori(0, HEADS) as h:
                def proj(b, loc):
                    project(bank[b][:, :], U_HEAD, loc, h, HEAD_UNITS)
                pe.wait_ge(q["sgb_done"], h + 1)
                proj(0, 0)
                pe.wait_ge(q["rg_sig"], h + 1)
                proj(1, 1)
                pe.wait_ge(q["ig_sig"], h + 1)
                project_tokens(bank[5], U_HEAD, 2, h, HEAD_UNITS)
                pe.wait_ge(q["yb_done"], h + 1)
                proj(7, 3)
                pe.wait_ge(q["q_evac"], 2 * h + 2)
                mm(bank[0][:, :], ones[:, :], M["QSQ"], start=True, stop=True).then_inc(q["q_ms"], 1)
                pe.wait_ge(q["k_evac"], 2 * h + 2)
                mm(bank[1][:, :], ones[:, :], M["KSQ"], start=True, stop=True).then_inc(q["k_ms"], 1)
                pe.wait_ge(q["v_evac"], h + 1)
                proj(5, 4)
                pe.wait_ge(q["qn_done"], h + 1)
                pe.wait_ge(q["kn_done"], h + 1)
                for i in (0, 1, 3, 2):
                    mm(seg_bank((2, 3, 4), i), M["KN"][:, i * P:(i + 1) * P], M["QN"][:, i * P:S],
                       start=(i != 3), stop=False, skip_group_check=True)
                    b, c = SEG_BANK[i]
                    last = mm(bank[2 + b][:, c:c + P], identb[:, :], strictb[:, :], start=False,
                              stop=False, skip_group_check=True)
                last.then_inc(q["z_done"], 1)
                pe.wait_ge(q["xr_evac"], h + 1)
                proj(7, 5)
                pe.wait_ge(q["rq_done"], h + 1)
                proj(0, 6)
                pe.wait_ge(q["p_done"], 3 * h + 3)
                for i in range(NT):
                    for j in range(i, NT):
                        last = mm(seg_bank((2, 3, 4), i, (j - i) * P), (negtri if i == j else negones)[:, :],
                                  M["PP"][:, SEG_OFF[j]:SEG_OFF[j] + SEG_W[j]], start=False,
                                  stop=(i == NT - 1), skip_group_check=True)
                last.then_inc(q["s_done"], 1)
                unit_wait(U_HEAD, 7, h, HEAD_UNITS)
                pe.wait_ge(q["conv_done"], 4 * h + 4)
                pe.wait_ge(q["rk_done"], h + 1)
                mm(bank[1][:, :], blk(U_HEAD, 7, 0), M["XC"], start=True, stop=True).then_inc(q["r_mm"], 1)
                pe.wait_ge(q["gy_done"], h + 1)
                mm(bank[5][:, :], blk(U_HEAD, 7, 1), M["XC"], start=True, stop=True).then_inc(unit_done, 1)
                for j in range(4):
                    ada(h * 4 + 16 + j, U_HEAD, 8 + j, h, HEAD_UNITS)
                pe.wait_ge(q["att_done"], 3 * h + 3)
                pe.wait_ge(q["sga_done"], h + 1)
                for i in range(NT):
                    last = mm(bank[7][:, i * P:S], M["VT"][:, i * P:(i + 1) * P],
                              M["AT"][:, SEG_OFF[i]:SEG_OFF[i] + SEG_W[i]], start=(i == 0), stop=(i == NT - 1))
                last.then_inc(q["pv_done"], 1)

            pe.wait_ge(q["mix_done"], HEADS)
            with pe.Fori(0, 2) as i:
                for m in range(4):
                    pe.wait_ge(res_done, i * 4 + (8 + m - 3))
                    unit_wait(U_OUT1, m, i, 4)
                    for k in range(KD):
                        last = mm(bank[m][:, :], blk(U_OUT1, m, k), tile_of(MIX, k), start=(k == 0), stop=(k == KD - 1))
                    last.then_inc(unit_done, 1)

            def ffn(u_up, u_dn, nj, before, n_res, conv):
                with pe.Fori(0, nj // 2) as i:
                    for jl in range(2):
                        if conv:
                            pe.wait_ge(cg_dve, i * 4 + (2 * jl + 2))
                        else:
                            pe.wait_ge(up_act, i * 2 + (before + jl + 1))
                        project(bank[2 * jl][:, :], u_up, 2 * jl, i, 4)
                        if conv:
                            pe.wait_ge(cv_dve, i * 4 + (2 * jl + 2))
                        else:
                            pe.wait_ge(ff_done, i * 2 + (before + jl + 1))
                        project(bank[2 * jl + 1][:, :], u_up, 2 * jl + 1, i, 4)
                pe.wait_ge(ff_done, 2 + before + nj)
                with pe.Fori(0, 2) as i:
                    for m in range(4):
                        pe.wait_ge(res_done, i * 4 + (8 * n_res + m - 3))
                        for n in range(3):
                            unit_wait(u_dn, 3 * m + n, i, 12)
                            for k in range(n * BLOCKS, min((n + 1) * BLOCKS, nj)):
                                last = mm(bank[4 + m][:, :], blk(u_dn, 3 * m + n, k - n * BLOCKS),
                                          tile_of(ARENA, k), start=(k == 0), stop=(k == nj - 1))
                            last.then_inc(unit_done, 1)

            sum_squares(1)
            pe.wait_ge(h_add, 16)
            ffn(U_UP1, U_DN1, NJ1, 0, 2, True)
            sum_squares(2)
            pe.wait_ge(h_mul, 24)
            ffn(U_UPA, U_DNA, NJ2, NJ1, 3, False)
            sum_squares(3)
            pe.wait_ge(h_mul, 32)

            N = mixer2_tiles()
            for n in range(4):
                project(bank[n][:, :], U_BC, n)
            project(bank[4][:, :], U_BC, 4)
            pe.wait_ge(r["dt_sp"], 1)
            for t in range(NT):
                mm(bank[5][:, t * 16:(t + 1) * 16], N["DT"][:, t * P:(t + 1) * P], ident[:, 0:16], start=True, stop=True)
            pe.wait_ge(r["cs_done"], 1)
            for t in range(NT):
                last = mm(bank[5][:, 64 + t * 16:64 + (t + 1) * 16], N["CS"][:, t * P:(t + 1) * P], ident[:, 0:16],
                          start=True, stop=True)
            last.then_inc(r["tr_dt"], 1)
            for g in range(2):
                pe.wait_ge(r["bc_silu"], 4)
                if g:
                    pe.wait_ge(r["g_evac"], 3)
                for i in (0, 1, 3, 2):
                    last = mm(seg_bank((0, 1, 2), i), N["BT"][:, g * S + i * P:g * S + (i + 1) * P],
                              N["CT"][:, g * S + i * P:(g + 1) * S], start=(i != 3), stop=True, skip_group_check=True)
                last.then_inc(r["g_mm"], 1)
            pe.wait_ge(r["g_evac"], 6)
            pe.wait_ge(r["tr_evac"], 2)

            with pe.Fori(0, 4) as t:
                def proj(b, loc):
                    project(bank[b][:, :], U_PAIR, loc, t, PAIR_UNITS)

                def source_rows(a, b):
                    pe.wait_ge(r["xs_silu"], 2 * t + a + 1)
                    for i in range(NT):
                        last = nc.tensor.transpose(bank[b][:, i * P:(i + 1) * P], N["XS"][a][:, i * P:(i + 1) * P], ident[:, :])
                    last.then_inc(r["xs_tr"], 1)

                def spread_cs(a, hh, b):
                    pe.wait_ge(r["sel_done"], 4 * t + 2 * a + hh + 1)
                    mm(bank[b][:, :], N["SELH"][:, hh * P:(hh + 1) * P], N["CS"], start=True, stop=True).then_inc(r["csb_done"], 1)

                def head_y(a, hh, b):
                    pe.wait_ge(r["mm_done"], 4 * t + 2 * a + hh + 1)
                    for i in range(NT):
                        last = mm(bank[b][hh * 64:(hh + 1) * 64, i * P:S], N["XD"][a][:, i * P + hh * 64:i * P + (hh + 1) * 64],
                                  N[f"ED{hh}"][:, SEG_OFF[i]:SEG_OFF[i] + SEG_W[i]], start=(i == 0), stop=(i == NT - 1))
                    last.then_inc(r["y_mm"], 1)

                def scores(hh):
                    for i in (3, 2, 0, 1):
                        b, c = SEG_BANK[3 - i]
                        b = (5, 6, 0)[b]
                        w = (i + 1) * P
                        mm(bank[b][:, c:c + w], N["Q2"][hh * 64:(hh + 1) * 64, i * P:(i + 1) * P],
                           N["K2"][hh * 64:(hh + 1) * 64, 0:w], start=(i != 0), stop=False, skip_group_check=True)
                        last = mm(bank[b][:, c + w - P:c + w], identb[:, :], chunkb[:, :], start=False, stop=True,
                                  skip_group_check=True)
                    last.then_inc(r["s_mm"], 1)

                def turn(hh):
                    pe.wait_ge(r["s_nrm"], 8 * t + 4 * hh + 4)
                    if hh:
                        unit_wait(U_PAIR, 7, t, PAIR_UNITS)
                    for j in range(NT):
                        for i in range(j, NT):
                            b, c = SEG_BANK[j]
                            b = (5, 6, 0)[b]
                            at = SEG_OFF[3 - i] + j * P
                            last = nc.tensor.transpose(bank[b][:, c + (i - j) * P:c + (i - j + 1) * P],
                                                       N["SC"][:, at:at + P], ident[:, :])
                    last.then_inc(r["t_mm"], 1)

                def values(hh):
                    pe.wait_ge(r["t_evac"], 6 * t + 3 * hh + 6)
                    for j in range(NT):
                        last = mm(bank[1][hh * 64:(hh + 1) * 64, j * P:S], N["V2"][:, j * P + hh * 64:j * P + (hh + 1) * 64],
                                  N["PT"][:, SEG_OFF[j]:SEG_OFF[j] + SEG_W[j]], start=(j == 0), stop=(j == NT - 1))
                    if hh:
                        last.then_inc(unit_done, 1)

                pe.wait_ge(r["t_evac"], 6 * t + 3)
                proj(0, 0)
                pe.wait_ge(r["o_evac"], t + 1)
                proj(1, 1)
                proj(5, 2)
                pe.wait_ge(r["y_skip"], 2 * t + 2)
                source_rows(0, 2)
                proj(6, 3)
                spread_cs(0, 0, 3)
                spread_cs(0, 1, 4)
                pe.wait_ge(r["xd_done"], 2 * t + 1)
                proj(7, 4)
                pe.wait_ge(r["qk_evac"], 2 * t + 2)
                scores(0)
                pe.wait_ge(r["xd_done"], 2 * t + 2)
                head_y(0, 0, 2)
                head_y(0, 1, 2)
                project_tokens(bank[3], U_PAIR, 5, t, PAIR_UNITS)
                source_rows(1, 7)
                turn(0)
                proj(4, 6)
                pe.wait_ge(r["z_silu"], 2 * t + 1)
                pe.wait_ge(r["v_evac"], t + 1)
                values(0)
                scores(1)
                spread_cs(1, 0, 3)
                pe.wait_ge(r["z_silu"], 2 * t + 2)
                spread_cs(1, 1, 4)
                pe.wait_ge(r["y_skip"], 2 * t + 3)
                pe.wait_ge(r["xd_done"], 2 * t + 3)
                head_y(1, 0, 2)
                head_y(1, 1, 2)
                turn(1)
                values(1)

            pe.wait_ge(r["yss_done"], 8)
            mm(bank[7][:, :], ones[:, :], SS[:, :], start=True, stop=True).then_inc(r["yms"], 1)
            pe.wait_ge(r["ynorm"], 8)
            pe.wait_ge(r["o_evac"], 4 + 1)
            for m in range(KD):
                if m >= 4:
                    pe.wait_ge(res_done, 8 * 4 + m - 3)
                for k in range(12):
                    b = m * 12 + k
                    if b % BLOCKS == 0:
                        unit_wait(U_OUT2, b // BLOCKS)
                    last = mm(bank[m % 4][:, :], blk(U_OUT2, b // BLOCKS, b % BLOCKS), tile_of(MIX, k),
                              start=(k == 0), stop=(k == 11))
                    if b % BLOCKS == BLOCKS - 1:
                        last.then_inc(unit_done, 1)
                    elif k == 11:
                        last.then_inc(r["yms"], 1)
            sum_squares(4)
            pe.wait_ge(h_mul, 40)
            ffn(U_UPB, U_DNB, NJ2, NJ1 + NJ2, 5, False)
            sum_squares(5)

        @block.scalar
        def _(act):
            A = nc.scalar.activation

            def norm(n, eps):
                act.wait_ge(ms_done, n + 1)
                A(RT[:, :], bank[7][:, :], ACT.Sqrt, bias=eps[:, :], scale=1.0 / D).then_inc(rt_done, 1)

            def shift(n, col):
                for k in range(KD):
                    act.wait_ge(h_mul, 8 * n + k + 1)
                    A(tile_of(HT, k), tile_of(HT, k), ACT.Identity, bias=MOD[:, col + k:col + k + 1]).then_inc(h_add, 1)

            for s_, by in ((up_act, 2), (q["rg_sig"], 1), (q["ig_sig"], 1), (q["sgb_done"], 1), (r["t_evac"], 3), (r["o_evac"], 1)):
                act.sem_inc(s_, by)
            act.wait_ge(vec_in_s, 16)
            act.wait_ge(prep_v, 1)
            lam = v("rg_lambda", 0, HEADS)
            A(lam_t[:, 0:8], lam, ACT.Abs).then_inc(prep_a, 1)
            act.wait_ge(prep_a, 1)
            A(lam_t[:, 8:16], lam_t[:, 0:8], ACT.Exp, scale=-1.0).then_inc(prep_a, 1)
            act.wait_ge(prep_a, 2)
            A(lam_t[:, 16:24], lam_t[:, 8:16], ACT.Ln, bias=one[:, :]).then_inc(prep_a, 1)
            A(aneg[:, :], v("a_log_2"), ACT.Exp).then_inc(prep_a, 1)
            norm(0, eps1)
            act.wait_ge(mod_done, 1)
            shift(0, 0)

            M = mixer1_tiles()
            with act.Fori(0, HEADS) as h:
                u = h * HEAD_UNITS + U_HEAD
                act.wait_ge(unit_done, u + 1)
                A(M["QR"], bank[0][:, :], ACT.Copy).then_inc(q["q_evac"], 1)
                A(M["QSQ"], bank[0][:, :], ACT.Square).then_inc(q["q_evac"], 1)
                act.wait_ge(unit_done, u + 2)
                A(M["KR"], bank[1][:, :], ACT.Copy).then_inc(q["k_evac"], 1)
                A(M["KSQ"], bank[1][:, :], ACT.Square).then_inc(q["k_evac"], 1)
                act.wait_ge(unit_done, u + 3)
                A(M["VT"], bank[5][:, :], ACT.Copy).then_inc(q["v_evac"], 1)
                act.wait_ge(unit_done, u + 4)
                A(M["XR"][:, 3:3 + S], bank[7][:, :], ACT.Copy).then_inc(q["xr_evac"], 1)
                act.wait_ge(q["q_ms"], h + 1)
                A(M["RQ"], bank[0][:, :], ACT.Sqrt, bias=eps1[:, :], scale=1.0 / P).then_inc(q["rq_done"], 1)
                act.wait_ge(q["k_ms"], h + 1)
                A(M["RK"], bank[1][:, :], ACT.Sqrt, bias=eps1[:, :], scale=1.0 / P).then_inc(q["rk_done"], 1)
                act.wait_ge(unit_done, u + 5)
                A(M["GY"], bank[5][:, :], ACT.Gelu_apprx_tanh).then_inc(q["gy_done"], 1)
                act.wait_ge(q["z_done"], h + 1)
                for b, w, at in BANK_PART:
                    A(M["AZ"][:, at:at + w], bank[2 + b][:, 0:w], ACT.Abs).then_inc(q["absz_done"], 1)
                act.wait_ge(q["absz_done"], 3 * h + 3)
                A(M["EZ"], M["AZ"], ACT.Exp, scale=-1.0).then_inc(q["ez_done"], 1)
                act.wait_ge(q["ez_done"], h + 1)
                A(M["LP"], M["EZ"], ACT.Ln, bias=one[:, :]).then_inc(q["lnp_done"], 1)
                act.wait_ge(unit_done, u + 6)
                A(M["SGA"], bank[7][:, :], ACT.Sigmoid).then_inc(q["sga_done"], 1)
                act.wait_ge(unit_done, u + 7)
                A(M["SGB"], bank[0][:, :], ACT.Sigmoid).then_inc(q["sgb_done"], 1)
                act.wait_ge(q["s_done"], h + 1)
                for b, w, at in BANK_PART:
                    A(M["AT"][:, at:at + w], bank[2 + b][:, 0:w], ACT.Exp).then_inc(q["att_done"], 1)
                act.wait_ge(q["r_mm"], h + 1)
                A(M["RG"], bank[1][:, :], ACT.Sigmoid, bias=vd("rg_ba", h)).then_inc(q["rg_sig"], 1)
                act.wait_ge(unit_done, u + 8)
                A(M["IG"], bank[5][:, :], ACT.Sigmoid, bias=vd("rg_bx", h)).then_inc(q["ig_sig"], 1)
                act.wait_ge(q["rg_sig"], h + 2)
                A(M["AD"], M["RG"], ACT.Exp, scale=c8[:, bass.ds(h, 1)]).then_inc(q["a_dec"], 1)
                A(M["TH"], M["RG"], ACT.Tanh, scale=nc8[:, bass.ds(h, 1)]).then_inc(q["th_dec"], 1)
                act.wait_ge(q["m2_done"], h + 1)
                A(M["ML"], M["M2"], ACT.Sqrt).then_inc(q["mult_done"], 1)

            norm(1, eps1)
            shift(1, 24)
            with act.Fori(0, NJ1 // 2) as i:
                for jl in range(2):
                    for n, T in ((0, CG), (1, CV)):
                        j = i * 2 + (jl + NJ1 * n)
                        act.wait_ge(unit_done, i * 4 + (U_UP1 + 2 * jl + n + 1))
                        if n:
                            act.wait_ge(ff_done, i * 2 + (jl + 1))
                        A(T[:, jl, :], bank[2 * jl + n][:, :], ACT.Identity, bias=vd("ffn_conv_b", j),
                          scale=vd("ffn_conv_w", j + 2 * 48)).then_inc(cgv_act, 1)
                    act.wait_ge(cg_dve, i * 4 + (2 * jl + 2 + 4))
                    A(TG[:, jl, :], CG[:, jl, :], ACT.Gelu_apprx_tanh).then_inc(up_act, 1)
            norm(2, eps2)

            def ffn(u_up, before):
                with act.Fori(0, NJ2 // 2) as i:
                    for jl in range(2):
                        act.wait_ge(unit_done, i * 4 + (u_up + 2 * jl + 1))
                        act.wait_ge(ff_done, i * 2 + (before + jl + 1))
                        A(TG[:, jl, :], bank[2 * jl][:, :], ACT.Silu).then_inc(up_act, 1)
            ffn(U_UPA, NJ1)
            norm(3, eps2)

            N = mixer2_tiles()
            for n in range(4):
                act.wait_ge(unit_done, U_BC + n + 1)
                if n:
                    act.wait_ge(r["bc_silu"], n)
                A(N["BC"], bank[n][:, :], ACT.Identity, bias=v("conv_b_2", 8 + n),
                  scale=v("conv_w_2", 3 * 12 + 8 + n)).then_inc(r["bc_conv"], 1)
                act.wait_ge(r["bc_tap"], 3 * n + 3)
                T = N["BT"] if n < 2 else N["CT"]
                A(T[:, (n % 2) * S:(n % 2 + 1) * S], N["BC"], ACT.Silu).then_inc(r["bc_silu"], 1)
            act.wait_ge(unit_done, U_BC + 5)
            A(N["DZ"], bank[4][:, :], ACT.Identity, bias=v("dt_bias_2")).then_inc(r["dt_z"], 1)
            act.wait_ge(r["dt_z"], 1)
            A(N["DE"], N["DZ"], ACT.Abs).then_inc(r["dt_abs"], 1)
            act.wait_ge(r["dt_abs"], 1)
            A(N["DE"], N["DE"], ACT.Exp, scale=-1.0).then_inc(r["dt_exp"], 1)
            act.wait_ge(r["dt_exp"], 1)
            A(N["DE"], N["DE"], ACT.Ln, bias=one[:, :]).then_inc(r["dt_ln"], 1)
            for g in range(2):
                act.wait_ge(r["g_mm"], g + 1)
                for b, w, at in BANK_PART:
                    A(N["GS"][:, g * TRI + at:g * TRI + at + w], bank[b][:, 0:w], ACT.Copy).then_inc(r["g_evac"], 1)
            act.wait_ge(r["tr_dt"], 1)
            A(N["DTT"], bank[5][:, 0:64], ACT.Copy).then_inc(r["tr_evac"], 1)
            A(N["CST"], bank[5][:, 64:128], ACT.Copy).then_inc(r["tr_evac"], 1)

            with act.Fori(0, 4) as t:
                u = t * PAIR_UNITS + U_PAIR

                def conv(a, b, loc):
                    act.wait_ge(unit_done, u + (loc + 1))
                    act.wait_ge(r["y_skip"], 2 * t + a + 1)
                    A(N["XS"][a], bank[b][:, :], ACT.Identity, bias=vd("conv_b_2", t + 4 * a),
                      scale=vd("conv_w_2", t + (3 * 12 + 4 * a))).then_inc(r["xs_conv"], 1)

                def silu(a):
                    act.wait_ge(r["xs_tap"], 6 * t + 3 * a + 3)
                    A(N["XS"][a], N["XS"][a], ACT.Silu).then_inc(r["xs_silu"], 1)

                def silu_z(a, b, loc):
                    act.wait_ge(unit_done, u + (loc + 1))
                    A(N["ZS"][a], bank[b][:, :], ACT.Silu).then_inc(r["z_silu"], 1)

                def decay(a, hh):
                    act.wait_ge(r["dd_done"], 16 * t + 8 * a + 4 * hh + 4)
                    A(N[f"ED{hh}"], N[f"ED{hh}"], ACT.Exp).then_inc(r["ed_done"], 1)

                def soften(hh):
                    act.wait_ge(r["s_neg"], 2 * t + hh + 1)
                    for i in range(NT):
                        at, w = SEG_OFF[3 - i], (i + 1) * P
                        A(N["SC"][:, at:at + w], N["SC"][:, at:at + w], ACT.Exp, bias=N["nmx"][:, i:i + 1],
                          accum_out=N["sm"][:, i:i + 1]).then_inc(r["s_exp"], 1)

                def turned(hh):
                    act.wait_ge(r["t_mm"], 2 * t + hh + 1)
                    for b, w, at in BANK_PART:
                        A(N["PT"][:, at:at + w], bank[(5, 6, 0)[b]][:, 0:w], ACT.Copy).then_inc(r["t_evac"], 1)

                conv(0, 0, 0)
                silu(0)
                silu_z(0, 1, 1)
                act.wait_ge(unit_done, u + 3)
                A(N["Q2"], bank[5][:, :], ACT.Copy, scale=0.125).then_inc(r["qk_evac"], 1)
                act.wait_ge(unit_done, u + 4)
                A(N["K2"], bank[6][:, :], ACT.Copy).then_inc(r["qk_evac"], 1)
                decay(0, 0)
                decay(0, 1)
                conv(1, 7, 4)
                soften(0)
                silu(1)
                act.wait_ge(unit_done, u + 6)
                A(N["V2"], bank[3][:, :], ACT.Copy).then_inc(r["v_evac"], 1)
                turned(0)
                silu_z(1, 4, 6)
                decay(1, 0)
                decay(1, 1)
                soften(1)
                turned(1)
                act.wait_ge(unit_done, u + 8)
                A(tile_of(MIX, t + 8), bank[1][:, :], ACT.Copy).then_inc(r["o_evac"], 1)

            act.wait_ge(r["yms"], 1)
            A(RT[:, :], bank[7][:, :], ACT.Sqrt, bias=eps2[:, :], scale=1.0 / D).then_inc(r["yrt"], 1)
            norm(4, eps2)
            ffn(U_UPB, NJ1 + NJ2)
            norm(5, eps2)

        @block.vector
        def _(dve):
            V = nc.vector
            TT = V.tensor_tensor

            def STT(out_ap, in0, scalar, in1, op0, op1):
                return V.scalar_tensor_tensor(out=out_ap, in0=in0, scalar=scalar, in1=in1, op0=op0, op1=op1)

            def clear_ss(n):
                V.memset(SS[:, :], 0.0).then_inc(ss_clear, 1)
                dve.wait_ge(ss_clear, n)

            def squares(x, at, sem_ss=ss_done):
                dve.wait_ge(sem_ss, at)
                TT(SQ[:, :], x, x, ALU.mult).then_inc(sq_done, 1)

            def norm(n, gain, n_rt):
                dve.wait_ge(rt_done, n + 1)
                V.reciprocal(RS[:, :], RT[:, :]).then_inc(rs_done, 1)
                dve.wait_ge(rs_done, n + 1)
                for k in range(KD):
                    STT(tile_of(HT, k), tile_of(XT, k), gain(k), RS[:, :], ALU.mult, ALU.mult).then_inc(h_mul, 1)

            def residual(n, first_unit, per, gate, banks, one_more=None):
                clear_ss(CLEAR[n])
                with dve.Fori(0, 2) as i:
                    for m in range(4):
                        dve.wait_ge(unit_done, i * (4 * per) + (first_unit + per * (m + 1)))
                        x = tile_of(XT, i * 4 + m)
                        g = gate(i * 4 + m)
                        STT(x, bank[banks + m][:, :], g, x, ALU.mult, ALU.add).then_inc(res_done, 1)
                        dve.wait_ge(res_done, i * 4 + (8 * n + m + 1))
                        TT(SQ[:, :], x, x, ALU.mult).then_inc(sq_done, 1)
                        dve.wait_ge(sq_done, i * 4 + (SQ_BEFORE[n] + m + 1))
                        TT(SS[:, :], SS[:, :], SQ[:, :], ALU.add).then_inc(ss_done, 1)
                        dve.wait_ge(ss_done, i * 4 + (8 * n + m + 1))

            CLEAR = [1, 2, 3, 4, 6, 7]
            SQ_BEFORE = [0, 8, 16, 24, 40, 48]

            for s_, by in ((ff_done, 2), (cg_dve, 4), (cv_dve, 4), (q["yb_done"], 1), (r["y_skip"], 2), (r["xd_done"], 1)):
                dve.sem_inc(s_, by)
            M = mixer1_tiles()
            V.memset(eps1[:, :], EPS1)
            V.memset(eps2[:, :], EPS2)
            V.memset(zero[:, :], 0.0)
            V.memset(M["XR"][:, 0:3], 0.0)
            V.memset(one[:, :], 1.0).then_inc(prep_v, 1)
            clear_ss(1)
            dve.wait_ge(x_in_s, 16)
            for k in range(KD):
                TT(SQ[:, :], tile_of(XT, k), tile_of(XT, k), ALU.mult).then_inc(sq_done, 1)
                dve.wait_ge(sq_done, k + 1)
                TT(SS[:, :], SS[:, :], SQ[:, :], ALU.add).then_inc(ss_done, 1)
                dve.wait_ge(ss_done, k + 1)
            dve.sem_inc(res_done, 8)
            dve.wait_ge(vec_in_s, 16)
            dve.wait_ge(prep_a, 4)
            V.tensor_scalar(lam_t[:, 0:8], v("rg_lambda", 0, HEADS), -1.0, 0.0, ALU.mult, ALU.max).then_inc(prep_v, 1)
            dve.wait_ge(prep_v, 2)
            TT(lam_t[:, 0:8], lam_t[:, 0:8], lam_t[:, 16:24], ALU.add).then_inc(prep_v, 1)
            dve.wait_ge(prep_v, 3)
            V.tensor_scalar(c8[:, :], lam_t[:, 0:8], -8.0, None, ALU.mult).then_inc(prep_v, 1)
            V.tensor_scalar(nc8[:, :], lam_t[:, 0:8], 8.0, None, ALU.mult).then_inc(prep_v, 1)
            V.tensor_scalar(qg[:, :], v("q_norm_g"), float(P) ** -0.5, None, ALU.mult).then_inc(prep_v, 1)
            V.tensor_scalar(aneg[:, :], aneg[:, :], -1.0, None, ALU.mult).then_inc(prep_v, 1)
            dve.wait_ge(unit_done, U_HEAD)
            TT(MOD[:, 0:16], bank[6][:, 0:16], v("ada_b", 0, 16), ALU.add).then_inc(mod_done, 1)
            dve.wait_ge(mod_done, 1)
            STT(G1[:, :], MOD[:, 8:16], one[:, :], v("norm1_g", 0, KD), ALU.add, ALU.mult).then_inc(prep_v, 1)
            dve.wait_ge(prep_v, 8)
            norm(0, lambda k: G1[:, k:k + 1], 0)

            with dve.Fori(0, HEADS) as h:
                dve.wait_ge(q["rq_done"], h + 1)
                V.reciprocal(M["RSQ"], M["RQ"]).then_inc(q["rsq"], 1)
                dve.wait_ge(q["rsq"], h + 1)
                STT(M["QN"], M["QR"], qg[:, :], M["RSQ"], ALU.mult, ALU.mult).then_inc(q["qn_done"], 1)
                dve.wait_ge(q["rk_done"], h + 1)
                V.reciprocal(M["RSK"], M["RK"]).then_inc(q["rsk"], 1)
                dve.wait_ge(q["rsk"], h + 1)
                STT(M["KN"], M["KR"], v("k_norm_g"), M["RSK"], ALU.mult, ALU.mult).then_inc(q["kn_done"], 1)
                dve.wait_ge(q["xr_evac"], h + 1)
                V.tensor_scalar(M["XC"], M["XR"][:, 0:S], vd("conv_w", h), vd("conv_b", h), ALU.mult, ALU.add).then_inc(q["conv_done"], 1)
                for k in range(1, 4):
                    dve.wait_ge(q["conv_done"], 4 * h + k)
                    STT(M["XC"], M["XR"][:, k:k + S], vd("conv_w", h + 8 * k), M["XC"], ALU.mult, ALU.add).then_inc(q["conv_done"], 1)
                dve.wait_ge(q["lnp_done"], h + 1)
                for b, w, at in BANK_PART:
                    STT(M["PP"][:, at:at + w], bank[2 + b][:, 0:w], zero[:, :], M["LP"][:, at:at + w], ALU.max, ALU.add).then_inc(q["p_done"], 1)
                dve.wait_ge(q["a_dec"], h + 1)
                TT(M["A2"], M["AD"], M["AD"], ALU.mult).then_inc(q["a2_done"], 1)
                dve.wait_ge(q["th_dec"], h + 1)
                dve.wait_ge(q["a2_done"], h + 1)
                STT(M["M2"], M["A2"], one[:, :], M["TH"], ALU.add, ALU.mult).then_inc(q["m2_done"], 1)
                dve.wait_ge(q["conv_done"], 4 * h + 4)
                dve.wait_ge(q["ig_sig"], h + 2)
                TT(M["IX"], M["IG"], M["XC"], ALU.mult).then_inc(q["ix_done"], 1)
                dve.wait_ge(q["ix_done"], h + 1)
                dve.wait_ge(q["mult_done"], h + 1)
                TT(M["U"], M["ML"], M["IX"], ALU.mult).then_inc(q["u_done"], 1)
                dve.wait_ge(q["u_done"], h + 1)
                V.tensor_tensor_scan(M["HS"], M["AD"], M["U"], 0.0, ALU.mult, ALU.add).then_inc(q["scan_done"], 1)
                dve.wait_ge(q["scan_done"], h + 1)
                dve.wait_ge(q["gy_done"], h + 1)
                TT(M["YA"], M["HS"], M["GY"], ALU.mult).then_inc(q["ya_done"], 1)
                dve.wait_ge(q["ya_done"], 2 * h + 1)
                dve.wait_ge(q["sga_done"], h + 1)
                TT(M["YA"], M["YA"], M["SGA"], ALU.mult).then_inc(q["ya_done"], 1)
                dve.wait_ge(q["pv_done"], h + 1)
                dve.wait_ge(q["sgb_done"], h + 2)
                TT(M["YB"], bank[7][:, :], M["SGB"], ALU.mult).then_inc(q["yb_done"], 1)
                dve.wait_ge(q["ya_done"], 2 * h + 2)
                dve.wait_ge(q["yb_done"], h + 2)
                TT(tile_of(MIX, h), M["YA"], M["YB"], ALU.add).then_inc(q["mix_done"], 1)

            dve.wait_ge(unit_done, U_OUT1)
            TT(MOD[:, 16:48], bank[6][:, 16:48], v("ada_b", 16, 32), ALU.add).then_inc(mod_done, 1)
            dve.wait_ge(mod_done, 2)
            STT(G2[:, :], MOD[:, 32:40], one[:, :], v("norm2_g", 0, KD), ALU.add, ALU.mult).then_inc(prep_v, 1)
            dve.wait_ge(prep_v, 9)
            residual(1, U_OUT1, 1, lambda m: MOD[:, bass.ds(m + 16, 1)], 0)
            norm(1, lambda k: G2[:, k:k + 1], 1)

            with dve.Fori(0, NJ1 // 2) as i:
                for jl in range(2):
                    for n, T, tap_done in ((0, CG, cg_dve), (1, CV, cv_dve)):
                        j = i * 2 + (jl + NJ1 * n)
                        dve.wait_ge(cgv_act, i * 4 + (2 * jl + n + 1))
                        for k in (1, 2):
                            STT(T[:, jl, k:S], bank[2 * jl + n][:, 0:S - k], vd("ffn_conv_w", j + (2 - k) * 48), T[:, jl, k:S],
                                ALU.mult, ALU.add).then_inc(tap_done, 1)
                            dve.wait_ge(tap_done, i * 4 + (4 + 2 * jl + k))
                    dve.wait_ge(up_act, i * 2 + (2 + jl + 1))
                    TT(tile_of(ARENA, i * 2 + jl), TG[:, jl, :], CV[:, jl, :], ALU.mult).then_inc(ff_done, 1)
            residual(2, U_DN1, 3, lambda m: MOD[:, bass.ds(m + 40, 1)], 4)
            norm(2, lambda k: v("ffn1_norm_2", k), 2)

            def ffn(u_up, before):
                with dve.Fori(0, NJ2 // 2) as i:
                    for jl in range(2):
                        dve.wait_ge(unit_done, i * 4 + (u_up + 2 * jl + 2))
                        dve.wait_ge(up_act, i * 2 + (2 + before + jl + 1))
                        TT(tile_of(ARENA, i * 2 + jl), TG[:, jl, :], bank[2 * jl + 1][:, :], ALU.mult).then_inc(ff_done, 1)
            ffn(U_UPA, NJ1)
            residual(3, U_DNA, 3, lambda m: 0.5, 4)
            norm(3, lambda k: v("mix_norm_2", k), 3)

            N = mixer2_tiles()
            for n in range(4):
                dve.wait_ge(r["bc_conv"], n + 1)
                for k in (1, 2, 3):
                    STT(N["BC"][:, k:S], bank[n][:, 0:S - k], v("conv_w_2", (3 - k) * 12 + 8 + n), N["BC"][:, k:S],
                        ALU.mult, ALU.add).then_inc(r["bc_tap"], 1)
                    dve.wait_ge(r["bc_tap"], 3 * n + k)
            dve.wait_ge(r["dt_ln"], 1)
            STT(N["DT"], N["DZ"], zero[:, :], N["DE"], ALU.max, ALU.add).then_inc(r["dt_sp"], 1)
            dve.wait_ge(r["dt_sp"], 1)
            V.tensor_scalar(N["LA"], N["DT"], aneg[:, :], None, ALU.mult).then_inc(r["dt_la"], 1)
            dve.wait_ge(r["dt_la"], 1)
            V.memset(SQ[:, :], 1.0).then_inc(r["dt_la"], 1)
            dve.wait_ge(r["dt_la"], 2)
            V.tensor_tensor_scan(N["CS"], SQ[:, :], N["LA"], 0.0, ALU.mult, ALU.add).then_inc(r["cs_done"], 1)
            dve.wait_ge(r["cs_done"], 1)
            clear_ss(5)
            dve.wait_ge(r["tr_evac"], 2)
            dve.wait_ge(r["g_mask"], 8)

            with dve.Fori(0, 4) as t:
                def taps(a, b):
                    dve.wait_ge(r["xs_conv"], 2 * t + a + 1)
                    for k in (1, 2, 3):
                        STT(N["XS"][a][:, k:S], bank[b][:, 0:S - k], vd("conv_w_2", t + ((3 - k) * 12 + 4 * a)),
                            N["XS"][a][:, k:S], ALU.mult, ALU.add).then_inc(r["xs_tap"], 1)
                        dve.wait_ge(r["xs_tap"], 6 * t + 3 * a + k)

                def select(a, hh):
                    n = 4 * t + 2 * a + hh
                    if a:
                        dve.wait_ge(r["csb_done"], n - 1)
                    V.tensor_copy(N["SELH"][:, hh * P:(hh + 1) * P],
                                  ident[:, bass.ds(t * 2 + (8 * a + hh), 1)].to_broadcast([P, P])).then_inc(r["sel_done"], 1)

                def with_dt(a, b):
                    dve.wait_ge(r["xs_tr"], 2 * t + a + 1)
                    dtt = N["DTT"].rearrange("p (i h) -> p i h", h=16)[:, :, bass.ds(t * 2 + 8 * a, 2)]
                    TT(N["XD"][a].rearrange("p (i h c) -> p i h c", i=NT, h=2),
                       bank[b][:, :].rearrange("p (i h c) -> p i h c", i=NT, h=2),
                       dtt.unsqueeze(3).to_broadcast([P, NT, 2, 64]), ALU.mult).then_inc(r["xd_done"], 1)

                def distance(a, hh, b):
                    n = 4 * t + 2 * a + hh
                    dve.wait_ge(r["csb_done"], n + 1)
                    for i in range(NT):
                        V.tensor_scalar(N[f"ED{hh}"][:, SEG_OFF[i]:SEG_OFF[i] + SEG_W[i]], bank[b][:, i * P:S],
                                        N["CST"][:, bass.ds(t * 2 + (i * 16 + 8 * a + hh), 1)], 0.0,
                                        ALU.subtract, ALU.min).then_inc(r["dd_done"], 1)

                def times_g(a, hh):
                    dve.wait_ge(r["ed_done"], 4 * t + 2 * a + hh + 1)
                    TT(N[f"ED{hh}"], N[f"ED{hh}"], N["GS"][:, a * TRI:(a + 1) * TRI], ALU.mult).then_inc(r["mm_done"], 1)

                def finish(a):
                    n = 2 * t + a
                    dve.wait_ge(r["y_mm"], 2 * n + 2)
                    dve.wait_ge(r["xs_silu"], n + 1)
                    STT(N["YY"], N["XS"][a], vd("d_skip_2", t + 4 * a), bank[2][:, :], ALU.mult, ALU.add).then_inc(r["y_skip"], 1)
                    dve.wait_ge(r["y_skip"], n + 3)
                    dve.wait_ge(r["z_silu"], n + 1)
                    y = tile_of(MIX, t + 4 * a)
                    TT(y, N["YY"], N["ZS"][a], ALU.mult).then_inc(r["yz_done"], 1)
                    dve.wait_ge(r["yz_done"], n + 1)
                    TT(SQ[:, :], y, y, ALU.mult).then_inc(sq_done, 1)
                    dve.wait_ge(sq_done, n + 33)
                    TT(SS[:, :], SS[:, :], SQ[:, :], ALU.add).then_inc(r["yss_done"], 1)
                    dve.wait_ge(r["yss_done"], n + 1)

                def biased_max(hh):
                    dve.wait_ge(r["s_mm"], 2 * t + hh + 1)
                    if hh == 0:
                        u = U_PAIR + 7
                        dve.wait_ge(arrived[u % RING], t * (16 * PAIR_UNITS // RING) + 16 * (u // RING + 1))
                    for i in range(NT):
                        b, c = SEG_BANK[3 - i]
                        at, w = SEG_OFF[3 - i], (i + 1) * P
                        TT(N["SC"][:, at:at + w], bank[(5, 6, 0)[b]][:, c:c + w],
                           ring[:, (U_PAIR + 7) % RING, hh * S + (NT - 1 - i) * P:(hh + 1) * S], ALU.add).then_inc(r["s_add"], 1)
                    dve.wait_ge(r["s_add"], 8 * t + 4 * hh + 4)
                    for i in range(NT):
                        at, w = SEG_OFF[3 - i], (i + 1) * P
                        V.tensor_reduce(N["mx"][:, i:i + 1], N["SC"][:, at:at + w], AX.X, ALU.max).then_inc(r["s_max"], 1)
                    dve.wait_ge(r["s_max"], 8 * t + 4 * hh + 4)
                    V.tensor_scalar(N["nmx"], N["mx"], -1.0, None, ALU.mult).then_inc(r["s_neg"], 1)

                def normalise(hh):
                    dve.wait_ge(r["s_exp"], 8 * t + 4 * hh + 4)
                    V.reciprocal(N["rsm"], N["sm"]).then_inc(r["s_rec"], 1)
                    dve.wait_ge(r["s_rec"], 2 * t + hh + 1)
                    for i in range(NT):
                        at, w = SEG_OFF[3 - i], (i + 1) * P
                        V.tensor_scalar(N["SC"][:, at:at + w], N["SC"][:, at:at + w], N["rsm"][:, i:i + 1], None,
                                        ALU.mult).then_inc(r["s_nrm"], 1)

                select(0, 0)
                select(0, 1)
                taps(0, 0)
                with_dt(0, 2)
                distance(0, 0, 3)
                distance(0, 1, 4)
                times_g(0, 0)
                times_g(0, 1)
                select(1, 0)
                select(1, 1)
                biased_max(0)
                taps(1, 7)
                finish(0)
                normalise(0)
                with_dt(1, 7)
                biased_max(1)
                distance(1, 0, 3)
                distance(1, 1, 4)
                times_g(1, 0)
                times_g(1, 1)
                normalise(1)
                finish(1)

            dve.wait_ge(r["yrt"], 1)
            V.reciprocal(RS[:, :], RT[:, :]).then_inc(r["yrs"], 1)
            dve.wait_ge(r["yrs"], 1)
            for k in range(KD):
                STT(tile_of(MIX, k), tile_of(MIX, k), v("ssd_norm_2", k), RS[:, :], ALU.mult, ALU.mult).then_inc(r["ynorm"], 1)

            clear_ss(CLEAR[4])
            for m in range(KD):
                if m % 2:
                    dve.wait_ge(unit_done, U_OUT2 + 12 * (m + 1) // BLOCKS)
                else:
                    dve.wait_ge(r["yms"], m // 2 + 2)
                x = tile_of(XT, m)
                STT(x, bank[m % 4][:, :], one[:, :], x, ALU.mult, ALU.add).then_inc(res_done, 1)
                dve.wait_ge(res_done, 8 * 4 + m + 1)
                TT(SQ[:, :], x, x, ALU.mult).then_inc(sq_done, 1)
                dve.wait_ge(sq_done, SQ_BEFORE[4] + m + 1)
                TT(SS[:, :], SS[:, :], SQ[:, :], ALU.add).then_inc(ss_done, 1)
                dve.wait_ge(ss_done, 8 * 4 + m + 1)
            norm(4, lambda k: v("ffn2_norm_2", k), 4)
            ffn(U_UPB, NJ1 + NJ2)
            residual(5, U_DNB, 3, lambda m: 0.5, 4)
            norm(5, lambda k: v("final_norm_2", k), 5)


def _blocks(w):
    k, m = w.shape
    return w.reshape(k // P, P, m // P, P).transpose(2, 0, 1, 3).reshape(-1, P, P)


def _units(blocks):
    pad = -len(blocks) % BLOCKS
    if pad:
        blocks = np.concatenate([blocks, np.zeros((pad, P, P), np.float32)])
    return blocks.reshape(-1, BLOCKS, P, P).transpose(0, 2, 1, 3).reshape(-1, P, UNIT)


def _down(w, nj):
    b = _blocks(w).reshape(KD, nj, P, P)
    full = np.zeros((KD, 3 * BLOCKS, P, P), np.float32)
    full[:, :nj] = b
    return _units(full.reshape(-1, P, P))


def lay_out(a):
    w = {k: np.asarray(x)[0] if k not in ("x", "c", "final_norm_2") else np.asarray(x) for k, x in a.items()}
    ada = _units(_blocks(w["ada_w"]))
    win = _units(_blocks(w["w_in"])).reshape(7, HEADS, P, UNIT)
    parts = [ada[:16]]
    for h in range(HEADS):
        gates = np.zeros((BLOCKS, P, P), np.float32)
        gates[0], gates[1] = w["rg_wa"][h], w["rg_wx"][h]
        parts += [win[[2, 3, 4, 0, 1, 5, 6], h], _units(gates), ada[16 + 4 * h:20 + 4 * h]]
    parts.append(_units(_blocks(w["w_out"])))
    up = _units(_blocks(w["ffn_up"])).reshape(2, NJ1, P, UNIT)
    parts += [up.transpose(1, 0, 2, 3).reshape(-1, P, UNIT), _down(w["ffn_down"], NJ1)]

    def ffn2(n):
        both = np.stack([_units(_blocks(w[f"ffn{n}_w_gate_2"])), _units(_blocks(w[f"ffn{n}_w_up_2"]))], 1)
        return [both.reshape(-1, P, UNIT), _down(w[f"ffn{n}_w_down_2"], NJ2)]
    parts += ffn2(1)
    w2 = w["w_in_2"]
    z, xbc, dt, qkv = w2[:, :1024], w2[:, 1024:2560], w2[:, 2560:2576], w2[:, 2576:]
    z, xbc, qkv = (_units(_blocks(np.ascontiguousarray(y))) for y in (z, xbc, qkv))
    dtp = np.zeros((D, P), np.float32)
    dtp[:, :16] = dt
    parts += [xbc[8:12], _units(_blocks(dtp))]
    rel = np.clip(np.arange(P)[:, None] - (np.arange(S)[None, :] - 384), -256, 256) + 256
    bias = w["rel_bias_2"][:, rel]
    for t in range(4):
        b = bias[2 * t:2 * t + 2].transpose(1, 0, 2).reshape(1, P, UNIT)
        parts += [xbc[t:t + 1], z[t:t + 1], qkv[t:t + 1], qkv[4 + t:5 + t], xbc[4 + t:5 + t],
                  qkv[8 + t:9 + t], z[4 + t:5 + t], b]
    parts.append(_units(_blocks(w["w_out_2"])))
    parts += ffn2(2)
    stream = np.concatenate(parts)
    assert stream.shape == (N_UNITS, P, UNIT), stream.shape

    def cols(x):
        return x.reshape(-1, P).T
    small = dict(w)
    small["d_skip_2"] = np.repeat(w["d_skip_2"], 64)
    for n in ("dt_bias_2", "a_log_2"):
        small[n] = np.concatenate([w[n], np.zeros(P - 16, np.float32)])
    vec = np.concatenate([cols(small[n]) for n, _ in VEC_SIZES], 1)
    assert vec.shape == (P, N_VEC), vec.shape
    x = w["x"][0].T.reshape(KD, P, S).transpose(1, 0, 2).reshape(P, KD * S)
    return {k: np.ascontiguousarray(y) for k, y in (("xt", x), ("vec", vec), ("stream", stream))}


def kernel(**inputs):
    import concourse.bacc as _bacc
    from concourse.bass_utils import run_bass_kernel_spmd as _run

    arrays = lay_out(inputs)
    nc = _bacc.Bacc("TRN2", target_bir_lowering=False, num_devices=1)
    args = [nc.dram_tensor("in_" + n, a.shape, F32, kind="ExternalInput").ap() for n, a in arrays.items()]
    out = nc.dram_tensor("result", (P, KD * S), F32, kind="ExternalOutput").ap()
    program(nc, *args, out)
    got = _run(nc, [{"in_" + n: a for n, a in arrays.items()}], core_ids=[0]).results[0]["result"]
    return np.ascontiguousarray(got.reshape(P, KD, S).transpose(2, 1, 0).reshape(1, S, D))
```

```python
import numpy as np
import concourse.bass as bass
from concourse import mybir
from contextlib import ExitStack

F32 = mybir.dt.float32
F32R = mybir.dt.float32r
BF16 = mybir.dt.bfloat16
ACT = mybir.ActivationFunctionType
ALU = mybir.AluOpType
AX = mybir.AxisListType

P = 128
S = 512
D = 1024
KD = D // P
HEADS = 8
NJ1 = 3 * D // P
NJ2 = 2816 // P
NT = S // P
RING = 4
BLOCKS = 8
UNIT = BLOCKS * P
ARENA_COLS = 28 * S + 264
EPS1 = 1e-6
EPS2 = 1e-5
NEG = -1e30

SEG_OFF = [0, 512, 1024, 896]
SEG_BANK = [(0, 0), (1, 0), (2, 0), (1, 384)]
SEG_W = [S - P * i for i in range(NT)]
BANK_PART = [(0, 512, 0), (1, 512, 512), (2, 256, 1024)]
TRI = 1280

U_ADA = 0
U_HEAD = U_ADA + 16
HEAD_UNITS = 12
U_OUT1 = U_HEAD + HEADS * HEAD_UNITS
U_UP1 = U_OUT1 + 8
U_DN1 = U_UP1 + 2 * NJ1
U_UPA = U_DN1 + 24
U_DNA = U_UPA + 2 * NJ2
U_BC = U_DNA + 24
U_PAIR = U_BC + 5
PAIR_UNITS = 8
U_OUT2 = U_PAIR + 4 * PAIR_UNITS
U_UPB = U_OUT2 + 12
U_DNB = U_UPB + 2 * NJ2
N_UNITS = U_DNB + 24

SPLIT_BEFORE = {U_HEAD: 0}
for _from, _to, _n in ((U_HEAD, U_OUT1, 7 * HEADS), (U_OUT1, U_UP1, 8), (U_UP1, U_DN1, 2 * NJ1),
                       (U_DN1, U_UPA, 24), (U_UPA, U_DNA, 2 * NJ2), (U_DNA, U_BC, 24), (U_BC, U_PAIR, 5),
                       (U_PAIR, U_OUT2, 28), (U_OUT2, U_UPB, 12), (U_UPB, U_DNB, 2 * NJ2)):
    SPLIT_BEFORE[_to] = SPLIT_BEFORE[_from] + _n

VEC_SIZES = [("c", 8), ("ada_b", 48), ("norm1_g", 8), ("conv_w", 32), ("conv_b", 8), ("rg_ba", 8),
             ("rg_bx", 8), ("rg_lambda", 8), ("q_norm_g", 1), ("k_norm_g", 1), ("norm2_g", 8),
             ("ffn_conv_w", 3 * 48), ("ffn_conv_b", 48), ("ffn1_norm_2", 8), ("mix_norm_2", 8),
             ("conv_w_2", 48), ("conv_b_2", 12), ("d_skip_2", 8), ("ssd_norm_2", 8),
             ("ffn2_norm_2", 8), ("final_norm_2", 8), ("dt_bias_2", 1), ("a_log_2", 1)]
VEC = {}
_at = 0
for _name, _n in VEC_SIZES:
    VEC[_name] = _at
    _at += _n
N_VEC = _at


def program(nc, xt_in, vec_in, stream, out):
    ctx = ExitStack()
    with ctx:
        def sb(name, shape, dt=F32):
            return ctx.enter_context(nc.sbuf_tensor(name, shape, dt))

        def sem(name):
            return ctx.enter_context(nc.semaphore(name))

        XT = sb("XT", [P, KD * S])
        HH = sb("HH", [P, KD * S], F32R)
        HL = sb("HL", [P, KD * S], F32R)
        with ExitStack() as hidden:
            FH = hidden.enter_context(nc.sbuf_tensor("FH", [P, NJ1 * S], F32R))
            FL = hidden.enter_context(nc.sbuf_tensor("FL", [P, NJ1 * S], F32R))
        with ExitStack() as mixers:
            ARENA = mixers.enter_context(nc.sbuf_tensor("ARENA", [P, ARENA_COLS], F32))
            MIX = mixers.enter_context(nc.sbuf_tensor("MIX", [P, KD * S], F32))
            MH = mixers.enter_context(nc.sbuf_tensor("MH", [P, 4 * S], F32R))
            ML = mixers.enter_context(nc.sbuf_tensor("ML", [P, 4 * S], F32R))
        region = ctx.enter_context(nc.sbuf_tensor("region", [P, 2 * NJ1 * S], F32))
        ring = sb("ring", [P, RING, UNIT])
        WH = sb("WH", [P, 2, UNIT], F32R)
        WL = sb("WL", [P, 2, UNIT], F32R)
        vec = sb("vec", [P, N_VEC])
        MOD = sb("MOD", [P, 48])
        G1 = sb("G1", [P, KD])
        G2 = sb("G2", [P, KD])
        c8 = sb("c8", [P, HEADS])
        nc8 = sb("nc8", [P, HEADS])
        lam_t = sb("lam_t", [P, 3 * HEADS])
        qg = sb("qg", [P, 1])
        aneg = sb("aneg", [P, 1])
        eps1 = sb("eps1", [P, 1])
        eps2 = sb("eps2", [P, 1])
        one = sb("one", [P, 1])
        zero = sb("zero", [P, 1])
        ones = sb("ones", [P, P])
        negones = sb("negones", [P, P])
        negtri = sb("negtri", [P, P])
        ident = sb("ident", [P, P])
        identb = sb("identb", [P, P], BF16)
        strictb = sb("strictb", [P, P], BF16)
        chunkb = sb("chunkb", [P, P], BF16)
        SS = sb("SS", [P, S])
        SQ = sb("SQ", [P, S])
        RT = sb("RT", [P, S])
        RS = sb("RS", [P, S])
        TG = sb("TG", [P, 2, S])
        CG = sb("CG", [P, 2, S])
        CV = sb("CV", [P, 2, S])

        NTMP = [CG[:, 0, :], CG[:, 1, :], CV[:, 0, :], CV[:, 1, :]]

        def arena():
            at = [0]

            def take(n):
                at[0] += n
                assert at[0] <= ARENA_COLS, at[0]
                return ARENA[:, at[0] - n:at[0]]
            return take

        def mixer1_tiles():
            t = arena()
            d = {n: t(S) for n in "QR QSQ KR KSQ RQ RK VT GY SGA SGB XC RG IG AD TH M2 IX HS YA YB".split()}
            d.update(QN=d["QR"], KN=d["KR"], RSQ=d["RQ"], RSK=d["RK"], A2=d["M2"], ML=d["M2"], U=d["IX"])
            d["XR"] = t(S + 4)[:, 0:S + 3]
            for n in ("AZ", "PP", "AT"):
                d[n] = t(TRI)
            d["EZ"] = d["LP"] = d["AZ"]
            return d

        def mixer2_tiles():
            t = arena()
            d = {}
            d["BT"] = t(2 * S)
            d["CT"] = t(2 * S)
            d["GS"] = t(2 * TRI)
            d["CS"] = t(S)
            for n in ("ED0", "ED1", "SC"):
                d[n] = t(TRI)
            d["PT"] = t(TRI)
            d["Q2"] = t(S)
            d["K2"] = t(S)
            d["V2"] = t(S)
            d["DTT"] = t(64)
            d["CST"] = t(64)
            d["mx"] = t(4)
            d["nmx"] = t(4)
            d["sm"] = t(4)
            d["rsm"] = t(4)
            d["DT"] = d["Q2"]
            d["DZ"] = d["K2"]
            d["DE"] = d["V2"]
            d["LA"] = d["SC"][:, 0:S]
            d["BC"] = d["ED0"][:, 0:S]
            d["XS"] = [CG[:, 0, :], CG[:, 1, :]]
            d["ZS"] = [TG[:, 0, :], TG[:, 1, :]]
            d["XD"] = [CV[:, 0, :], CV[:, 1, :]]
            d["YY"] = t(S)
            d["SELH"] = t(2 * P)
            return d

        bank = [ctx.enter_context(nc.psum_tensor(f"bank{b}", [P, S], F32)) for b in range(8)]

        def v(name, k=0, n=1):
            return vec[:, VEC[name] + k:VEC[name] + k + n]

        def vd(name, k):
            return vec[:, bass.ds(k + VEC[name], 1)]

        def tile_of(T, m):
            return T[:, m * S:(m + 1) * S] if isinstance(m, int) else T[:, bass.ds(m * S, S)]

        def seg_bank(first, i, lo=0):
            b, c = SEG_BANK[i]
            return bank[first[b]][:, c + lo:c + SEG_W[i]]

        arrived = [sem(f"arrived{s}") for s in range(RING)]
        w_high = sem("w_high")
        w_low = sem("w_low")
        h_high = sem("h_high")
        h_low = sem("h_low")
        f_tmp = sem("f_tmp")
        f_high = sem("f_high")
        unit_done = sem("unit_done")
        vec_in_s = sem("vec_in_s")
        x_in_s = sem("x_in_s")
        out_s = sem("out_s")
        consts = sem("consts")
        pool_step = sem("pool_step")
        prep_a = sem("prep_a")
        prep_v = sem("prep_v")
        mod_done = sem("mod_done")
        res_done = sem("res_done")
        sq_done = sem("sq_done")
        ss_done = sem("ss_done")
        ss_clear = sem("ss_clear")
        ms_done = sem("ms_done")
        rt_done = sem("rt_done")
        rs_done = sem("rs_done")
        h_mul = sem("h_mul")
        h_add = sem("h_add")
        up_act = sem("up_act")
        ff_done = sem("ff_done")

        N_RES = 6

        names = ("q_evac k_evac v_evac xr_evac q_ms k_ms rq_done rk_done rsq rsk qn_done kn_done "
                 "gy_done conv_done z_done absz_done ez_done lnp_done p_done s_done att_done pv_done "
                 "sga_done sgb_done r_mm i_mm rg_sig ig_sig a_dec th_dec a2_done m2_done mult_done "
                 "ix_done u_done scan_done ya_done yb_done mix_done").split()
        q = {n: sem("m1_" + n) for n in names}
        cgv_act = sem("cgv_act")
        cg_dve = sem("cg_dve")
        cv_dve = sem("cv_dve")
        names = ("bc_conv bc_tap bc_silu dt_z dt_abs dt_exp dt_ln dt_sp dt_la cs_done tr_dt tr_evac "
                 "g_mm g_evac g_mask xs_conv xs_tap xs_silu xs_tr xd_done sel_done csb_done "
                 "dd_done ed_done mm_done y_mm y_skip z_silu yz_done yss_done qk_evac v_evac "
                 "s_mm s_add s_max s_neg s_exp s_rec s_nrm t_mm t_evac o_high o_low "
                 "yms yrt yrs ynorm").split()
        r = {n: sem("m2_" + n) for n in names}

        block = ctx.enter_context(nc.Block())

        @block.sync
        def _(sp):
            sp.dma_start(vec[:, :], vec_in).then_inc(vec_in_s, 16)
            sp.dma_start(XT[:, :], xt_in).then_inc(x_in_s, 16)
            for s in range(RING):
                sp.dma_start(ring[:, s, :], stream[s]).then_inc(arrived[s], 16)
            full = N_UNITS // RING
            with sp.Fori(1, full) as i:
                for s in range(RING):
                    sp.wait_ge(unit_done, (i - 1) * RING + s + 1)
                    sp.dma_start(ring[:, s, :], stream[bass.ds(i * RING + s, 1)].rearrange("a p n -> (a p) n")).then_inc(arrived[s], 16)
            for u in range(full * RING, N_UNITS):
                sp.wait_ge(unit_done, u - RING + 1)
                sp.dma_start(ring[:, u % RING, :], stream[u]).then_inc(arrived[u % RING], 16)
            for k in range(0, KD, 2):
                sp.wait_ge(h_mul, 8 * (N_RES - 1) + k + 2)
                sp.dma_start(out[:, k * S:(k + 2) * S], XT[:, k * S:(k + 2) * S]).then_inc(out_s, 16)
            sp.wait_ge(out_s, 16 * KD // 2)

        @block.gpsimd
        def _(pool):
            n = [0]

            def step(ins):
                n[0] += 1
                ins.then_inc(pool_step, 1)
                pool.wait_ge(pool_step, n[0])

            def keep(t, cmp, fill, pattern, mult, base=0):
                step(nc.gpsimd.affine_select(out=t, in_=t, compare_op=cmp, fill=fill, base=base,
                                             pattern=pattern, channel_multiplier=mult))

            for t, value in ((ones, 1.0), (negones, -1.0), (negtri, -1.0), (ident, 0.0),
                             (identb, 0.0), (strictb, NEG), (chunkb, NEG)):
                step(nc.gpsimd.memset(t[:, :], value))
            keep(negtri[:, :], ALU.is_ge, 0.0, [[-1, P]], 1)
            keep(strictb[:, :], ALU.is_ge, 0.0, [[-1, P]], 1)
            keep(ident[:, :], ALU.not_equal, 1.0, [[-1, P]], 1)
            keep(identb[:, :], ALU.not_equal, 1.0, [[-1, P]], 1)
            keep(chunkb[:, :], ALU.is_ge, 0.0, [[0, P]], -1, base=63)
            keep(chunkb[:, :], ALU.is_ge, 0.0, [[1, P]], 0, base=-64)
            pool.sem_inc(consts, 1)

            def split(base, loc, n, i=0, stride=0, per=0):
                u = base + loc
                pool.wait_ge(w_high, i * per + (n + 1))
                nc.gpsimd.tensor_tensor(WL[:, u % 2, :], ring[:, u % RING, :], WH[:, u % 2, :].bitcast(F32),
                                        ALU.subtract).then_inc(w_low, 1)

            with pool.Fori(0, HEADS) as h:
                for j in range(7):
                    split(U_HEAD, j, j, h, HEAD_UNITS, 7)

            def split_all(base, units, body, n):
                with pool.Fori(0, units // body) as i:
                    for j in range(body):
                        split(base, j, n + j, i, body, body)

            split_all(U_OUT1, U_BC - U_OUT1, 4, SPLIT_BEFORE[U_OUT1])
            for j in range(5):
                split(U_BC, j, SPLIT_BEFORE[U_BC] + j)
            GS = mixer2_tiles()["GS"]
            for g in range(2):
                pool.wait_ge(r["g_evac"], 3 * (g + 1))
                for i in range(NT):
                    at = g * TRI + SEG_OFF[i]
                    ins = nc.gpsimd.affine_select(out=GS[:, at:at + P], in_=GS[:, at:at + P],
                                                  compare_op=ALU.is_ge, fill=0.0, base=0,
                                                  pattern=[[1, P]], channel_multiplier=-1)
                    ins.then_inc(r["g_mask"], 1)
            with pool.Fori(0, 4) as t:
                for j in range(7):
                    split(U_PAIR, j, SPLIT_BEFORE[U_PAIR] + j, t, PAIR_UNITS, 7)
            split_all(U_OUT2, N_UNITS - U_OUT2, 4, SPLIT_BEFORE[U_OUT2])

        @block.tensor
        def _(pe):
            mm = nc.tensor.matmul

            def unit_wait(base, loc, i=0, stride=0):
                u = base + loc
                pe.wait_ge(arrived[u % RING], 16 * (u // RING + 1) + i * (16 * (stride // RING)))

            def blk(base, loc, b, n=1):
                return ring[:, (base + loc) % RING, b * P:(b + n) * P]

            def part(W, base, loc, b):
                return W[:, (base + loc) % 2, b * P:(b + 1) * P]

            def split_wait(base, loc, i=0, per=0, before=None):
                n = SPLIT_BEFORE[base] + loc if before is None else before
                pe.wait_ge(w_low, i * per + (n + 1))

            def product(out_ap, base, loc, xh, xl, n, start=True, stop=True, ready=None):
                for k in range(n):
                    if ready is not None:
                        pe.wait_ge(h_high, ready + k + 1)
                    mm(out_ap, part(WL, base, loc, k), xh(k), start=(start and k == 0), stop=False)
                    mm(out_ap, part(WH, base, loc, k), xh(k), start=False, stop=False)
                for k in range(n):
                    if ready is not None:
                        pe.wait_ge(h_low, ready + k + 1)
                    last = mm(out_ap, part(WH, base, loc, k), xl(k), start=False, stop=(stop and k == n - 1))
                return last

            def project(out_ap, base, loc, i=0, stride=0, ready=None):
                per = 7 if base in (U_HEAD, U_PAIR) else stride
                split_wait(base, loc, i, per)
                product(out_ap, base, loc, lambda k: tile_of(HH, k), lambda k: tile_of(HL, k), KD,
                        ready=ready).then_inc(unit_done, 1)

            def project_tokens(out_bank, base, loc, i=0, stride=0):
                split_wait(base, loc, i, 7)
                for t in range(NT):
                    for k in range(KD):
                        at = slice(k * S + t * P, k * S + (t + 1) * P)
                        for n, (x, W) in enumerate(((HH, WH), (HH, WL), (HL, WH))):
                            last = mm(out_bank[:, t * P:(t + 1) * P], x[:, at], part(W, base, loc, k),
                                      start=(k == 0 and n == 0), stop=(k == KD - 1 and n == 2))
                last.then_inc(unit_done, 1)

            def sum_squares(n):
                pe.wait_ge(ss_done, 8 * (n + 1))
                mm(bank[7][:, :], ones[:, :], SS[:, :], start=True, stop=True).then_inc(ms_done, 1)

            def ada(col, base, loc, i=0, stride=0):
                unit_wait(base, loc, i, stride)
                for k in range(KD):
                    out_ap = bank[6][:, col:col + 1] if isinstance(col, int) else bank[6][:, bass.ds(col, 1)]
                    last = mm(out_ap, blk(base, loc, k), v("c", k), start=(k == 0), stop=(k == KD - 1))
                last.then_inc(unit_done, 1)

            pe.wait_ge(consts, 1)
            sum_squares(0)
            pe.wait_ge(vec_in_s, 16)
            with pe.Fori(0, 4) as i:
                for j in range(4):
                    ada(i * 4 + j, U_ADA, j, i, 4)
            M = mixer1_tiles()
            with pe.Fori(0, HEADS) as h:
                def proj(b, loc):
                    project(bank[b][:, :], U_HEAD, loc, h, HEAD_UNITS, ready=0 if loc == 0 else None)
                pe.wait_ge(q["sgb_done"], h + 1)
                proj(0, 0)
                pe.wait_ge(q["rg_sig"], h + 1)
                proj(1, 1)
                pe.wait_ge(q["ig_sig"], h + 1)
                project_tokens(bank[5], U_HEAD, 2, h, HEAD_UNITS)
                pe.wait_ge(q["yb_done"], h + 1)
                proj(7, 3)
                pe.wait_ge(q["q_evac"], 2 * h + 2)
                mm(bank[0][:, :], ones[:, :], M["QSQ"], start=True, stop=True).then_inc(q["q_ms"], 1)
                pe.wait_ge(q["k_evac"], 2 * h + 2)
                mm(bank[1][:, :], ones[:, :], M["KSQ"], start=True, stop=True).then_inc(q["k_ms"], 1)
                pe.wait_ge(q["v_evac"], h + 1)
                proj(5, 4)
                pe.wait_ge(q["qn_done"], h + 1)
                pe.wait_ge(q["kn_done"], h + 1)
                for i in (0, 1, 3, 2):
                    mm(seg_bank((2, 3, 4), i), M["KN"][:, i * P:(i + 1) * P], M["QN"][:, i * P:S],
                       start=(i != 3), stop=False, skip_group_check=True)
                    b, c = SEG_BANK[i]
                    last = mm(bank[2 + b][:, c:c + P], identb[:, :], strictb[:, :], start=False,
                              stop=False, skip_group_check=True)
                last.then_inc(q["z_done"], 1)
                pe.wait_ge(q["xr_evac"], h + 1)
                proj(7, 5)
                pe.wait_ge(q["rq_done"], h + 1)
                proj(0, 6)
                pe.wait_ge(q["p_done"], 3 * h + 3)
                for i in range(NT):
                    for j in range(i, NT):
                        last = mm(seg_bank((2, 3, 4), i, (j - i) * P), (negtri if i == j else negones)[:, :],
                                  M["PP"][:, SEG_OFF[j]:SEG_OFF[j] + SEG_W[j]], start=False,
                                  stop=(i == NT - 1), skip_group_check=True)
                last.then_inc(q["s_done"], 1)
                unit_wait(U_HEAD, 7, h, HEAD_UNITS)
                pe.wait_ge(q["conv_done"], 4 * h + 4)
                pe.wait_ge(q["rk_done"], h + 1)
                mm(bank[1][:, :], blk(U_HEAD, 7, 0), M["XC"], start=True, stop=True).then_inc(q["r_mm"], 1)
                pe.wait_ge(q["gy_done"], h + 1)
                mm(bank[5][:, :], blk(U_HEAD, 7, 1), M["XC"], start=True, stop=True).then_inc(unit_done, 1)
                for j in range(4):
                    ada(h * 4 + 16 + j, U_HEAD, 8 + j, h, HEAD_UNITS)
                pe.wait_ge(q["att_done"], 3 * h + 3)
                pe.wait_ge(q["sga_done"], h + 1)
                for i in range(NT):
                    last = mm(bank[7][:, i * P:S], M["VT"][:, i * P:(i + 1) * P],
                              M["AT"][:, SEG_OFF[i]:SEG_OFF[i] + SEG_W[i]], start=(i == 0), stop=(i == NT - 1))
                last.then_inc(q["pv_done"], 1)

            with pe.Fori(0, 2) as i:
                for m in range(4):
                    pe.wait_ge(res_done, i * 4 + (8 + m - 3))
                    project(bank[m][:, :], U_OUT1, m, i, 4, ready=8 if m == 0 else None)

            def ffn(u_up, u_dn, nj, before, n_res, conv, ready):
                with pe.Fori(0, nj // 2) as i:
                    for jl in range(2):
                        if conv:
                            pe.wait_ge(cg_dve, i * 4 + (2 * jl + 2))
                        else:
                            pe.wait_ge(up_act, i * 2 + (before + jl + 1))
                        project(bank[2 * jl][:, :], u_up, 2 * jl, i, 4, ready=None if jl else ready)
                        if conv:
                            pe.wait_ge(cv_dve, i * 4 + (2 * jl + 2))
                        else:
                            pe.wait_ge(ff_done, i * 2 + (before + jl + 1))
                        project(bank[2 * jl + 1][:, :], u_up, 2 * jl + 1, i, 4)
                pe.wait_ge(ff_done, 2 + before + nj)
                with pe.Fori(0, 2) as i:
                    for m in range(4):
                        pe.wait_ge(res_done, i * 4 + (8 * n_res + m - 3))
                        for n in range(3):
                            split_wait(u_dn, 3 * m + n, i, 12)
                            product(bank[4 + m][:, :], u_dn, 3 * m + n,
                                    lambda k: tile_of(FH, n * BLOCKS + k), lambda k: tile_of(FL, n * BLOCKS + k),
                                    min(BLOCKS, nj - n * BLOCKS), n == 0, n == 2).then_inc(unit_done, 1)

            sum_squares(1)
            ffn(U_UP1, U_DN1, NJ1, 0, 2, True, 16)
            sum_squares(2)
            ffn(U_UPA, U_DNA, NJ2, NJ1, 3, False, 24)
            sum_squares(3)

            N = mixer2_tiles()
            for n in range(4):
                project(bank[n][:, :], U_BC, n, ready=32)
            project(bank[4][:, :], U_BC, 4)
            pe.wait_ge(r["dt_sp"], 1)
            for t in range(NT):
                mm(bank[5][:, t * 16:(t + 1) * 16], N["DT"][:, t * P:(t + 1) * P], ident[:, 0:16], start=True, stop=True)
            pe.wait_ge(r["cs_done"], 1)
            for t in range(NT):
                last = mm(bank[5][:, 64 + t * 16:64 + (t + 1) * 16], N["CS"][:, t * P:(t + 1) * P], ident[:, 0:16],
                          start=True, stop=True)
            last.then_inc(r["tr_dt"], 1)
            for g in range(2):
                pe.wait_ge(r["bc_silu"], 4)
                if g:
                    pe.wait_ge(r["g_evac"], 3)
                for i in (0, 1, 3, 2):
                    last = mm(seg_bank((0, 1, 2), i), N["BT"][:, g * S + i * P:g * S + (i + 1) * P],
                              N["CT"][:, g * S + i * P:(g + 1) * S], start=(i != 3), stop=True, skip_group_check=True)
                last.then_inc(r["g_mm"], 1)
            pe.wait_ge(r["g_evac"], 6)
            pe.wait_ge(r["tr_evac"], 2)

            with pe.Fori(0, 4) as t:
                def proj(b, loc):
                    project(bank[b][:, :], U_PAIR, loc, t, PAIR_UNITS)

                def source_rows(a, b):
                    pe.wait_ge(r["xs_silu"], 2 * t + a + 1)
                    for i in range(NT):
                        last = nc.tensor.transpose(bank[b][:, i * P:(i + 1) * P], N["XS"][a][:, i * P:(i + 1) * P], ident[:, :])
                    last.then_inc(r["xs_tr"], 1)

                def spread_cs(a, hh, b):
                    pe.wait_ge(r["sel_done"], 4 * t + 2 * a + hh + 1)
                    mm(bank[b][:, :], N["SELH"][:, hh * P:(hh + 1) * P], N["CS"], start=True, stop=True).then_inc(r["csb_done"], 1)

                def head_y(a, hh, b):
                    pe.wait_ge(r["mm_done"], 4 * t + 2 * a + hh + 1)
                    for i in range(NT):
                        last = mm(bank[b][hh * 64:(hh + 1) * 64, i * P:S], N["XD"][a][:, i * P + hh * 64:i * P + (hh + 1) * 64],
                                  N[f"ED{hh}"][:, SEG_OFF[i]:SEG_OFF[i] + SEG_W[i]], start=(i == 0), stop=(i == NT - 1))
                    last.then_inc(r["y_mm"], 1)

                def scores(hh):
                    for i in (3, 2, 0, 1):
                        b, c = SEG_BANK[3 - i]
                        b = (5, 6, 0)[b]
                        w = (i + 1) * P
                        mm(bank[b][:, c:c + w], N["Q2"][hh * 64:(hh + 1) * 64, i * P:(i + 1) * P],
                           N["K2"][hh * 64:(hh + 1) * 64, 0:w], start=(i != 0), stop=False, skip_group_check=True)
                        last = mm(bank[b][:, c + w - P:c + w], identb[:, :], chunkb[:, :], start=False, stop=True,
                                  skip_group_check=True)
                    last.then_inc(r["s_mm"], 1)

                def turn(hh):
                    pe.wait_ge(r["s_nrm"], 8 * t + 4 * hh + 4)
                    if hh:
                        unit_wait(U_PAIR, 7, t, PAIR_UNITS)
                    for j in range(NT):
                        for i in range(j, NT):
                            b, c = SEG_BANK[j]
                            b = (5, 6, 0)[b]
                            at = SEG_OFF[3 - i] + j * P
                            last = nc.tensor.transpose(bank[b][:, c + (i - j) * P:c + (i - j + 1) * P],
                                                       N["SC"][:, at:at + P], ident[:, :])
                    last.then_inc(r["t_mm"], 1)

                def values(hh):
                    pe.wait_ge(r["t_evac"], 6 * t + 3 * hh + 6)
                    for j in range(NT):
                        last = mm(bank[1][hh * 64:(hh + 1) * 64, j * P:S], N["V2"][:, j * P + hh * 64:j * P + (hh + 1) * 64],
                                  N["PT"][:, SEG_OFF[j]:SEG_OFF[j] + SEG_W[j]], start=(j == 0), stop=(j == NT - 1))
                    if hh:
                        last.then_inc(unit_done, 1)

                pe.wait_ge(r["t_evac"], 6 * t + 3)
                proj(0, 0)
                pe.wait_ge(r["o_low"], t + 1)
                proj(1, 1)
                proj(5, 2)
                pe.wait_ge(r["y_skip"], 2 * t + 2)
                source_rows(0, 2)
                proj(6, 3)
                spread_cs(0, 0, 3)
                spread_cs(0, 1, 4)
                pe.wait_ge(r["xd_done"], 2 * t + 1)
                proj(7, 4)
                pe.wait_ge(r["qk_evac"], 2 * t + 2)
                scores(0)
                pe.wait_ge(r["xd_done"], 2 * t + 2)
                head_y(0, 0, 2)
                head_y(0, 1, 2)
                project_tokens(bank[3], U_PAIR, 5, t, PAIR_UNITS)
                source_rows(1, 7)
                turn(0)
                proj(4, 6)
                pe.wait_ge(r["z_silu"], 2 * t + 1)
                pe.wait_ge(r["v_evac"], t + 1)
                values(0)
                scores(1)
                spread_cs(1, 0, 3)
                pe.wait_ge(r["z_silu"], 2 * t + 2)
                spread_cs(1, 1, 4)
                pe.wait_ge(r["y_skip"], 2 * t + 3)
                pe.wait_ge(r["xd_done"], 2 * t + 3)
                head_y(1, 0, 2)
                head_y(1, 1, 2)
                turn(1)
                values(1)

            pe.wait_ge(r["yss_done"], 8)
            mm(bank[7][:, :], ones[:, :], SS[:, :], start=True, stop=True).then_inc(r["yms"], 1)
            for m in range(KD):
                if m >= 4:
                    pe.wait_ge(res_done, 8 * 4 + m - 3)
                for k in range(12):
                    b = m * 12 + k
                    if b % BLOCKS == 0:
                        split_wait(U_OUT2, b // BLOCKS)
                    if k < KD:
                        pe.wait_ge(h_low, 40 + k + 1)
                    else:
                        pe.wait_ge(r["o_low"], 4 + 1)
                    xh, xl = (tile_of(HH, k), tile_of(HL, k)) if k < KD else (tile_of(MH, k - KD), tile_of(ML, k - KD))
                    wh, wl = (part(W, U_OUT2, b // BLOCKS, b % BLOCKS) for W in (WH, WL))
                    mm(bank[m % 4][:, :], wl, xh, start=(k == 0), stop=False)
                    mm(bank[m % 4][:, :], wh, xh, start=False, stop=False)
                    last = mm(bank[m % 4][:, :], wh, xl, start=False, stop=(k == 11))
                    if b % BLOCKS == BLOCKS - 1:
                        last.then_inc(unit_done, 1)
                    elif k == 11:
                        last.then_inc(r["yms"], 1)
            sum_squares(4)
            ffn(U_UPB, U_DNB, NJ2, NJ1 + NJ2, 5, False, 48)
            sum_squares(5)

        @block.scalar
        def _(act):
            A = nc.scalar.activation

            def norm(n, eps):
                act.wait_ge(ms_done, n + 1)
                A(RT[:, :], bank[7][:, :], ACT.Sqrt, bias=eps[:, :], scale=1.0 / D).then_inc(rt_done, 1)

            def weight_high(base, loc, i=0, stride=0):
                u = base + loc
                act.wait_ge(arrived[u % RING], i * (16 * (stride // RING)) + 16 * (u // RING + 1))
                A(WH[:, u % 2, :], ring[:, u % RING, :], ACT.Copy).then_inc(w_high, 1)

            def weights_only(base, units, body=4):
                with act.Fori(0, units // body) as i:
                    for j in range(body):
                        act.wait_ge(unit_done, i * body + (base + j + 1))
                        weight_high(base, j + 2, i, body)

            def high(n, col=None):
                for k in range(KD):
                    act.wait_ge(h_mul, 8 * n + k + 1)
                    if col is None:
                        A(tile_of(HH, k), NTMP[k % 4], ACT.Copy).then_inc(h_high, 1)
                    else:
                        A(tile_of(HH, k), NTMP[k % 4], ACT.Identity, bias=MOD[:, col + k:col + k + 1]).then_inc(h_high, 1)

            def high_of_mix(done, before):
                for k in range(KD):
                    act.wait_ge(done, before + k + 1)
                    A(tile_of(HH, k), tile_of(MIX, k), ACT.Copy).then_inc(h_high, 1)

            for s_, by in ((up_act, 2), (q["rg_sig"], 1), (q["ig_sig"], 1), (q["sgb_done"], 1), (r["t_evac"], 3)):
                act.sem_inc(s_, by)
            act.wait_ge(vec_in_s, 16)
            act.wait_ge(prep_v, 1)
            lam = v("rg_lambda", 0, HEADS)
            A(lam_t[:, 0:8], lam, ACT.Abs).then_inc(prep_a, 1)
            act.wait_ge(prep_a, 1)
            A(lam_t[:, 8:16], lam_t[:, 0:8], ACT.Exp, scale=-1.0).then_inc(prep_a, 1)
            act.wait_ge(prep_a, 2)
            A(lam_t[:, 16:24], lam_t[:, 8:16], ACT.Ln, bias=one[:, :]).then_inc(prep_a, 1)
            A(aneg[:, :], v("a_log_2"), ACT.Exp).then_inc(prep_a, 1)
            norm(0, eps1)
            weight_high(U_HEAD, 0)
            weight_high(U_HEAD, 1)
            act.wait_ge(mod_done, 1)
            high(0, 0)

            M = mixer1_tiles()
            with act.Fori(0, HEADS) as h:
                u = h * HEAD_UNITS + U_HEAD
                act.wait_ge(unit_done, u + 1)
                weight_high(U_HEAD, 2, h, HEAD_UNITS)
                A(M["QR"], bank[0][:, :], ACT.Copy).then_inc(q["q_evac"], 1)
                A(M["QSQ"], bank[0][:, :], ACT.Square).then_inc(q["q_evac"], 1)
                act.wait_ge(unit_done, u + 2)
                weight_high(U_HEAD, 3, h, HEAD_UNITS)
                A(M["KR"], bank[1][:, :], ACT.Copy).then_inc(q["k_evac"], 1)
                A(M["KSQ"], bank[1][:, :], ACT.Square).then_inc(q["k_evac"], 1)
                act.wait_ge(unit_done, u + 3)
                weight_high(U_HEAD, 4, h, HEAD_UNITS)
                A(M["VT"], bank[5][:, :], ACT.Copy).then_inc(q["v_evac"], 1)
                act.wait_ge(unit_done, u + 4)
                weight_high(U_HEAD, 5, h, HEAD_UNITS)
                A(M["XR"][:, 3:3 + S], bank[7][:, :], ACT.Copy).then_inc(q["xr_evac"], 1)
                act.wait_ge(q["q_ms"], h + 1)
                A(M["RQ"], bank[0][:, :], ACT.Sqrt, bias=eps1[:, :], scale=1.0 / P).then_inc(q["rq_done"], 1)
                act.wait_ge(q["k_ms"], h + 1)
                A(M["RK"], bank[1][:, :], ACT.Sqrt, bias=eps1[:, :], scale=1.0 / P).then_inc(q["rk_done"], 1)
                act.wait_ge(unit_done, u + 5)
                weight_high(U_HEAD, 6, h, HEAD_UNITS)
                A(M["GY"], bank[5][:, :], ACT.Gelu_apprx_tanh).then_inc(q["gy_done"], 1)
                act.wait_ge(q["z_done"], h + 1)
                for b, w, at in BANK_PART:
                    A(M["AZ"][:, at:at + w], bank[2 + b][:, 0:w], ACT.Abs).then_inc(q["absz_done"], 1)
                act.wait_ge(q["absz_done"], 3 * h + 3)
                A(M["EZ"], M["AZ"], ACT.Exp, scale=-1.0).then_inc(q["ez_done"], 1)
                act.wait_ge(q["ez_done"], h + 1)
                A(M["LP"], M["EZ"], ACT.Ln, bias=one[:, :]).then_inc(q["lnp_done"], 1)
                act.wait_ge(unit_done, u + 6)
                A(M["SGA"], bank[7][:, :], ACT.Sigmoid).then_inc(q["sga_done"], 1)
                act.wait_ge(unit_done, u + 7)
                A(M["SGB"], bank[0][:, :], ACT.Sigmoid).then_inc(q["sgb_done"], 1)
                act.wait_ge(q["s_done"], h + 1)
                for b, w, at in BANK_PART:
                    A(M["AT"][:, at:at + w], bank[2 + b][:, 0:w], ACT.Exp).then_inc(q["att_done"], 1)
                act.wait_ge(q["r_mm"], h + 1)
                A(M["RG"], bank[1][:, :], ACT.Sigmoid, bias=vd("rg_ba", h)).then_inc(q["rg_sig"], 1)
                act.wait_ge(unit_done, u + 8)
                A(M["IG"], bank[5][:, :], ACT.Sigmoid, bias=vd("rg_bx", h)).then_inc(q["ig_sig"], 1)
                act.wait_ge(q["rg_sig"], h + 2)
                A(M["AD"], M["RG"], ACT.Exp, scale=c8[:, bass.ds(h, 1)]).then_inc(q["a_dec"], 1)
                A(M["TH"], M["RG"], ACT.Tanh, scale=nc8[:, bass.ds(h, 1)]).then_inc(q["th_dec"], 1)
                for n in range(2):
                    weight_high(U_HEAD, HEAD_UNITS + n, h, HEAD_UNITS)
                act.wait_ge(q["m2_done"], h + 1)
                A(M["ML"], M["M2"], ACT.Sqrt).then_inc(q["mult_done"], 1)

            high_of_mix(q["mix_done"], 0)
            weights_only(U_OUT1, 8)
            norm(1, eps1)
            high(1, 24)
            with act.Fori(0, NJ1 // 2) as i:
                for jl in range(2):
                    for n, T in ((0, CG), (1, CV)):
                        j = i * 2 + (jl + NJ1 * n)
                        act.wait_ge(unit_done, i * 4 + (U_UP1 + 2 * jl + n + 1))
                        weight_high(U_UP1, 2 * jl + n + 2, i, 4)
                        if n:
                            act.wait_ge(ff_done, i * 2 + (jl + 1))
                        A(T[:, jl, :], bank[2 * jl + n][:, :], ACT.Identity, bias=vd("ffn_conv_b", j),
                          scale=vd("ffn_conv_w", j + 2 * 48)).then_inc(cgv_act, 1)
                    act.wait_ge(cg_dve, i * 4 + (2 * jl + 2 + 4))
                    A(TG[:, jl, :], CG[:, jl, :], ACT.Gelu_apprx_tanh).then_inc(up_act, 1)
                    act.wait_ge(f_tmp, i * 2 + (jl + 1))
                    A(tile_of(FH, i * 2 + jl), TG[:, jl, :], ACT.Copy).then_inc(f_high, 1)
            weights_only(U_DN1, 24)
            norm(2, eps2)
            high(2)

            def ffn(u_up, before):
                with act.Fori(0, NJ2 // 2) as i:
                    for jl in range(2):
                        act.wait_ge(unit_done, i * 4 + (u_up + 2 * jl + 1))
                        weight_high(u_up, 2 * jl + 2, i, 4)
                        act.wait_ge(ff_done, i * 2 + (before + jl + 1))
                        A(TG[:, jl, :], bank[2 * jl][:, :], ACT.Silu).then_inc(up_act, 1)
                        act.wait_ge(unit_done, i * 4 + (u_up + 2 * jl + 2))
                        weight_high(u_up, 2 * jl + 3, i, 4)
                        act.wait_ge(f_tmp, i * 2 + (before + jl + 1))
                        A(tile_of(FH, i * 2 + jl), TG[:, jl, :], ACT.Copy).then_inc(f_high, 1)
            ffn(U_UPA, NJ1)
            weights_only(U_DNA, 24)
            norm(3, eps2)
            high(3)

            N = mixer2_tiles()
            for n in range(4):
                act.wait_ge(unit_done, U_BC + n + 1)
                weight_high(U_BC, n + 2)
                if n:
                    act.wait_ge(r["bc_silu"], n)
                A(N["BC"], bank[n][:, :], ACT.Identity, bias=v("conv_b_2", 8 + n),
                  scale=v("conv_w_2", 3 * 12 + 8 + n)).then_inc(r["bc_conv"], 1)
                act.wait_ge(r["bc_tap"], 3 * n + 3)
                T = N["BT"] if n < 2 else N["CT"]
                A(T[:, (n % 2) * S:(n % 2 + 1) * S], N["BC"], ACT.Silu).then_inc(r["bc_silu"], 1)
            act.wait_ge(unit_done, U_BC + 5)
            weight_high(U_BC, 6)
            A(N["DZ"], bank[4][:, :], ACT.Identity, bias=v("dt_bias_2")).then_inc(r["dt_z"], 1)
            act.wait_ge(r["dt_z"], 1)
            A(N["DE"], N["DZ"], ACT.Abs).then_inc(r["dt_abs"], 1)
            act.wait_ge(r["dt_abs"], 1)
            A(N["DE"], N["DE"], ACT.Exp, scale=-1.0).then_inc(r["dt_exp"], 1)
            act.wait_ge(r["dt_exp"], 1)
            A(N["DE"], N["DE"], ACT.Ln, bias=one[:, :]).then_inc(r["dt_ln"], 1)
            for g in range(2):
                act.wait_ge(r["g_mm"], g + 1)
                for b, w, at in BANK_PART:
                    A(N["GS"][:, g * TRI + at:g * TRI + at + w], bank[b][:, 0:w], ACT.Copy).then_inc(r["g_evac"], 1)
            act.wait_ge(r["tr_dt"], 1)
            A(N["DTT"], bank[5][:, 0:64], ACT.Copy).then_inc(r["tr_evac"], 1)
            A(N["CST"], bank[5][:, 64:128], ACT.Copy).then_inc(r["tr_evac"], 1)

            with act.Fori(0, 4) as t:
                u = t * PAIR_UNITS + U_PAIR

                def conv(a, b, loc):
                    act.wait_ge(unit_done, u + (loc + 1))
                    weight_high(U_PAIR, loc + 2, t, PAIR_UNITS)
                    act.wait_ge(r["y_skip"], 2 * t + a + 1)
                    A(N["XS"][a], bank[b][:, :], ACT.Identity, bias=vd("conv_b_2", t + 4 * a),
                      scale=vd("conv_w_2", t + (3 * 12 + 4 * a))).then_inc(r["xs_conv"], 1)

                def silu(a):
                    act.wait_ge(r["xs_tap"], 6 * t + 3 * a + 3)
                    A(N["XS"][a], N["XS"][a], ACT.Silu).then_inc(r["xs_silu"], 1)

                def silu_z(a, b, loc):
                    act.wait_ge(unit_done, u + (loc + 1))
                    if loc == 1:
                        weight_high(U_PAIR, 3, t, PAIR_UNITS)
                    else:
                        weight_high(U_PAIR, 8, t, PAIR_UNITS)
                        weight_high(U_PAIR, 9, t, PAIR_UNITS)
                    A(N["ZS"][a], bank[b][:, :], ACT.Silu).then_inc(r["z_silu"], 1)

                def decay(a, hh):
                    act.wait_ge(r["dd_done"], 16 * t + 8 * a + 4 * hh + 4)
                    A(N[f"ED{hh}"], N[f"ED{hh}"], ACT.Exp).then_inc(r["ed_done"], 1)

                def soften(hh):
                    act.wait_ge(r["s_neg"], 2 * t + hh + 1)
                    for i in range(NT):
                        at, w = SEG_OFF[3 - i], (i + 1) * P
                        A(N["SC"][:, at:at + w], N["SC"][:, at:at + w], ACT.Exp, bias=N["nmx"][:, i:i + 1],
                          accum_out=N["sm"][:, i:i + 1]).then_inc(r["s_exp"], 1)

                def turned(hh):
                    act.wait_ge(r["t_mm"], 2 * t + hh + 1)
                    for b, w, at in BANK_PART:
                        A(N["PT"][:, at:at + w], bank[(5, 6, 0)[b]][:, 0:w], ACT.Copy).then_inc(r["t_evac"], 1)

                conv(0, 0, 0)
                silu(0)
                silu_z(0, 1, 1)
                act.wait_ge(unit_done, u + 3)
                weight_high(U_PAIR, 4, t, PAIR_UNITS)
                A(N["Q2"], bank[5][:, :], ACT.Copy, scale=0.125).then_inc(r["qk_evac"], 1)
                act.wait_ge(unit_done, u + 4)
                weight_high(U_PAIR, 5, t, PAIR_UNITS)
                A(N["K2"], bank[6][:, :], ACT.Copy).then_inc(r["qk_evac"], 1)
                decay(0, 0)
                decay(0, 1)
                conv(1, 7, 4)
                soften(0)
                silu(1)
                act.wait_ge(unit_done, u + 6)
                A(N["V2"], bank[3][:, :], ACT.Copy).then_inc(r["v_evac"], 1)
                turned(0)
                silu_z(1, 4, 6)
                decay(1, 0)
                decay(1, 1)
                soften(1)
                turned(1)
                act.wait_ge(unit_done, u + 8)
                A(tile_of(MH, t), bank[1][:, :], ACT.Copy).then_inc(r["o_high"], 1)

            act.wait_ge(r["yms"], 1)
            A(RT[:, :], bank[7][:, :], ACT.Sqrt, bias=eps2[:, :], scale=1.0 / D).then_inc(r["yrt"], 1)
            high_of_mix(r["ynorm"], 0)
            for n in range(12):
                act.wait_ge(unit_done, U_OUT2 + n + 1)
                weight_high(U_OUT2, n + 2)
            norm(4, eps2)
            high(4)
            ffn(U_UPB, NJ1 + NJ2)
            weights_only(U_DNB, 20)
            for n in (20, 21):
                act.wait_ge(unit_done, U_DNB + n + 1)
                weight_high(U_DNB, n + 2)
            norm(5, eps2)

        @block.vector
        def _(dve):
            V = nc.vector
            TT = V.tensor_tensor

            def STT(out_ap, in0, scalar, in1, op0, op1):
                return V.scalar_tensor_tensor(out=out_ap, in0=in0, scalar=scalar, in1=in1, op0=op0, op1=op1)

            def clear_ss(n):
                V.memset(SS[:, :], 0.0).then_inc(ss_clear, 1)
                dve.wait_ge(ss_clear, n)

            def squares(x, at, sem_ss=ss_done):
                dve.wait_ge(sem_ss, at)
                TT(SQ[:, :], x, x, ALU.mult).then_inc(sq_done, 1)

            def low(k, before, x, shift=None):
                dve.wait_ge(h_high, before + k + 1)
                high = tile_of(HH, k).bitcast(F32)
                if shift is None:
                    TT(tile_of(HL, k), x, high, ALU.subtract).then_inc(h_low, 1)
                else:
                    STT(tile_of(HL, k), x, shift(k), high, ALU.add, ALU.subtract).then_inc(h_low, 1)

            def norm(n, gain, before, shift=None):
                dve.wait_ge(rt_done, n + 1)
                V.reciprocal(RS[:, :], RT[:, :]).then_inc(rs_done, 1)
                dve.wait_ge(rs_done, n + 1)
                for k in range(KD + 2):
                    if k < KD:
                        if k >= 4:
                            dve.wait_ge(h_low, before + k - 3)
                        STT(NTMP[k % 4], tile_of(XT, k), gain(k), RS[:, :], ALU.mult, ALU.mult).then_inc(h_mul, 1)
                    if k >= 2:
                        dve.wait_ge(h_mul, 8 * n + k - 1)
                        low(k - 2, before, NTMP[(k - 2) % 4], shift)

            def low_of_mix(before):
                for k in range(KD):
                    low(k, before, tile_of(MIX, k))

            def residual(n, first_unit, per, gate, banks, one_more=None):
                clear_ss(CLEAR[n])
                with dve.Fori(0, 2) as i:
                    for m in range(4):
                        dve.wait_ge(unit_done, i * (4 * per) + (first_unit + per * (m + 1)))
                        x = tile_of(XT, i * 4 + m)
                        g = gate(i * 4 + m)
                        STT(x, bank[banks + m][:, :], g, x, ALU.mult, ALU.add).then_inc(res_done, 1)
                        dve.wait_ge(res_done, i * 4 + (8 * n + m + 1))
                        TT(SQ[:, :], x, x, ALU.mult).then_inc(sq_done, 1)
                        dve.wait_ge(sq_done, i * 4 + (SQ_BEFORE[n] + m + 1))
                        TT(SS[:, :], SS[:, :], SQ[:, :], ALU.add).then_inc(ss_done, 1)
                        dve.wait_ge(ss_done, i * 4 + (8 * n + m + 1))

            CLEAR = [1, 2, 3, 4, 6, 7]
            SQ_BEFORE = [0, 8, 16, 24, 40, 48]

            for s_, by in ((ff_done, 2), (cg_dve, 4), (cv_dve, 4), (q["yb_done"], 1), (r["y_skip"], 2), (r["xd_done"], 1), (r["o_low"], 1)):
                dve.sem_inc(s_, by)
            M = mixer1_tiles()
            V.memset(eps1[:, :], EPS1)
            V.memset(eps2[:, :], EPS2)
            V.memset(zero[:, :], 0.0)
            V.memset(M["XR"][:, 0:3], 0.0)
            V.memset(one[:, :], 1.0).then_inc(prep_v, 1)
            clear_ss(1)
            dve.wait_ge(x_in_s, 16)
            for k in range(KD):
                TT(SQ[:, :], tile_of(XT, k), tile_of(XT, k), ALU.mult).then_inc(sq_done, 1)
                dve.wait_ge(sq_done, k + 1)
                TT(SS[:, :], SS[:, :], SQ[:, :], ALU.add).then_inc(ss_done, 1)
                dve.wait_ge(ss_done, k + 1)
            dve.sem_inc(res_done, 8)
            dve.wait_ge(vec_in_s, 16)
            dve.wait_ge(prep_a, 4)
            V.tensor_scalar(lam_t[:, 0:8], v("rg_lambda", 0, HEADS), -1.0, 0.0, ALU.mult, ALU.max).then_inc(prep_v, 1)
            dve.wait_ge(prep_v, 2)
            TT(lam_t[:, 0:8], lam_t[:, 0:8], lam_t[:, 16:24], ALU.add).then_inc(prep_v, 1)
            dve.wait_ge(prep_v, 3)
            V.tensor_scalar(c8[:, :], lam_t[:, 0:8], -8.0, None, ALU.mult).then_inc(prep_v, 1)
            V.tensor_scalar(nc8[:, :], lam_t[:, 0:8], 8.0, None, ALU.mult).then_inc(prep_v, 1)
            V.tensor_scalar(qg[:, :], v("q_norm_g"), float(P) ** -0.5, None, ALU.mult).then_inc(prep_v, 1)
            V.tensor_scalar(aneg[:, :], aneg[:, :], -1.0, None, ALU.mult).then_inc(prep_v, 1)
            dve.wait_ge(unit_done, U_HEAD)
            TT(MOD[:, 0:16], bank[6][:, 0:16], v("ada_b", 0, 16), ALU.add).then_inc(mod_done, 1)
            dve.wait_ge(mod_done, 1)
            STT(G1[:, :], MOD[:, 8:16], one[:, :], v("norm1_g", 0, KD), ALU.add, ALU.mult).then_inc(prep_v, 1)
            dve.wait_ge(prep_v, 8)
            norm(0, lambda k: G1[:, k:k + 1], 0, lambda k: MOD[:, k:k + 1])

            with dve.Fori(0, HEADS) as h:
                dve.wait_ge(q["rq_done"], h + 1)
                V.reciprocal(M["RSQ"], M["RQ"]).then_inc(q["rsq"], 1)
                dve.wait_ge(q["rsq"], h + 1)
                STT(M["QN"], M["QR"], qg[:, :], M["RSQ"], ALU.mult, ALU.mult).then_inc(q["qn_done"], 1)
                dve.wait_ge(q["rk_done"], h + 1)
                V.reciprocal(M["RSK"], M["RK"]).then_inc(q["rsk"], 1)
                dve.wait_ge(q["rsk"], h + 1)
                STT(M["KN"], M["KR"], v("k_norm_g"), M["RSK"], ALU.mult, ALU.mult).then_inc(q["kn_done"], 1)
                dve.wait_ge(q["xr_evac"], h + 1)
                V.tensor_scalar(M["XC"], M["XR"][:, 0:S], vd("conv_w", h), vd("conv_b", h), ALU.mult, ALU.add).then_inc(q["conv_done"], 1)
                for k in range(1, 4):
                    dve.wait_ge(q["conv_done"], 4 * h + k)
                    STT(M["XC"], M["XR"][:, k:k + S], vd("conv_w", h + 8 * k), M["XC"], ALU.mult, ALU.add).then_inc(q["conv_done"], 1)
                dve.wait_ge(q["lnp_done"], h + 1)
                for b, w, at in BANK_PART:
                    STT(M["PP"][:, at:at + w], bank[2 + b][:, 0:w], zero[:, :], M["LP"][:, at:at + w], ALU.max, ALU.add).then_inc(q["p_done"], 1)
                dve.wait_ge(q["a_dec"], h + 1)
                TT(M["A2"], M["AD"], M["AD"], ALU.mult).then_inc(q["a2_done"], 1)
                dve.wait_ge(q["th_dec"], h + 1)
                dve.wait_ge(q["a2_done"], h + 1)
                STT(M["M2"], M["A2"], one[:, :], M["TH"], ALU.add, ALU.mult).then_inc(q["m2_done"], 1)
                dve.wait_ge(q["conv_done"], 4 * h + 4)
                dve.wait_ge(q["ig_sig"], h + 2)
                TT(M["IX"], M["IG"], M["XC"], ALU.mult).then_inc(q["ix_done"], 1)
                dve.wait_ge(q["ix_done"], h + 1)
                dve.wait_ge(q["mult_done"], h + 1)
                TT(M["U"], M["ML"], M["IX"], ALU.mult).then_inc(q["u_done"], 1)
                dve.wait_ge(q["u_done"], h + 1)
                V.tensor_tensor_scan(M["HS"], M["AD"], M["U"], 0.0, ALU.mult, ALU.add).then_inc(q["scan_done"], 1)
                dve.wait_ge(q["scan_done"], h + 1)
                dve.wait_ge(q["gy_done"], h + 1)
                TT(M["YA"], M["HS"], M["GY"], ALU.mult).then_inc(q["ya_done"], 1)
                dve.wait_ge(q["ya_done"], 2 * h + 1)
                dve.wait_ge(q["sga_done"], h + 1)
                TT(M["YA"], M["YA"], M["SGA"], ALU.mult).then_inc(q["ya_done"], 1)
                dve.wait_ge(q["pv_done"], h + 1)
                dve.wait_ge(q["sgb_done"], h + 2)
                TT(M["YB"], bank[7][:, :], M["SGB"], ALU.mult).then_inc(q["yb_done"], 1)
                dve.wait_ge(q["ya_done"], 2 * h + 2)
                dve.wait_ge(q["yb_done"], h + 2)
                TT(tile_of(MIX, h), M["YA"], M["YB"], ALU.add).then_inc(q["mix_done"], 1)

            dve.wait_ge(unit_done, U_OUT1)
            TT(MOD[:, 16:48], bank[6][:, 16:48], v("ada_b", 16, 32), ALU.add).then_inc(mod_done, 1)
            dve.wait_ge(mod_done, 2)
            STT(G2[:, :], MOD[:, 32:40], one[:, :], v("norm2_g", 0, KD), ALU.add, ALU.mult).then_inc(prep_v, 1)
            dve.wait_ge(prep_v, 9)
            low_of_mix(8)
            residual(1, U_OUT1, 1, lambda m: MOD[:, bass.ds(m + 16, 1)], 0)
            norm(1, lambda k: G2[:, k:k + 1], 16, lambda k: MOD[:, 24 + k:25 + k])

            with dve.Fori(0, NJ1 // 2) as i:
                for jl in range(2):
                    for n, T, tap_done in ((0, CG, cg_dve), (1, CV, cv_dve)):
                        j = i * 2 + (jl + NJ1 * n)
                        dve.wait_ge(cgv_act, i * 4 + (2 * jl + n + 1))
                        for k in (1, 2):
                            STT(T[:, jl, k:S], bank[2 * jl + n][:, 0:S - k], vd("ffn_conv_w", j + (2 - k) * 48), T[:, jl, k:S],
                                ALU.mult, ALU.add).then_inc(tap_done, 1)
                            dve.wait_ge(tap_done, i * 4 + (4 + 2 * jl + k))
                    dve.wait_ge(up_act, i * 2 + (2 + jl + 1))
                    TT(TG[:, jl, :], TG[:, jl, :], CV[:, jl, :], ALU.mult).then_inc(f_tmp, 1)
                    dve.wait_ge(f_high, i * 2 + (jl + 1))
                    TT(tile_of(FL, i * 2 + jl), TG[:, jl, :], tile_of(FH, i * 2 + jl).bitcast(F32), ALU.subtract).then_inc(ff_done, 1)
            residual(2, U_DN1, 3, lambda m: MOD[:, bass.ds(m + 40, 1)], 4)
            norm(2, lambda k: v("ffn1_norm_2", k), 24)

            def ffn(u_up, before):
                with dve.Fori(0, NJ2 // 2) as i:
                    for jl in range(2):
                        dve.wait_ge(unit_done, i * 4 + (u_up + 2 * jl + 2))
                        dve.wait_ge(up_act, i * 2 + (2 + before + jl + 1))
                        TT(TG[:, jl, :], TG[:, jl, :], bank[2 * jl + 1][:, :], ALU.mult).then_inc(f_tmp, 1)
                        dve.wait_ge(f_high, i * 2 + (before + jl + 1))
                        TT(tile_of(FL, i * 2 + jl), TG[:, jl, :], tile_of(FH, i * 2 + jl).bitcast(F32), ALU.subtract).then_inc(ff_done, 1)
            ffn(U_UPA, NJ1)
            residual(3, U_DNA, 3, lambda m: 0.5, 4)
            norm(3, lambda k: v("mix_norm_2", k), 32)

            N = mixer2_tiles()
            for n in range(4):
                dve.wait_ge(r["bc_conv"], n + 1)
                for k in (1, 2, 3):
                    STT(N["BC"][:, k:S], bank[n][:, 0:S - k], v("conv_w_2", (3 - k) * 12 + 8 + n), N["BC"][:, k:S],
                        ALU.mult, ALU.add).then_inc(r["bc_tap"], 1)
                    dve.wait_ge(r["bc_tap"], 3 * n + k)
            dve.wait_ge(r["dt_ln"], 1)
            STT(N["DT"], N["DZ"], zero[:, :], N["DE"], ALU.max, ALU.add).then_inc(r["dt_sp"], 1)
            dve.wait_ge(r["dt_sp"], 1)
            V.tensor_scalar(N["LA"], N["DT"], aneg[:, :], None, ALU.mult).then_inc(r["dt_la"], 1)
            dve.wait_ge(r["dt_la"], 1)
            V.memset(SQ[:, :], 1.0).then_inc(r["dt_la"], 1)
            dve.wait_ge(r["dt_la"], 2)
            V.tensor_tensor_scan(N["CS"], SQ[:, :], N["LA"], 0.0, ALU.mult, ALU.add).then_inc(r["cs_done"], 1)
            dve.wait_ge(r["cs_done"], 1)
            clear_ss(5)
            dve.wait_ge(r["tr_evac"], 2)
            dve.wait_ge(r["g_mask"], 8)

            with dve.Fori(0, 4) as t:
                def taps(a, b):
                    dve.wait_ge(r["xs_conv"], 2 * t + a + 1)
                    for k in (1, 2, 3):
                        STT(N["XS"][a][:, k:S], bank[b][:, 0:S - k], vd("conv_w_2", t + ((3 - k) * 12 + 4 * a)),
                            N["XS"][a][:, k:S], ALU.mult, ALU.add).then_inc(r["xs_tap"], 1)
                        dve.wait_ge(r["xs_tap"], 6 * t + 3 * a + k)

                def select(a, hh):
                    n = 4 * t + 2 * a + hh
                    if a:
                        dve.wait_ge(r["csb_done"], n - 1)
                    V.tensor_copy(N["SELH"][:, hh * P:(hh + 1) * P],
                                  ident[:, bass.ds(t * 2 + (8 * a + hh), 1)].to_broadcast([P, P])).then_inc(r["sel_done"], 1)

                def with_dt(a, b):
                    dve.wait_ge(r["xs_tr"], 2 * t + a + 1)
                    dtt = N["DTT"].rearrange("p (i h) -> p i h", h=16)[:, :, bass.ds(t * 2 + 8 * a, 2)]
                    TT(N["XD"][a].rearrange("p (i h c) -> p i h c", i=NT, h=2),
                       bank[b][:, :].rearrange("p (i h c) -> p i h c", i=NT, h=2),
                       dtt.unsqueeze(3).to_broadcast([P, NT, 2, 64]), ALU.mult).then_inc(r["xd_done"], 1)

                def distance(a, hh, b):
                    n = 4 * t + 2 * a + hh
                    dve.wait_ge(r["csb_done"], n + 1)
                    for i in range(NT):
                        V.tensor_scalar(N[f"ED{hh}"][:, SEG_OFF[i]:SEG_OFF[i] + SEG_W[i]], bank[b][:, i * P:S],
                                        N["CST"][:, bass.ds(t * 2 + (i * 16 + 8 * a + hh), 1)], 0.0,
                                        ALU.subtract, ALU.min).then_inc(r["dd_done"], 1)

                def times_g(a, hh):
                    dve.wait_ge(r["ed_done"], 4 * t + 2 * a + hh + 1)
                    TT(N[f"ED{hh}"], N[f"ED{hh}"], N["GS"][:, a * TRI:(a + 1) * TRI], ALU.mult).then_inc(r["mm_done"], 1)

                def finish(a):
                    n = 2 * t + a
                    dve.wait_ge(r["y_mm"], 2 * n + 2)
                    dve.wait_ge(r["xs_silu"], n + 1)
                    STT(N["YY"], N["XS"][a], vd("d_skip_2", t + 4 * a), bank[2][:, :], ALU.mult, ALU.add).then_inc(r["y_skip"], 1)
                    dve.wait_ge(r["y_skip"], n + 3)
                    dve.wait_ge(r["z_silu"], n + 1)
                    y = tile_of(MIX, t + 4 * a)
                    TT(y, N["YY"], N["ZS"][a], ALU.mult).then_inc(r["yz_done"], 1)
                    dve.wait_ge(r["yz_done"], n + 1)
                    TT(SQ[:, :], y, y, ALU.mult).then_inc(sq_done, 1)
                    dve.wait_ge(sq_done, n + 33)
                    TT(SS[:, :], SS[:, :], SQ[:, :], ALU.add).then_inc(r["yss_done"], 1)
                    dve.wait_ge(r["yss_done"], n + 1)

                def biased_max(hh):
                    dve.wait_ge(r["s_mm"], 2 * t + hh + 1)
                    if hh == 0:
                        u = U_PAIR + 7
                        dve.wait_ge(arrived[u % RING], t * (16 * PAIR_UNITS // RING) + 16 * (u // RING + 1))
                    for i in range(NT):
                        b, c = SEG_BANK[3 - i]
                        at, w = SEG_OFF[3 - i], (i + 1) * P
                        TT(N["SC"][:, at:at + w], bank[(5, 6, 0)[b]][:, c:c + w],
                           ring[:, (U_PAIR + 7) % RING, hh * S + (NT - 1 - i) * P:(hh + 1) * S], ALU.add).then_inc(r["s_add"], 1)
                    dve.wait_ge(r["s_add"], 8 * t + 4 * hh + 4)
                    for i in range(NT):
                        at, w = SEG_OFF[3 - i], (i + 1) * P
                        V.tensor_reduce(N["mx"][:, i:i + 1], N["SC"][:, at:at + w], AX.X, ALU.max).then_inc(r["s_max"], 1)
                    dve.wait_ge(r["s_max"], 8 * t + 4 * hh + 4)
                    V.tensor_scalar(N["nmx"], N["mx"], -1.0, None, ALU.mult).then_inc(r["s_neg"], 1)

                def normalise(hh):
                    dve.wait_ge(r["s_exp"], 8 * t + 4 * hh + 4)
                    V.reciprocal(N["rsm"], N["sm"]).then_inc(r["s_rec"], 1)
                    dve.wait_ge(r["s_rec"], 2 * t + hh + 1)
                    for i in range(NT):
                        at, w = SEG_OFF[3 - i], (i + 1) * P
                        V.tensor_scalar(N["SC"][:, at:at + w], N["SC"][:, at:at + w], N["rsm"][:, i:i + 1], None,
                                        ALU.mult).then_inc(r["s_nrm"], 1)

                select(0, 0)
                select(0, 1)
                taps(0, 0)
                with_dt(0, 2)
                distance(0, 0, 3)
                distance(0, 1, 4)
                times_g(0, 0)
                times_g(0, 1)
                select(1, 0)
                select(1, 1)
                biased_max(0)
                taps(1, 7)
                finish(0)
                normalise(0)
                with_dt(1, 7)
                biased_max(1)
                distance(1, 0, 3)
                distance(1, 1, 4)
                times_g(1, 0)
                times_g(1, 1)
                normalise(1)
                finish(1)
                dve.wait_ge(r["o_high"], t + 1)
                TT(tile_of(ML, t), bank[1][:, :], tile_of(MH, t).bitcast(F32), ALU.subtract).then_inc(r["o_low"], 1)

            dve.wait_ge(r["yrt"], 1)
            V.reciprocal(RS[:, :], RT[:, :]).then_inc(r["yrs"], 1)
            dve.wait_ge(r["yrs"], 1)
            for k in range(KD):
                STT(tile_of(MIX, k), tile_of(MIX, k), v("ssd_norm_2", k), RS[:, :], ALU.mult, ALU.mult).then_inc(r["ynorm"], 1)
            low_of_mix(40)

            clear_ss(CLEAR[4])
            for m in range(KD):
                if m % 2:
                    dve.wait_ge(unit_done, U_OUT2 + 12 * (m + 1) // BLOCKS)
                else:
                    dve.wait_ge(r["yms"], m // 2 + 2)
                x = tile_of(XT, m)
                STT(x, bank[m % 4][:, :], one[:, :], x, ALU.mult, ALU.add).then_inc(res_done, 1)
                dve.wait_ge(res_done, 8 * 4 + m + 1)
                TT(SQ[:, :], x, x, ALU.mult).then_inc(sq_done, 1)
                dve.wait_ge(sq_done, SQ_BEFORE[4] + m + 1)
                TT(SS[:, :], SS[:, :], SQ[:, :], ALU.add).then_inc(ss_done, 1)
                dve.wait_ge(ss_done, 8 * 4 + m + 1)
            norm(4, lambda k: v("ffn2_norm_2", k), 48)
            ffn(U_UPB, NJ1 + NJ2)
            residual(5, U_DNB, 3, lambda m: 0.5, 4)
            dve.wait_ge(rt_done, 6)
            V.reciprocal(RS[:, :], RT[:, :]).then_inc(rs_done, 1)
            dve.wait_ge(rs_done, 6)
            for k in range(KD):
                STT(tile_of(XT, k), tile_of(XT, k), v("final_norm_2", k), RS[:, :], ALU.mult, ALU.mult).then_inc(h_mul, 1)


def _blocks(w):
    k, m = w.shape
    return w.reshape(k // P, P, m // P, P).transpose(2, 0, 1, 3).reshape(-1, P, P)


def _units(blocks):
    pad = -len(blocks) % BLOCKS
    if pad:
        blocks = np.concatenate([blocks, np.zeros((pad, P, P), np.float32)])
    return blocks.reshape(-1, BLOCKS, P, P).transpose(0, 2, 1, 3).reshape(-1, P, UNIT)


def _down(w, nj):
    b = _blocks(w).reshape(KD, nj, P, P)
    full = np.zeros((KD, 3 * BLOCKS, P, P), np.float32)
    full[:, :nj] = b
    return _units(full.reshape(-1, P, P))


def lay_out(a):
    w = {k: np.asarray(x)[0] if k not in ("x", "c", "final_norm_2") else np.asarray(x) for k, x in a.items()}
    ada = _units(_blocks(w["ada_w"]))
    win = _units(_blocks(w["w_in"])).reshape(7, HEADS, P, UNIT)
    parts = [ada[:16]]
    for h in range(HEADS):
        gates = np.zeros((BLOCKS, P, P), np.float32)
        gates[0], gates[1] = w["rg_wa"][h], w["rg_wx"][h]
        parts += [win[[2, 3, 4, 0, 1, 5, 6], h], _units(gates), ada[16 + 4 * h:20 + 4 * h]]
    parts.append(_units(_blocks(w["w_out"])))
    up = _units(_blocks(w["ffn_up"])).reshape(2, NJ1, P, UNIT)
    parts += [up.transpose(1, 0, 2, 3).reshape(-1, P, UNIT), _down(w["ffn_down"], NJ1)]

    def ffn2(n):
        both = np.stack([_units(_blocks(w[f"ffn{n}_w_gate_2"])), _units(_blocks(w[f"ffn{n}_w_up_2"]))], 1)
        return [both.reshape(-1, P, UNIT), _down(w[f"ffn{n}_w_down_2"], NJ2)]
    parts += ffn2(1)
    w2 = w["w_in_2"]
    z, xbc, dt, qkv = w2[:, :1024], w2[:, 1024:2560], w2[:, 2560:2576], w2[:, 2576:]
    z, xbc, qkv = (_units(_blocks(np.ascontiguousarray(y))) for y in (z, xbc, qkv))
    dtp = np.zeros((D, P), np.float32)
    dtp[:, :16] = dt
    parts += [xbc[8:12], _units(_blocks(dtp))]
    rel = np.clip(np.arange(P)[:, None] - (np.arange(S)[None, :] - 384), -256, 256) + 256
    bias = w["rel_bias_2"][:, rel]
    for t in range(4):
        b = bias[2 * t:2 * t + 2].transpose(1, 0, 2).reshape(1, P, UNIT)
        parts += [xbc[t:t + 1], z[t:t + 1], qkv[t:t + 1], qkv[4 + t:5 + t], xbc[4 + t:5 + t],
                  qkv[8 + t:9 + t], z[4 + t:5 + t], b]
    parts.append(_units(_blocks(w["w_out_2"])))
    parts += ffn2(2)
    stream = np.concatenate(parts)
    assert stream.shape == (N_UNITS, P, UNIT), stream.shape

    def cols(x):
        return x.reshape(-1, P).T
    small = dict(w)
    small["d_skip_2"] = np.repeat(w["d_skip_2"], 64)
    for n in ("dt_bias_2", "a_log_2"):
        small[n] = np.concatenate([w[n], np.zeros(P - 16, np.float32)])
    vec = np.concatenate([cols(small[n]) for n, _ in VEC_SIZES], 1)
    assert vec.shape == (P, N_VEC), vec.shape
    x = w["x"][0].T.reshape(KD, P, S).transpose(1, 0, 2).reshape(P, KD * S)
    return {k: np.ascontiguousarray(y) for k, y in (("xt", x), ("vec", vec), ("stream", stream))}


def kernel(**inputs):
    import concourse.bacc as _bacc
    from concourse.bass_utils import run_bass_kernel_spmd as _run

    arrays = lay_out(inputs)
    nc = _bacc.Bacc("TRN2", target_bir_lowering=False, num_devices=1)
    args = [nc.dram_tensor("in_" + n, a.shape, F32, kind="ExternalInput").ap() for n, a in arrays.items()]
    out = nc.dram_tensor("result", (P, KD * S), F32, kind="ExternalOutput").ap()
    program(nc, *args, out)
    got = _run(nc, [{"in_" + n: a for n, a in arrays.items()}], core_ids=[0]).results[0]["result"]
    return np.ascontiguousarray(got.reshape(P, KD, S).transpose(2, 1, 0).reshape(1, S, D))
```

```python
import numpy as np
import concourse.bass as bass
from concourse import mybir
from contextlib import ExitStack

F32 = mybir.dt.float32
F32R = mybir.dt.float32r
BF16 = mybir.dt.bfloat16
ACT = mybir.ActivationFunctionType
ALU = mybir.AluOpType
AX = mybir.AxisListType

P = 128
S = 512
D = 1024
KD = D // P
HEADS = 8
NJ1 = 3 * D // P
NJ2 = 2816 // P
NT = S // P
RING = 4
BLOCKS = 8
UNIT = BLOCKS * P
ARENA_COLS = 26 * S + 264
EPS1 = 1e-6
EPS2 = 1e-5
NEG = -1e30

SEG_OFF = [0, 512, 1024, 896]
SEG_BANK = [(0, 0), (1, 0), (2, 0), (1, 384)]
SEG_W = [S - P * i for i in range(NT)]
BANK_PART = [(0, 512, 0), (1, 512, 512), (2, 256, 1024)]
TRI = 1280

U_ADA = 0
U_HEAD = U_ADA + RING
HEAD_UNITS = 12
U_OUT1 = U_HEAD + HEADS * HEAD_UNITS
U_UP1 = U_OUT1 + 8
U_DN1 = U_UP1 + 2 * NJ1
U_UPA = U_DN1 + 24
U_DNA = U_UPA + 2 * NJ2
U_BC = U_DNA + 24
U_PAIR = U_BC + 5
PAIR_UNITS = 8
U_OUT2 = U_PAIR + 4 * PAIR_UNITS
U_UPB = U_OUT2 + 12
U_DNB = U_UPB + 2 * NJ2
N_UNITS = U_DNB + 24

ADA_FIRST = 16
ADA_BY_PE = (1, 4, 7, 10, 13)
ADA_BY_DVE = tuple(_c for _c in range(ADA_FIRST) if _c not in ADA_BY_PE)
N_FIRST = len(ADA_BY_DVE)

SPLIT_BEFORE = {U_HEAD: 0}
for _from, _to, _n in ((U_HEAD, U_OUT1, 7 * HEADS), (U_OUT1, U_UP1, 8), (U_UP1, U_DN1, 2 * NJ1),
                       (U_DN1, U_UPA, 24), (U_UPA, U_DNA, 2 * NJ2), (U_DNA, U_BC, 24), (U_BC, U_PAIR, 5),
                       (U_PAIR, U_OUT2, 28), (U_OUT2, U_UPB, 12), (U_UPB, U_DNB, 2 * NJ2)):
    SPLIT_BEFORE[_to] = SPLIT_BEFORE[_from] + _n

Q, K, ADA0, V, ADA1, XR, ADA2, YR, ADA3, GA, GATES, GB = range(HEAD_UNITS)
HEAD_SPLIT = {Q: (0, 0), K: (1, 1), V: (2, 0), XR: (3, 1), YR: (4, 0), GA: (5, 1), GB: (6, 0),
              HEAD_UNITS + Q: (7, 0), HEAD_UNITS + K: (8, 1)}
HEAD_ADA = (ADA0, ADA1, ADA2, ADA3)
BIAS = 7


def split_at(base, loc):
    if base == U_HEAD:
        n, slot = HEAD_SPLIT[loc]
        return SPLIT_BEFORE[base] + n, slot
    if base == U_PAIR and loc > BIAS:
        return SPLIT_BEFORE[base] + loc - 1, (base + loc) % 2
    return SPLIT_BEFORE[base] + loc, (base + loc) % 2


def per_iteration(base, stride):
    return 7 if base in (U_HEAD, U_PAIR) else stride


POOL_TILES = 4
POOL_LOW, LOW = {}, {}
_pool = _vector = 0
for _before, _shifted in ((0, True), (8, False), (16, True), (24, False), (32, False), (40, False), (48, False)):
    LOW[_before] = _vector
    if not _shifted:
        POOL_LOW[_before] = _pool
        _pool += POOL_TILES
    _vector += KD - (0 if _shifted else POOL_TILES)

VEC_SIZES = [("c", 8), ("ada_b", 48), ("norm1_g", 8), ("conv_w", 32), ("conv_b", 8), ("rg_ba", 8),
             ("rg_bx", 8), ("rg_lambda", 8), ("q_norm_g", 1), ("k_norm_g", 1), ("norm2_g", 8),
             ("ffn_conv_w", 3 * 48), ("ffn_conv_b", 48), ("ffn1_norm_2", 8), ("mix_norm_2", 8),
             ("conv_w_2", 48), ("conv_b_2", 12), ("d_skip_2", 8), ("ssd_norm_2", 8),
             ("ffn2_norm_2", 8), ("final_norm_2", 8), ("dt_bias_2", 1), ("a_log_2", 1)]
VEC = {}
_at = 0
for _name, _n in VEC_SIZES:
    VEC[_name] = _at
    _at += _n
N_VEC = _at


def program(nc, xt_in, vec_in, ada_in, stream, out):
    ctx = ExitStack()
    with ctx:
        def sb(name, shape, dt=F32):
            return ctx.enter_context(nc.sbuf_tensor(name, shape, dt))

        def sem(name):
            return ctx.enter_context(nc.semaphore(name))

        XT = sb("XT", [P, KD * S])
        HH = sb("HH", [P, KD * S], F32R)
        HL = sb("HL", [P, KD * S], F32R)
        with ExitStack() as hidden:
            FH = hidden.enter_context(nc.sbuf_tensor("FH", [P, NJ1 * S], F32R))
            FL = hidden.enter_context(nc.sbuf_tensor("FL", [P, NJ1 * S], F32R))
        with ExitStack() as mixers:
            ARENA = mixers.enter_context(nc.sbuf_tensor("ARENA", [P, ARENA_COLS], F32))
            MIX = mixers.enter_context(nc.sbuf_tensor("MIX", [P, KD * S], F32))
            MH = mixers.enter_context(nc.sbuf_tensor("MH", [P, 4 * S], F32R))
            ML = mixers.enter_context(nc.sbuf_tensor("ML", [P, 4 * S], F32R))
            PARTS = mixers.enter_context(nc.sbuf_tensor("PARTS", [P, 2 * TRI], F32R))
        region = ctx.enter_context(nc.sbuf_tensor("region", [P, 2 * NJ1 * S], F32))
        ring = sb("ring", [P, RING, UNIT])
        WH = sb("WH", [P, 2, UNIT], F32R)
        WL = sb("WL", [P, 2, UNIT], F32R)
        vec = sb("vec", [P, N_VEC])
        MOD = sb("MOD", [P, 48])
        G1 = sb("G1", [P, KD])
        G2 = sb("G2", [P, KD])
        c8 = sb("c8", [P, HEADS])
        nc8 = sb("nc8", [P, HEADS])
        lam_t = sb("lam_t", [P, 3 * HEADS])
        qg = sb("qg", [P, 1])
        aneg = sb("aneg", [P, 1])
        sqrt_scratch = sb("sqrt_scratch", [P, 1])
        ADA = sb("ADA", [P, 4 * P])
        eps1 = sb("eps1", [P, 1])
        eps2 = sb("eps2", [P, 1])
        one = sb("one", [P, 1])
        zero = sb("zero", [P, 1])
        ones = sb("ones", [P, P])
        negones = sb("negones", [P, P])
        negtri = sb("negtri", [P, P])
        negones_r = sb("negones_r", [P, P], F32R)
        negtri_r = sb("negtri_r", [P, P], F32R)
        ident = sb("ident", [P, P])
        identb = sb("identb", [P, P], BF16)
        strictb = sb("strictb", [P, P], BF16)
        chunkb = sb("chunkb", [P, P], BF16)
        SS = sb("SS", [P, S])
        SQ = sb("SQ", [P, S])
        RT = sb("RT", [P, S])
        RS = sb("RS", [P, S])
        TG = sb("TG", [P, 2, S])
        CG = sb("CG", [P, 2, S])
        CV = sb("CV", [P, 2, S])

        def arena():
            at = [0]

            def take(n):
                at[0] += n
                assert at[0] <= ARENA_COLS, at[0]
                return ARENA[:, at[0] - n:at[0]]
            return take

        def mixer1_tiles():
            t = arena()
            d = {n: t(S) for n in "QR QSQ KR KSQ RQ RK VT GY SGA SGB XC RG IG AD TH M2 IX HS YA YB".split()}
            d.update(QN=d["QR"], KN=d["KR"], RSQ=d["RQ"], RSK=d["RK"], A2=d["M2"], ML=d["M2"], U=d["IX"])
            d["XR"] = t(S + 4)[:, 0:S + 3]
            d["PH"], d["PL"] = PARTS[:, 0:TRI], PARTS[:, TRI:2 * TRI]
            for n in ("AZ", "AT"):
                d[n] = t(TRI)
            d["EZ"] = d["LP"] = d["PP"] = d["AZ"]
            d["VF"] = d["AZ"][:, 0:S]
            return d

        def mixer2_tiles():
            t = arena()
            d = {}
            d["BT"] = t(2 * S)
            d["CT"] = t(2 * S)
            d["GS"] = t(2 * TRI)
            d["CS"] = t(S)
            d["CSH"] = PARTS[:, 0:S]
            d["CSL"] = PARTS[:, S:2 * S]
            d["SELH"] = PARTS[:, 2 * S:2 * S + 2 * P]
            for n in ("ED0", "ED1", "SC"):
                d[n] = t(TRI)
            d["PT"] = t(TRI)
            d["Q2"] = t(S)
            d["K2"] = t(S)
            d["V2"] = t(S)
            d["DTT"] = t(64)
            d["CST"] = t(64)
            d["mx"] = t(4)
            d["nmx"] = t(4)
            d["sm"] = t(4)
            d["rsm"] = t(4)
            d["DT"] = d["Q2"]
            d["DZ"] = d["K2"]
            d["DE"] = d["V2"]
            d["VF"] = d["PT"][:, 0:S]
            d["LA"] = d["SC"][:, 0:S]
            d["BC"] = d["ED0"][:, 0:S]
            d["XS"] = [CG[:, 0, :], CG[:, 1, :]]
            d["ZS"] = [TG[:, 0, :], TG[:, 1, :]]
            d["XD"] = [CV[:, 0, :], CV[:, 1, :]]
            d["YY"] = t(S)
            return d

        bank = [ctx.enter_context(nc.psum_tensor(f"bank{b}", [P, S], F32)) for b in range(8)]

        def v(name, k=0, n=1):
            return vec[:, VEC[name] + k:VEC[name] + k + n]

        def vd(name, k):
            return vec[:, bass.ds(k + VEC[name], 1)]

        def tile_of(T, m):
            return T[:, m * S:(m + 1) * S] if isinstance(m, int) else T[:, bass.ds(m * S, S)]

        def first_unit(col):
            return ring[:, col, :] if col < RING else ARENA[:, (col - RING) * UNIT:(col - RING + 1) * UNIT]

        def seg_bank(first, i, lo=0):
            b, c = SEG_BANK[i]
            return bank[first[b]][:, c + lo:c + SEG_W[i]]

        arrived = [sem(f"arrived{s}") for s in range(RING)]
        w_high = sem("w_high")
        w_low = sem("w_low")
        h_high = sem("h_high")
        h_low = sem("h_low")
        pool_low = sem("pool_low")
        ada_mul = sem("ada_mul")
        ada_sum = sem("ada_sum")
        ada_arrived = [sem(f"ada_arrived{i}") for i in range((ADA_FIRST - RING) // 2)]
        ada_col = sem("ada_col")
        sq0_done = sem("sq0_done")
        sum0_done = sem("sum0_done")
        f_tmp = sem("f_tmp")
        f_high = sem("f_high")
        unit_done = sem("unit_done")
        vec_in_s = sem("vec_in_s")
        x_in_s = sem("x_in_s")
        out_s = sem("out_s")
        consts = sem("consts")
        pool_step = sem("pool_step")
        prep_a = sem("prep_a")
        prep_v = sem("prep_v")
        signs = sem("signs")
        mod_done = sem("mod_done")
        res_done = sem("res_done")
        sq_done = sem("sq_done")
        ss_done = sem("ss_done")
        ss_clear = sem("ss_clear")
        ms_done = sem("ms_done")
        rt_done = sem("rt_done")
        rc_done = sem("rc_done")
        dg_done = sem("dg_done")
        rs_done = sem("rs_done")
        h_mul = sem("h_mul")
        up_act = sem("up_act")
        ff_done = sem("ff_done")

        N_RES = 6
        SUM_BANK = [7, 7, 3, 3, 7, 3]
        SQ_BEFORE = [0, 8, 16, 24, 40, 48]
        SS_BEFORE = [0] + [8 + 6 * n for n in range(N_RES - 1)]

        names = ("q_evac k_evac v_evac v_tr xr_evac q_ms k_ms rq_done rk_done rsq rsk qn_done kn_done "
                 "gy_done conv_done z_done absz_done ez_done lnp_done p_done ph_done pl_done s_done att_done pv_done "
                 "sga_done sgb_done r_mm rg_sig ig_sig a_dec th_dec a2_done m2_done mult_done "
                 "ix_done u_done scan_done ya_done yb_done mix_done").split()
        q = {n: sem("m1_" + n) for n in names}
        cgv_act = sem("cgv_act")
        cg_dve = sem("cg_dve")
        cv_dve = sem("cv_dve")
        names = ("bc_conv bc_tap bc_silu dt_z dt_abs dt_exp dt_ln dt_sp dt_la cs_done tr_dt tr_evac "
                 "g_mm g_evac g_mask xs_conv xs_tap xs_silu xs_tr xd_done sel_done csb_done "
                 "dd_done ed_done mm_done y_mm y_skip z_silu yz_done yss_done qk_evac v_evac v_tr pv_mm "
                 "s_mm s_add s_max s_neg s_exp s_rec s_nrm t_mm t_evac o_high o_low "
                 "yms yrt yrc ydg yrs ynorm").split()
        r = {n: sem("m2_" + n) for n in names}

        block = ctx.enter_context(nc.Block())

        @block.sync
        def _(sp):
            sp.dma_start(vec[:, :], vec_in).then_inc(vec_in_s, 16)
            for u in range(RING):
                sp.dma_start(ring[:, u, :], stream[u]).then_inc(arrived[u], 16)
            for i in range((ADA_FIRST - RING) // 2):
                if i == 3:
                    sp.dma_start(XT[:, :], xt_in).then_inc(x_in_s, 16)
                two = slice(2 * i * UNIT, 2 * (i + 1) * UNIT)
                sp.dma_start(ARENA[:, two], ada_in[:, two]).then_inc(ada_arrived[i], 16)

            def next_unit(base, loc, i, stride):
                u = base + loc + RING
                src = stream[u] if isinstance(i, int) else stream[bass.ds(i * stride + u, 1)].rearrange("a p n -> (a p) n")
                sp.dma_start(ring[:, u % RING, :], src).then_inc(arrived[u % RING], 16)

            def after_split(base, loc, i=0, stride=0):
                sp.wait_ge(w_low, i * per_iteration(base, stride) + (split_at(base, loc)[0] + 1))
                next_unit(base, loc, i, stride)

            def all_split(base, units, body=4):
                with sp.Fori(0, units // body) as i:
                    for j in range(body):
                        after_split(base, j, i, body)

            for col in range(RING):
                if col in ADA_BY_DVE:
                    sp.wait_ge(ada_mul, ADA_BY_DVE.index(col) + 1)
                else:
                    sp.wait_ge(unit_done, col + 1)
                next_unit(U_ADA, col, 0, 0)
            with sp.Fori(0, HEADS) as h:
                for loc in range(HEAD_UNITS):
                    if loc in HEAD_ADA:
                        sp.wait_ge(ada_mul, h * 4 + (N_FIRST + HEAD_ADA.index(loc) + 1))
                        next_unit(U_HEAD, loc, h, HEAD_UNITS)
                    elif loc == GATES:
                        sp.wait_ge(unit_done, h * HEAD_UNITS + (U_HEAD + loc + 1))
                        next_unit(U_HEAD, loc, h, HEAD_UNITS)
                    else:
                        after_split(U_HEAD, loc, h, HEAD_UNITS)
            all_split(U_OUT1, U_BC - U_OUT1)
            for j in range(5):
                after_split(U_BC, j)
            with sp.Fori(0, 4) as t:
                for loc in range(PAIR_UNITS):
                    if loc == BIAS:
                        sp.wait_ge(r["s_add"], t * 8 + 8)
                        next_unit(U_PAIR, loc, t, PAIR_UNITS)
                    else:
                        after_split(U_PAIR, loc, t, PAIR_UNITS)
            all_split(U_OUT2, N_UNITS - RING - U_OUT2)
            for k in range(0, KD, 2):
                sp.wait_ge(h_mul, 8 * (N_RES - 1) + k + 2)
                sp.dma_start(out[:, k * S:(k + 2) * S], XT[:, k * S:(k + 2) * S]).then_inc(out_s, 16)
            sp.wait_ge(out_s, 16 * KD // 2)

        @block.gpsimd
        def _(pool):
            n = [0]

            def step(ins):
                n[0] += 1
                ins.then_inc(pool_step, 1)
                pool.wait_ge(pool_step, n[0])

            def keep(t, cmp, fill, pattern, mult, base=0):
                step(nc.gpsimd.affine_select(out=t, in_=t, compare_op=cmp, fill=fill, base=base,
                                             pattern=pattern, channel_multiplier=mult))

            for t, value in ((ones, 1.0), (negones, -1.0), (negtri, -1.0), (ident, 0.0),
                             (identb, 0.0), (strictb, NEG), (chunkb, NEG)):
                step(nc.gpsimd.memset(t[:, :], value))
            keep(negtri[:, :], ALU.is_ge, 0.0, [[-1, P]], 1)
            keep(strictb[:, :], ALU.is_ge, 0.0, [[-1, P]], 1)
            keep(ident[:, :], ALU.not_equal, 1.0, [[-1, P]], 1)
            keep(identb[:, :], ALU.not_equal, 1.0, [[-1, P]], 1)
            keep(chunkb[:, :], ALU.is_ge, 0.0, [[0, P]], -1, base=63)
            keep(chunkb[:, :], ALU.is_ge, 0.0, [[1, P]], 0, base=-64)
            pool.sem_inc(consts, 1)
            for k in range(1, KD):
                pool.wait_ge(sq0_done, k + 1)
                if k > 1:
                    pool.wait_ge(sum0_done, k - 1)
                nc.gpsimd.tensor_tensor(SS[:, :], tile_of(MIX, 0) if k == 1 else SS[:, :], tile_of(MIX, k),
                                        ALU.add).then_inc(sum0_done, 1)

            def split(base, loc, n, i=0, stride=0, per=0):
                u = base + loc
                slot = split_at(base, loc)[1]
                pool.wait_ge(w_high, i * per + (n + 1))
                nc.gpsimd.tensor_tensor(WL[:, slot, :], ring[:, u % RING, :], WH[:, slot, :].bitcast(F32),
                                        ALU.subtract).then_inc(w_low, 1)

            def split_units(first, end):
                start = U_OUT1 if first < U_PAIR else U_OUT2
                loops = (end - first) // 4
                if loops > 1:
                    with pool.Fori(0, loops) as i:
                        for j in range(4):
                            split(start, first - start + j, SPLIT_BEFORE[start] + first - start + j, i, 4, 4)
                else:
                    loops = 0
                for u in range(first + 4 * loops, end):
                    split(start, u - start, SPLIT_BEFORE[start] + u - start)

            def lows(before):
                for k in range(POOL_TILES):
                    pool.wait_ge(h_high, before + k + 1)
                    nc.gpsimd.tensor_tensor(tile_of(HL, k), tile_of(MIX, k), tile_of(HH, k).bitcast(F32),
                                            ALU.subtract).then_inc(pool_low, 1)

            split(U_HEAD, Q, 0)
            with pool.Fori(0, HEADS) as h:
                pool.wait_ge(w_low, h * 7 + 1)
                for j, loc in enumerate((K, V, XR, YR, GA, GB)):
                    split(U_HEAD, loc, 1 + j, h, HEAD_UNITS, 7)

            pool.wait_ge(w_low, SPLIT_BEFORE[U_OUT1] + 1)
            split_units(U_OUT1 + 1, U_OUT1 + 2)
            lows(8)
            split_units(U_OUT1 + 2, U_UPA + 2)
            lows(24)
            split_units(U_UPA + 2, U_BC + 2)
            lows(32)
            split_units(U_BC + 2, U_BC + 5)
            GS = mixer2_tiles()["GS"]
            for g in range(2):
                for j in (2 * g, 2 * g + 1):
                    split(U_PAIR, j, SPLIT_BEFORE[U_PAIR] + j)
                pool.wait_ge(r["g_evac"], 3 * (g + 1))
                for i in range(NT):
                    at = g * TRI + SEG_OFF[i]
                    ins = nc.gpsimd.affine_select(out=GS[:, at:at + P], in_=GS[:, at:at + P],
                                                  compare_op=ALU.is_ge, fill=0.0, base=0,
                                                  pattern=[[1, P]], channel_multiplier=-1)
                    ins.then_inc(r["g_mask"], 1)
            rest = tuple(enumerate((4, 5, 6, 8, 9, 10, 11)))
            with pool.Fori(0, 3) as t:
                for j, loc in rest:
                    split(U_PAIR, loc, SPLIT_BEFORE[U_PAIR] + 4 + j, t, PAIR_UNITS, 7)
            for j, loc in rest:
                if loc == 10:
                    lows(40)
                split(U_PAIR, 3 * PAIR_UNITS + loc, SPLIT_BEFORE[U_PAIR] + 4 + 3 * 7 + j)
            split_units(U_OUT2 + 4, U_UPB + 2)
            lows(48)
            split_units(U_UPB + 2, N_UNITS)

        @block.tensor
        def _(pe):
            mm = nc.tensor.matmul

            def unit_wait(base, loc, i=0, stride=0):
                u = base + loc
                pe.wait_ge(arrived[u % RING], 16 * (u // RING + 1) + i * (16 * (stride // RING)))

            def blk(base, loc, b, n=1):
                return ring[:, (base + loc) % RING, b * P:(b + n) * P]

            def part(W, base, loc, b):
                return W[:, split_at(base, loc)[1], b * P:(b + 1) * P]

            def split_wait(base, loc, i=0, per=0):
                pe.wait_ge(w_low, i * per + (split_at(base, loc)[0] + 1))

            def low_wait(before, k):
                if before in POOL_LOW and k < POOL_TILES:
                    pe.wait_ge(pool_low, POOL_LOW[before] + k + 1)
                else:
                    pe.wait_ge(h_low, LOW[before] + k + 1 - (POOL_TILES if before in POOL_LOW else 0))

            def product(out_ap, base, loc, xh, xl, n, start=True, stop=True, ready=None):
                for k in range(n):
                    if ready is not None:
                        pe.wait_ge(h_high, ready + k + 1)
                    mm(out_ap, part(WL, base, loc, k), xh(k), start=(start and k == 0), stop=False)
                    mm(out_ap, part(WH, base, loc, k), xh(k), start=False, stop=False)
                for k in range(n):
                    if ready is not None:
                        low_wait(ready, k)
                    last = mm(out_ap, part(WH, base, loc, k), xl(k), start=False, stop=(stop and k == n - 1))
                return last

            def project(out_ap, base, loc, i=0, stride=0, ready=None):
                split_wait(base, loc, i, per_iteration(base, stride))
                product(out_ap, base, loc, lambda k: tile_of(HH, k), lambda k: tile_of(HL, k), KD,
                        ready=ready).then_inc(unit_done, 1)

            def token_sums(b):
                for t in range(NT):
                    last = mm(bank[b][:, t:t + 1], SS[:, t * P:(t + 1) * P], ones[:, 0:1], start=True, stop=True)
                return last

            def spread(b):
                return mm(bank[b][:, :], ones[:, :], RT[:, :], start=True, stop=True)

            def sum_squares(n):
                pe.wait_ge(ss_done, SS_BEFORE[n] + 6)
                for i, T in enumerate((SS[:, :], CG[:, 0, :], CG[:, 1, :])):
                    if i:
                        pe.wait_ge(sq_done, SQ_BEFORE[n] + 4 * i)
                    for t in range(NT):
                        last = mm(bank[SUM_BANK[n]][:, t:t + 1], T[:, t * P:(t + 1) * P], ones[:, 0:1],
                                  start=(i == 0 and t == 0), stop=(i == 2), skip_group_check=True)
                last.then_inc(ms_done, 1)
                pe.wait_ge(dg_done, n + 1)
                spread(SUM_BANK[n]).then_inc(rs_done, 1)

            def ada(col, n, i=0, per=0):
                pe.wait_ge(ada_sum, i * per + (n + 1))
                mm(bank[6][:, bass.ds(col, 1)], ADA[:, (n % 4) * P:(n % 4 + 1) * P], ones[:, 0:1],
                   start=True, stop=True).then_inc(unit_done, 1)

            pe.wait_ge(consts, 1)
            pe.wait_ge(vec_in_s, 16)
            for col in range(ADA_FIRST):
                if col in ADA_BY_DVE:
                    n = ADA_BY_DVE.index(col)
                    pe.wait_ge(ada_sum, n + 1)
                    last = mm(bank[6][:, col:col + 1], ADA[:, (n % 4) * P:(n % 4 + 1) * P], ones[:, 0:1], start=True, stop=True)
                else:
                    if col < RING:
                        unit_wait(U_ADA, col)
                    else:
                        pe.wait_ge(ada_arrived[(col - RING) // 2], 16)
                    for k in range(KD):
                        last = mm(bank[6][:, col:col + 1], first_unit(col)[:, k * P:(k + 1) * P], v("c", k),
                                  start=(k == 0), stop=(k == KD - 1))
                last.then_inc(unit_done if col < RING else ada_col, 1)
                if col == 12:
                    pe.wait_ge(sum0_done, KD - 1)
                    token_sums(7).then_inc(ms_done, 1)
            pe.wait_ge(dg_done, 1)
            spread(7).then_inc(rs_done, 1)

            M = mixer1_tiles()

            def head_q(h, ready):
                project(bank[0][:, :], U_HEAD, Q, h, HEAD_UNITS, ready=ready)

            def head_rest(h):
                def proj(b, loc):
                    project(bank[b][:, :], U_HEAD, loc, h, HEAD_UNITS)
                pe.wait_ge(q["rg_sig"], h + 1)
                proj(1, K)
                ada(h * 4 + (ADA_FIRST + 0), N_FIRST + 0, h, 4)
                pe.wait_ge(q["ig_sig"], h + 1)
                proj(5, V)
                ada(h * 4 + (ADA_FIRST + 1), N_FIRST + 1, h, 4)
                pe.wait_ge(q["q_evac"], 2 * h + 2)
                mm(bank[0][:, :], ones[:, :], M["QSQ"], start=True, stop=True).then_inc(q["q_ms"], 1)
                pe.wait_ge(q["k_evac"], 2 * h + 2)
                mm(bank[1][:, :], ones[:, :], M["KSQ"], start=True, stop=True).then_inc(q["k_ms"], 1)
                pe.wait_ge(q["yb_done"], h + 1)
                proj(7, XR)
                ada(h * 4 + (ADA_FIRST + 2), N_FIRST + 2, h, 4)
                pe.wait_ge(q["v_evac"], 2 * h + 1)
                for i in range(NT):
                    last = nc.tensor.transpose(bank[2][:, i * P:(i + 1) * P], M["VF"][:, i * P:(i + 1) * P], ident[:, :])
                last.then_inc(q["v_tr"], 1)
                proj(5, YR)
                pe.wait_ge(q["qn_done"], h + 1)
                pe.wait_ge(q["kn_done"], h + 1)
                pe.wait_ge(q["v_evac"], 2 * h + 2)
                for i in (0, 1, 3, 2):
                    mm(seg_bank((2, 3, 4), i), M["KN"][:, i * P:(i + 1) * P], M["QN"][:, i * P:S],
                       start=(i != 3), stop=False, skip_group_check=True)
                    b, c = SEG_BANK[i]
                    last = mm(bank[2 + b][:, c:c + P], identb[:, :], strictb[:, :], start=False,
                              stop=False, skip_group_check=True)
                last.then_inc(q["z_done"], 1)
                ada(h * 4 + (ADA_FIRST + 3), N_FIRST + 3, h, 4)
                pe.wait_ge(q["xr_evac"], h + 1)
                proj(7, GA)
                unit_wait(U_HEAD, GATES, h, HEAD_UNITS)
                pe.wait_ge(q["conv_done"], 4 * h + 4)
                pe.wait_ge(q["rk_done"], h + 1)
                mm(bank[1][:, :], blk(U_HEAD, GATES, 0), M["XC"], start=True, stop=True).then_inc(q["r_mm"], 1)
                pe.wait_ge(q["gy_done"], h + 1)
                mm(bank[5][:, :], blk(U_HEAD, GATES, 1), M["XC"], start=True, stop=True).then_inc(unit_done, 1)
                pe.wait_ge(q["rq_done"], h + 1)
                proj(0, GB)
                pe.wait_ge(signs, 2)
                pe.wait_ge(q["ph_done"], h + 1)
                for part_of_p in ("PH", "PL"):
                    if part_of_p == "PL":
                        pe.wait_ge(q["pl_done"], h + 1)
                    for i in range(NT):
                        for j in range(i, NT):
                            last = mm(seg_bank((2, 3, 4), i, (j - i) * P), (negtri_r if i == j else negones_r)[:, :],
                                      M[part_of_p][:, SEG_OFF[j]:SEG_OFF[j] + SEG_W[j]], start=False,
                                      stop=(part_of_p == "PL" and i == NT - 1), skip_group_check=True)
                last.then_inc(q["s_done"], 1)

            def head_out(h):
                pe.wait_ge(q["att_done"], 3 * h + 3)
                pe.wait_ge(q["sga_done"], h + 1)
                for i in range(NT):
                    last = mm(bank[7][:, i * P:S], M["VT"][:, i * P:(i + 1) * P],
                              M["AT"][:, SEG_OFF[i]:SEG_OFF[i] + SEG_W[i]], start=(i == 0), stop=(i == NT - 1))
                last.then_inc(q["pv_done"], 1)

            head_q(0, 0)
            with pe.Fori(0, HEADS - 1) as h:
                head_rest(h)
                pe.wait_ge(q["sgb_done"], h + 1)
                head_q(h + 1, None)
                head_out(h)
            head_rest(HEADS - 1)
            head_out(HEADS - 1)

            with pe.Fori(0, 2) as i:
                for m in range(4):
                    pe.wait_ge(res_done, i * 4 + (8 + m - 3))
                    project(bank[m][:, :], U_OUT1, m, i, 4, ready=8 if m == 0 else None)

            def ffn(u_up, u_dn, nj, before, n_res, conv, ready):
                with pe.Fori(0, nj // 2) as i:
                    for jl in range(2):
                        if conv:
                            pe.wait_ge(cg_dve, i * 4 + (2 * jl + 2))
                        else:
                            pe.wait_ge(up_act, i * 2 + (before + jl + 1))
                        project(bank[2 * jl][:, :], u_up, 2 * jl, i, 4, ready=None if jl else ready)
                        if conv:
                            pe.wait_ge(cv_dve, i * 4 + (2 * jl + 2))
                        else:
                            pe.wait_ge(ff_done, i * 2 + (before + jl + 1))
                        project(bank[2 * jl + 1][:, :], u_up, 2 * jl + 1, i, 4)
                with pe.Fori(0, 2) as i:
                    for m in range(4):
                        pe.wait_ge(res_done, i * 4 + (8 * n_res + m - 3))
                        for n in range(3):
                            if m == 0:
                                pe.wait_ge(ff_done, 2 + before + min((n + 1) * BLOCKS, nj))
                            split_wait(u_dn, 3 * m + n, i, 12)
                            product(bank[4 + m][:, :], u_dn, 3 * m + n,
                                    lambda k: tile_of(FH, n * BLOCKS + k), lambda k: tile_of(FL, n * BLOCKS + k),
                                    min(BLOCKS, nj - n * BLOCKS), n == 0, n == 2).then_inc(unit_done, 1)

            sum_squares(1)
            ffn(U_UP1, U_DN1, NJ1, 0, 2, True, 16)
            sum_squares(2)
            ffn(U_UPA, U_DNA, NJ2, NJ1, 3, False, 24)
            sum_squares(3)

            N = mixer2_tiles()
            for n in range(4):
                project(bank[n][:, :], U_BC, n, ready=32)
            project(bank[4][:, :], U_BC, 4)
            project(bank[6][:, :], U_PAIR, 0)

            def g_product(g):
                for i in (0, 1, 3, 2):
                    last = mm(seg_bank((0, 1, 2), i), N["BT"][:, g * S + i * P:g * S + (i + 1) * P],
                              N["CT"][:, g * S + i * P:(g + 1) * S], start=(i != 3), stop=True, skip_group_check=True)
                last.then_inc(r["g_mm"], 1)

            pe.wait_ge(r["bc_silu"], 4)
            g_product(0)
            project(bank[7][:, :], U_PAIR, 1)
            pe.wait_ge(r["dt_sp"], 1)
            for t in range(NT):
                mm(bank[5][:, t * 16:(t + 1) * 16], N["DT"][:, t * P:(t + 1) * P], ident[:, 0:16], start=True, stop=True)
            pe.wait_ge(r["cs_done"], 1)
            for t in range(NT):
                last = mm(bank[5][:, 64 + t * 16:64 + (t + 1) * 16], N["CS"][:, t * P:(t + 1) * P], ident[:, 0:16],
                          start=True, stop=True)
            last.then_inc(r["tr_dt"], 1)
            pe.wait_ge(r["g_evac"], 3)
            g_product(1)
            project(bank[4][:, :], U_PAIR, 2)
            pe.wait_ge(r["g_evac"], 6)
            pe.wait_ge(r["tr_evac"], 2)

            def pair(t, is_last):
                def proj(b, loc):
                    project(bank[b][:, :], U_PAIR, loc, t, PAIR_UNITS)

                def source_rows(a, b):
                    pe.wait_ge(r["xs_silu"], 2 * t + a + 1)
                    for i in range(NT):
                        last = nc.tensor.transpose(bank[b][:, i * P:(i + 1) * P], N["XS"][a][:, i * P:(i + 1) * P], ident[:, :])
                    last.then_inc(r["xs_tr"], 1)

                def spread_cs(a, hh, b):
                    pe.wait_ge(r["sel_done"], 4 * t + 2 * a + hh + 1)
                    pe.wait_ge(r["cs_done"], 3)
                    mm(bank[b][:, :], N["SELH"][:, hh * P:(hh + 1) * P], N["CSH"], start=True, stop=False)
                    mm(bank[b][:, :], N["SELH"][:, hh * P:(hh + 1) * P], N["CSL"], start=False, stop=True).then_inc(r["csb_done"], 1)

                def head_y(a, hh, b):
                    pe.wait_ge(r["mm_done"], 4 * t + 2 * a + hh + 1)
                    for i in range(NT):
                        last = mm(bank[b][hh * 64:(hh + 1) * 64, i * P:S], N["XD"][a][:, i * P + hh * 64:i * P + (hh + 1) * 64],
                                  N[f"ED{hh}"][:, SEG_OFF[i]:SEG_OFF[i] + SEG_W[i]], start=(i == 0), stop=(i == NT - 1))
                    last.then_inc(r["y_mm"], 1)

                def scores(hh):
                    for i in (3, 2, 0, 1):
                        b, c = SEG_BANK[3 - i]
                        b = (5, 6, 0)[b]
                        w = (i + 1) * P
                        first = mm(bank[b][:, c:c + w], N["Q2"][hh * 64:(hh + 1) * 64, i * P:(i + 1) * P],
                                   N["K2"][hh * 64:(hh + 1) * 64, 0:w], start=(i != 0), stop=False, skip_group_check=True)
                        if hh and i == 3:
                            first.then_inc(unit_done, 1)
                        last = mm(bank[b][:, c + w - P:c + w], identb[:, :], chunkb[:, :], start=False, stop=True,
                                  skip_group_check=True)
                    last.then_inc(r["s_mm"], 1)

                def turn(hh):
                    pe.wait_ge(r["s_nrm"], 8 * t + 4 * hh + 4)
                    for j in range(NT):
                        for i in range(j, NT):
                            b, c = SEG_BANK[j]
                            b = (5, 6, 0)[b]
                            at = SEG_OFF[3 - i] + j * P
                            last = nc.tensor.transpose(bank[b][:, c + (i - j) * P:c + (i - j + 1) * P],
                                                       N["SC"][:, at:at + P], ident[:, :])
                    last.then_inc(r["t_mm"], 1)

                def values(hh):
                    pe.wait_ge(r["t_evac"], 6 * t + 3 * hh + 6)
                    for j in range(NT):
                        last = mm(bank[7][hh * 64:(hh + 1) * 64, j * P:S], N["V2"][:, j * P + hh * 64:j * P + (hh + 1) * 64],
                                  N["PT"][:, SEG_OFF[j]:SEG_OFF[j] + SEG_W[j]], start=(j == 0), stop=(j == NT - 1))
                    last.then_inc(r["pv_mm"], 1)

                pe.wait_ge(r["y_skip"], 2 * t + 2)
                source_rows(0, 2)
                pe.wait_ge(r["t_evac"], 6 * t + 3)
                proj(6, 3)
                pe.wait_ge(r["qk_evac"], 2 * t + 1)
                spread_cs(0, 0, 3)
                spread_cs(0, 1, 4)
                pe.wait_ge(r["o_low"], t + 1)
                pe.wait_ge(r["z_silu"], 2 * t + 1)
                proj(7, 4)
                pe.wait_ge(r["qk_evac"], 2 * t + 2)
                scores(0)
                proj(1, 5)
                pe.wait_ge(r["xd_done"], 2 * t + 2)
                head_y(0, 0, 2)
                head_y(0, 1, 2)
                pe.wait_ge(r["v_evac"], 2 * t + 1)
                for i in range(NT):
                    last = nc.tensor.transpose(bank[1][:, i * P:(i + 1) * P], N["VF"][:, i * P:(i + 1) * P], ident[:, :])
                last.then_inc(r["v_tr"], 1)
                spread_cs(1, 0, 3)
                spread_cs(1, 1, 4)
                source_rows(1, 7)
                turn(0)
                pe.wait_ge(r["v_evac"], 2 * t + 2)
                proj(1, 6)
                pe.wait_ge(r["xd_done"], 2 * t + 3)
                values(0)
                scores(1)
                pe.wait_ge(r["y_skip"], 2 * t + 3)
                head_y(1, 0, 2)
                head_y(1, 1, 2)
                if is_last:
                    pe.wait_ge(r["yss_done"], 8)
                    token_sums(4).then_inc(r["yms"], 1)
                    turn(1)
                    pe.wait_ge(r["ydg"], 1)
                    spread(4).then_inc(r["yrs"], 1)
                else:
                    proj(3, 8)
                    pe.wait_ge(r["z_silu"], 2 * t + 2)
                    proj(1, 9)
                    turn(1)
                    proj(4, 10)
                values(1)

            with pe.Fori(0, 3) as t:
                pair(t, False)
            pair(3, True)

            for m in range(KD):
                if m == 1:
                    pe.wait_ge(r["z_silu"], 8)
                if m >= 4:
                    pe.wait_ge(res_done, 8 * 4 + m - 3)
                for k in range(12):
                    b = m * 12 + k
                    if b % BLOCKS == 0:
                        split_wait(U_OUT2, b // BLOCKS)
                    if k < 4:
                        pe.wait_ge(r["o_low"], k + 2)
                    else:
                        low_wait(40, k - 4)
                    xh, xl = (tile_of(MH, k), tile_of(ML, k)) if k < 4 else (tile_of(HH, k - 4), tile_of(HL, k - 4))
                    wh, wl = (part(W, U_OUT2, b // BLOCKS, b % BLOCKS) for W in (WH, WL))
                    mm(bank[m % 4][:, :], wl, xh, start=(k == 0), stop=False)
                    mm(bank[m % 4][:, :], wh, xh, start=False, stop=False)
                    last = mm(bank[m % 4][:, :], wh, xl, start=False, stop=(k == 11))
                    if b % BLOCKS == BLOCKS - 1:
                        last.then_inc(unit_done, 1)
                    elif k == 11:
                        last.then_inc(r["yms"], 1)
            sum_squares(4)
            ffn(U_UPB, U_DNB, NJ2, NJ1 + NJ2, 5, False, 48)
            sum_squares(5)

        @block.scalar
        def _(act):
            A = nc.scalar.activation

            def norm(n, eps):
                A(sqrt_scratch[:, :], one[:, :], ACT.Sqrt)
                act.wait_ge(ms_done, n + 1)
                A(RS[:, 0:NT], bank[SUM_BANK[n]][:, 0:NT], ACT.Sqrt, bias=eps[:, :], scale=1.0 / D).then_inc(rt_done, 1)

            def weight_high(base, loc, i=0, stride=0):
                u = base + loc
                act.wait_ge(arrived[u % RING], i * (16 * (stride // RING)) + 16 * (u // RING + 1))
                A(WH[:, split_at(base, loc)[1], :], ring[:, u % RING, :], ACT.Copy).then_inc(w_high, 1)

            def weights_only(base, units, body=4):
                with act.Fori(0, units // body) as i:
                    for j in range(body):
                        act.wait_ge(unit_done, i * body + (base + j + 1))
                        weight_high(base, j + 2, i, body)

            def high(n, col=None):
                for k in range(KD):
                    act.wait_ge(h_mul, 8 * n + k + 1)
                    if col is None:
                        A(tile_of(HH, k), tile_of(MIX, k), ACT.Copy).then_inc(h_high, 1)
                    else:
                        A(tile_of(HH, k), tile_of(MIX, k), ACT.Identity, bias=MOD[:, col + k:col + k + 1]).then_inc(h_high, 1)

            def high_of_mix(done, before):
                for k in range(KD):
                    act.wait_ge(done, before + k + 1)
                    A(tile_of(HH, k), tile_of(MIX, k), ACT.Copy).then_inc(h_high, 1)

            for s_, by in ((up_act, 2), (q["rg_sig"], 1), (q["ig_sig"], 1), (r["t_evac"], 3)):
                act.sem_inc(s_, by)
            act.wait_ge(vec_in_s, 16)
            act.wait_ge(prep_v, 1)
            lam = v("rg_lambda", 0, HEADS)
            A(lam_t[:, 0:8], lam, ACT.Abs).then_inc(prep_a, 1)
            act.wait_ge(prep_a, 1)
            A(lam_t[:, 8:16], lam_t[:, 0:8], ACT.Exp, scale=-1.0).then_inc(prep_a, 1)
            act.wait_ge(prep_a, 2)
            A(lam_t[:, 16:24], lam_t[:, 8:16], ACT.Ln, bias=one[:, :]).then_inc(prep_a, 1)
            A(aneg[:, :], v("a_log_2"), ACT.Exp).then_inc(prep_a, 1)
            act.wait_ge(consts, 1)
            A(negones_r[:, :], negones[:, :], ACT.Copy).then_inc(signs, 1)
            A(negtri_r[:, :], negtri[:, :], ACT.Copy).then_inc(signs, 1)
            act.wait_ge(x_in_s, 16)
            for k in range(KD):
                A(tile_of(MIX, k), tile_of(XT, k), ACT.Square).then_inc(sq0_done, 1)
            norm(0, eps1)
            weight_high(U_HEAD, 0)
            weight_high(U_HEAD, 1)
            act.wait_ge(mod_done, 1)
            high(0, 0)

            M = mixer1_tiles()
            with act.Fori(0, HEADS) as h:
                def finished(loc):
                    act.wait_ge(unit_done, h * HEAD_UNITS + (U_HEAD + loc + 1))

                finished(Q)
                A(M["QR"], bank[0][:, :], ACT.Copy).then_inc(q["q_evac"], 1)
                A(M["QSQ"], bank[0][:, :], ACT.Square).then_inc(q["q_evac"], 1)
                weight_high(U_HEAD, V, h, HEAD_UNITS)
                finished(K)
                weight_high(U_HEAD, XR, h, HEAD_UNITS)
                A(M["KR"], bank[1][:, :], ACT.Copy).then_inc(q["k_evac"], 1)
                A(M["KSQ"], bank[1][:, :], ACT.Square).then_inc(q["k_evac"], 1)
                finished(V)
                weight_high(U_HEAD, YR, h, HEAD_UNITS)
                A(M["VF"], bank[5][:, :], ACT.Copy).then_inc(q["v_evac"], 1)
                act.wait_ge(q["q_ms"], h + 1)
                A(M["RQ"], bank[0][:, :], ACT.Sqrt, bias=eps1[:, :], scale=1.0 / P).then_inc(q["rq_done"], 1)
                act.wait_ge(q["k_ms"], h + 1)
                A(M["RK"], bank[1][:, :], ACT.Sqrt, bias=eps1[:, :], scale=1.0 / P).then_inc(q["rk_done"], 1)
                finished(XR)
                A(M["XR"][:, 3:3 + S], bank[7][:, :], ACT.Copy).then_inc(q["xr_evac"], 1)
                weight_high(U_HEAD, GA, h, HEAD_UNITS)
                act.wait_ge(q["v_tr"], h + 1)
                A(M["VT"], bank[2][:, :], ACT.Copy).then_inc(q["v_evac"], 1)
                finished(YR)
                weight_high(U_HEAD, GB, h, HEAD_UNITS)
                A(M["GY"], bank[5][:, :], ACT.Gelu_apprx_tanh).then_inc(q["gy_done"], 1)
                act.wait_ge(q["z_done"], h + 1)
                for b, w, at in BANK_PART:
                    A(M["AZ"][:, at:at + w], bank[2 + b][:, 0:w], ACT.Abs).then_inc(q["absz_done"], 1)
                act.wait_ge(q["absz_done"], 3 * h + 3)
                A(M["EZ"], M["AZ"], ACT.Exp, scale=-1.0).then_inc(q["ez_done"], 1)
                act.wait_ge(q["ez_done"], h + 1)
                A(M["LP"], M["EZ"], ACT.Ln, bias=one[:, :]).then_inc(q["lnp_done"], 1)
                finished(GA)
                A(M["SGA"], bank[7][:, :], ACT.Sigmoid).then_inc(q["sga_done"], 1)
                act.wait_ge(q["r_mm"], h + 1)
                A(M["RG"], bank[1][:, :], ACT.Sigmoid, bias=vd("rg_ba", h)).then_inc(q["rg_sig"], 1)
                finished(GATES)
                A(M["IG"], bank[5][:, :], ACT.Sigmoid, bias=vd("rg_bx", h)).then_inc(q["ig_sig"], 1)
                act.wait_ge(q["rg_sig"], h + 2)
                A(M["TH"], M["RG"], ACT.Tanh, scale=nc8[:, bass.ds(h, 1)]).then_inc(q["th_dec"], 1)
                act.wait_ge(q["p_done"], 3 * h + 3)
                A(M["PH"], M["PP"], ACT.Copy).then_inc(q["ph_done"], 1)
                finished(GB)
                weight_high(U_HEAD, HEAD_UNITS + Q, h, HEAD_UNITS)
                A(M["SGB"], bank[0][:, :], ACT.Sigmoid).then_inc(q["sgb_done"], 1)
                weight_high(U_HEAD, HEAD_UNITS + K, h, HEAD_UNITS)
                A(M["AD"], M["RG"], ACT.Exp, scale=c8[:, bass.ds(h, 1)]).then_inc(q["a_dec"], 1)
                act.wait_ge(q["s_done"], h + 1)
                for b, w, at in BANK_PART:
                    A(M["AT"][:, at:at + w], bank[2 + b][:, 0:w], ACT.Exp).then_inc(q["att_done"], 1)
                act.wait_ge(q["m2_done"], h + 1)
                A(M["ML"], M["M2"], ACT.Sqrt).then_inc(q["mult_done"], 1)

            high_of_mix(q["mix_done"], 0)
            weights_only(U_OUT1, 8)
            norm(1, eps1)
            high(1, 24)
            with act.Fori(0, NJ1 // 2) as i:
                for jl in range(2):
                    for n, T in ((0, CG), (1, CV)):
                        j = i * 2 + (jl + NJ1 * n)
                        act.wait_ge(unit_done, i * 4 + (U_UP1 + 2 * jl + n + 1))
                        weight_high(U_UP1, 2 * jl + n + 2, i, 4)
                        if n:
                            act.wait_ge(ff_done, i * 2 + (jl + 1))
                        A(T[:, jl, :], bank[2 * jl + n][:, :], ACT.Identity, bias=vd("ffn_conv_b", j),
                          scale=vd("ffn_conv_w", j + 2 * 48)).then_inc(cgv_act, 1)
                    act.wait_ge(cg_dve, i * 4 + (2 * jl + 2 + 4))
                    A(TG[:, jl, :], CG[:, jl, :], ACT.Gelu_apprx_tanh).then_inc(up_act, 1)
                    act.wait_ge(f_tmp, i * 2 + (jl + 1))
                    A(tile_of(FH, i * 2 + jl), TG[:, jl, :], ACT.Copy).then_inc(f_high, 1)
            weights_only(U_DN1, 24)
            norm(2, eps2)
            high(2)

            def ffn(u_up, before):
                with act.Fori(0, NJ2 // 2) as i:
                    for jl in range(2):
                        act.wait_ge(unit_done, i * 4 + (u_up + 2 * jl + 1))
                        weight_high(u_up, 2 * jl + 2, i, 4)
                        act.wait_ge(ff_done, i * 2 + (before + jl + 1))
                        A(TG[:, jl, :], bank[2 * jl][:, :], ACT.Silu).then_inc(up_act, 1)
                        act.wait_ge(unit_done, i * 4 + (u_up + 2 * jl + 2))
                        weight_high(u_up, 2 * jl + 3, i, 4)
                        act.wait_ge(f_tmp, i * 2 + (before + jl + 1))
                        A(tile_of(FH, i * 2 + jl), TG[:, jl, :], ACT.Copy).then_inc(f_high, 1)
            ffn(U_UPA, NJ1)
            weights_only(U_DNA, 24)
            norm(3, eps2)
            high(3)

            N = mixer2_tiles()
            for n in range(4):
                act.wait_ge(unit_done, U_BC + n + 1)
                weight_high(U_BC, n + 2)
                if n:
                    act.wait_ge(r["bc_silu"], n)
                A(N["BC"], bank[n][:, :], ACT.Identity, bias=v("conv_b_2", 8 + n),
                  scale=v("conv_w_2", 3 * 12 + 8 + n)).then_inc(r["bc_conv"], 1)
                act.wait_ge(r["bc_tap"], 3 * n + 3)
                T = N["BT"] if n < 2 else N["CT"]
                A(T[:, (n % 2) * S:(n % 2 + 1) * S], N["BC"], ACT.Silu).then_inc(r["bc_silu"], 1)
            act.wait_ge(unit_done, U_BC + 5)
            weight_high(U_BC, 6)
            A(N["DZ"], bank[4][:, :], ACT.Identity, bias=v("dt_bias_2")).then_inc(r["dt_z"], 1)
            act.wait_ge(r["dt_z"], 1)
            A(N["DE"], N["DZ"], ACT.Abs).then_inc(r["dt_abs"], 1)
            act.wait_ge(r["dt_abs"], 1)
            A(N["DE"], N["DE"], ACT.Exp, scale=-1.0).then_inc(r["dt_exp"], 1)
            act.wait_ge(r["dt_exp"], 1)
            A(N["DE"], N["DE"], ACT.Ln, bias=one[:, :]).then_inc(r["dt_ln"], 1)

            def conv(a, b, loc, t, it=0):
                act.wait_ge(unit_done, it * PAIR_UNITS + (U_PAIR + loc + 1))
                weight_high(U_PAIR, loc + 2, it, PAIR_UNITS)
                act.wait_ge(r["y_skip"], 2 * t + a + 1)
                A(N["XS"][a], bank[b][:, :], ACT.Identity, bias=vd("conv_b_2", t + 4 * a),
                  scale=vd("conv_w_2", t + (3 * 12 + 4 * a))).then_inc(r["xs_conv"], 1)

            def silu(a, t):
                act.wait_ge(r["xs_tap"], 6 * t + 3 * a + 3)
                A(N["XS"][a], N["XS"][a], ACT.Silu).then_inc(r["xs_silu"], 1)

            def silu_z(a, b, t):
                act.wait_ge(r["yz_done"], 2 * t + a + 1)
                A(N["ZS"][a], bank[b][:, :], ACT.Silu).then_inc(r["z_silu"], 1)

            def g_evac(g):
                act.wait_ge(r["g_mm"], g + 1)
                for b, w, at in BANK_PART:
                    A(N["GS"][:, g * TRI + at:g * TRI + at + w], bank[b][:, 0:w], ACT.Copy).then_inc(r["g_evac"], 1)

            conv(0, 6, 0, 0)
            g_evac(0)
            silu(0, 0)
            act.wait_ge(unit_done, U_PAIR + 2)
            weight_high(U_PAIR, 3)
            silu_z(0, 7, 0)
            act.wait_ge(r["tr_dt"], 1)
            A(N["DTT"], bank[5][:, 0:64], ACT.Copy).then_inc(r["tr_evac"], 1)
            A(N["CST"], bank[5][:, 64:128], ACT.Copy).then_inc(r["tr_evac"], 1)
            A(N["CSH"], N["CS"], ACT.Copy).then_inc(r["cs_done"], 1)
            g_evac(1)

            def next_q(loc, it=0):
                act.wait_ge(unit_done, it * PAIR_UNITS + (U_PAIR + loc + 1))
                weight_high(U_PAIR, loc + 2, it, PAIR_UNITS)
                A(N["Q2"], bank[4][:, :], ACT.Copy, scale=0.125).then_inc(r["qk_evac"], 1)
            next_q(2)

            def pair(t, is_last):
                def finished(loc):
                    act.wait_ge(unit_done, t * PAIR_UNITS + (U_PAIR + loc + 1))

                def decay(a, hh):
                    act.wait_ge(r["dd_done"], 16 * t + 8 * a + 4 * hh + 4)
                    A(N[f"ED{hh}"], N[f"ED{hh}"], ACT.Exp).then_inc(r["ed_done"], 1)

                def soften(hh):
                    act.wait_ge(r["s_neg"], 2 * t + hh + 1)
                    for i in range(NT):
                        at, w = SEG_OFF[3 - i], (i + 1) * P
                        A(N["SC"][:, at:at + w], N["SC"][:, at:at + w], ACT.Exp, bias=N["nmx"][:, i:i + 1],
                          accum_out=N["sm"][:, i:i + 1]).then_inc(r["s_exp"], 1)

                def turned(hh):
                    act.wait_ge(r["t_mm"], 2 * t + hh + 1)
                    for b, w, at in BANK_PART:
                        A(N["PT"][:, at:at + w], bank[(5, 6, 0)[b]][:, 0:w], ACT.Copy).then_inc(r["t_evac"], 1)

                finished(3)
                weight_high(U_PAIR, 5, t, PAIR_UNITS)
                A(N["K2"], bank[6][:, :], ACT.Copy).then_inc(r["qk_evac"], 1)
                decay(0, 0)
                decay(0, 1)
                conv(1, 7, 4, t, t)
                soften(0)
                finished(5)
                A(N["VF"], bank[1][:, :], ACT.Copy).then_inc(r["v_evac"], 1)
                silu(1, t)
                act.wait_ge(r["v_tr"], t + 1)
                A(N["V2"], bank[1][:, :], ACT.Copy).then_inc(r["v_evac"], 1)
                turned(0)
                decay(1, 0)
                decay(1, 1)
                finished(6)
                weight_high(U_PAIR, 8, t, PAIR_UNITS)
                weight_high(U_PAIR, 9, t, PAIR_UNITS)
                silu_z(1, 1, t)
                soften(1)
                if is_last:
                    act.wait_ge(r["yms"], 1)
                    A(RS[:, 0:NT], bank[4][:, 0:NT], ACT.Sqrt, bias=eps2[:, :], scale=1.0 / D).then_inc(r["yrt"], 1)
                    turned(1)
                else:
                    conv(0, 3, 8, t + 1, t)
                    finished(9)
                    weight_high(U_PAIR, 11, t, PAIR_UNITS)
                    turned(1)
                    silu(0, t + 1)
                    silu_z(0, 1, t + 1)
                    next_q(10, t)
                act.wait_ge(r["pv_mm"], 2 * t + 2)
                A(tile_of(MH, t), bank[7][:, :], ACT.Copy).then_inc(r["o_high"], 1)

            with act.Fori(0, 3) as t:
                pair(t, False)
            pair(3, True)
            high_of_mix(r["ynorm"], 0)
            for n in range(12):
                act.wait_ge(unit_done, U_OUT2 + n + 1)
                weight_high(U_OUT2, n + 2)
            norm(4, eps2)
            high(4)
            ffn(U_UPB, NJ1 + NJ2)
            weights_only(U_DNB, 20)
            for n in (20, 21):
                act.wait_ge(unit_done, U_DNB + n + 1)
                weight_high(U_DNB, n + 2)
            norm(5, eps2)

        @block.vector
        def _(dve):
            V = nc.vector
            TT = V.tensor_tensor

            def STT(out_ap, in0, scalar, in1, op0, op1):
                return V.scalar_tensor_tensor(out=out_ap, in0=in0, scalar=scalar, in1=in1, op0=op0, op1=op1)

            def clear_ss(n):
                V.memset(SS[:, :], 0.0).then_inc(ss_clear, 1)
                dve.wait_ge(ss_clear, n)

            def low(k, before, x, shift=None):
                dve.wait_ge(h_high, before + k + 1)
                high = tile_of(HH, k).bitcast(F32)
                if shift is None:
                    TT(tile_of(HL, k), x, high, ALU.subtract).then_inc(h_low, 1)
                else:
                    STT(tile_of(HL, k), x, shift(k), high, ALU.add, ALU.subtract).then_inc(h_low, 1)

            def inverse_diagonal(recip_done, count, diag_done):
                V.reciprocal(RS[:, NT:2 * NT], RS[:, 0:NT]).then_inc(recip_done, 1)
                dve.wait_ge(recip_done, count)
                TT(RT[:, :].rearrange("p (i m) -> p i m", m=P), ident[:, :].unsqueeze(1).to_broadcast([P, NT, P]),
                   RS[:, NT:2 * NT].unsqueeze(2).to_broadcast([P, NT, P]), ALU.mult).then_inc(diag_done, 1)

            def inverse(n):
                dve.wait_ge(rt_done, n + 1)
                inverse_diagonal(rc_done, n + 1, dg_done)

            def norm(n, gain, before, shift=None):
                if n:
                    inverse(n)
                dve.wait_ge(rs_done, n + 1)
                for k in range(KD):
                    STT(tile_of(MIX, k), tile_of(XT, k), gain(k), bank[SUM_BANK[n]][:, :], ALU.mult, ALU.mult).then_inc(h_mul, 1)
                for k in range(POOL_TILES if before in POOL_LOW else 0, KD):
                    low(k, before, tile_of(MIX, k), shift)

            def low_of_mix(before):
                for k in range(POOL_TILES, KD):
                    low(k, before, tile_of(MIX, k))

            def residual(n, first_unit, per, gate, banks, one_more=None):
                clear_ss(CLEAR[n])
                with dve.Fori(0, 2) as i:
                    for m in range(4):
                        dve.wait_ge(unit_done, i * (4 * per) + (first_unit + per * (m + 1)))
                        x = tile_of(XT, i * 4 + m)
                        g = gate(i * 4 + m)
                        STT(x, bank[banks + m][:, :], g, x, ALU.mult, ALU.add).then_inc(res_done, 1)
                        dve.wait_ge(res_done, i * 4 + (8 * n + m + 1))
                        if m == 3:
                            TT(CG[:, i, :] if isinstance(i, int) else CG[:, bass.ds(i, 1), :].rearrange("p a n -> p (a n)"),
                               x, x, ALU.mult).then_inc(sq_done, 1)
                            continue
                        TT(SQ[:, :], x, x, ALU.mult).then_inc(sq_done, 1)
                        dve.wait_ge(sq_done, i * 4 + (SQ_BEFORE[n] + m + 1))
                        TT(SS[:, :], SS[:, :], SQ[:, :], ALU.add).then_inc(ss_done, 1)
                        dve.wait_ge(ss_done, i * 3 + (SS_BEFORE[n] + m + 1))

            CLEAR = [0, 1, 2, 3, 5, 6]

            for s_, by in ((ff_done, 2), (cg_dve, 4), (cv_dve, 4), (q["yb_done"], 1), (r["y_skip"], 2), (r["yz_done"], 2), (r["xd_done"], 1),
                          (r["o_low"], 1)):
                dve.sem_inc(s_, by)
            M = mixer1_tiles()
            V.memset(eps1[:, :], EPS1)
            V.memset(eps2[:, :], EPS2)
            V.memset(zero[:, :], 0.0)
            V.memset(one[:, :], 1.0).then_inc(prep_v, 1)
            for s_ in (res_done, sq_done, ss_done):
                dve.sem_inc(s_, 8)
            dve.wait_ge(vec_in_s, 16)

            def ada(unit, n, i=0, per=0):
                TT(TG[:, :, :].rearrange("p a n -> p (a n)").rearrange("p (k m) -> p k m", m=P),
                   unit.rearrange("p (k m) -> p k m", m=P),
                   v("c", 0, KD).unsqueeze(2).to_broadcast([P, KD, P]), ALU.mult).then_inc(ada_mul, 1)
                dve.wait_ge(ada_mul, i * per + (n + 1))
                V.tensor_reduce(ADA[:, (n % 4) * P:(n % 4 + 1) * P],
                                TG[:, :, :].rearrange("p a n -> p (a n)").rearrange("p (k m) -> p m k", m=P),
                                AX.X, ALU.add).then_inc(ada_sum, 1)
                dve.wait_ge(ada_sum, i * per + (n + 1))

            for n, col in enumerate(ADA_BY_DVE):
                if n >= 4:
                    used = ADA_BY_DVE[n - 4]
                    if used < RING:
                        dve.wait_ge(unit_done, used + 1)
                    else:
                        dve.wait_ge(ada_col, used - RING + 1)
                if col < RING:
                    dve.wait_ge(arrived[col], 16)
                else:
                    dve.wait_ge(ada_arrived[(col - RING) // 2], 16)
                ada(first_unit(col), n)
            dve.wait_ge(prep_a, 4)
            V.tensor_scalar(lam_t[:, 0:8], v("rg_lambda", 0, HEADS), -1.0, 0.0, ALU.mult, ALU.max).then_inc(prep_v, 1)
            dve.wait_ge(prep_v, 2)
            TT(lam_t[:, 0:8], lam_t[:, 0:8], lam_t[:, 16:24], ALU.add).then_inc(prep_v, 1)
            dve.wait_ge(prep_v, 3)
            V.tensor_scalar(c8[:, :], lam_t[:, 0:8], -8.0, None, ALU.mult).then_inc(prep_v, 1)
            V.tensor_scalar(nc8[:, :], lam_t[:, 0:8], 8.0, None, ALU.mult).then_inc(prep_v, 1)
            V.tensor_scalar(qg[:, :], v("q_norm_g"), float(P) ** -0.5, None, ALU.mult).then_inc(prep_v, 1)
            V.tensor_scalar(aneg[:, :], aneg[:, :], -1.0, None, ALU.mult).then_inc(prep_v, 1)
            inverse(0)
            dve.wait_ge(unit_done, U_HEAD)
            dve.wait_ge(ada_col, ADA_FIRST - RING)
            V.memset(M["XR"][:, 0:3], 0.0)
            TT(MOD[:, 0:16], bank[6][:, 0:16], v("ada_b", 0, 16), ALU.add).then_inc(mod_done, 1)
            dve.wait_ge(mod_done, 1)
            STT(G1[:, :], MOD[:, 8:16], one[:, :], v("norm1_g", 0, KD), ALU.add, ALU.mult).then_inc(prep_v, 1)
            dve.wait_ge(prep_v, 8)
            norm(0, lambda k: G1[:, k:k + 1], 0, lambda k: MOD[:, k:k + 1])

            with dve.Fori(0, HEADS) as h:
                def head_ada(j):
                    u = U_HEAD + HEAD_ADA[j]
                    dve.wait_ge(arrived[u % RING], h * (16 * (HEAD_UNITS // RING)) + 16 * (u // RING + 1))
                    ada(ring[:, u % RING, :], N_FIRST + j, h, 4)

                for j in range(4):
                    head_ada(j)
                dve.wait_ge(q["rq_done"], h + 1)
                V.reciprocal(M["RSQ"], M["RQ"]).then_inc(q["rsq"], 1)
                dve.wait_ge(q["rsq"], h + 1)
                STT(M["QN"], M["QR"], qg[:, :], M["RSQ"], ALU.mult, ALU.mult).then_inc(q["qn_done"], 1)
                dve.wait_ge(q["rk_done"], h + 1)
                V.reciprocal(M["RSK"], M["RK"]).then_inc(q["rsk"], 1)
                dve.wait_ge(q["rsk"], h + 1)
                STT(M["KN"], M["KR"], v("k_norm_g"), M["RSK"], ALU.mult, ALU.mult).then_inc(q["kn_done"], 1)
                dve.wait_ge(q["xr_evac"], h + 1)
                V.tensor_scalar(M["XC"], M["XR"][:, 0:S], vd("conv_w", h), vd("conv_b", h), ALU.mult, ALU.add).then_inc(q["conv_done"], 1)
                for k in range(1, 4):
                    dve.wait_ge(q["conv_done"], 4 * h + k)
                    STT(M["XC"], M["XR"][:, k:k + S], vd("conv_w", h + 8 * k), M["XC"], ALU.mult, ALU.add).then_inc(q["conv_done"], 1)
                dve.wait_ge(q["lnp_done"], h + 1)
                for b, w, at in BANK_PART:
                    STT(M["PP"][:, at:at + w], bank[2 + b][:, 0:w], zero[:, :], M["LP"][:, at:at + w], ALU.max, ALU.add).then_inc(q["p_done"], 1)
                dve.wait_ge(q["ph_done"], h + 1)
                TT(M["PL"], M["PP"], M["PH"].bitcast(F32), ALU.subtract).then_inc(q["pl_done"], 1)
                dve.wait_ge(w_high, h * 7 + 8)
                TT(WL[:, 0, :], ring[:, (U_HEAD + HEAD_UNITS) % RING, :], WH[:, 0, :].bitcast(F32), ALU.subtract).then_inc(w_low, 1)
                dve.wait_ge(q["a_dec"], h + 1)
                TT(M["A2"], M["AD"], M["AD"], ALU.mult).then_inc(q["a2_done"], 1)
                dve.wait_ge(q["th_dec"], h + 1)
                dve.wait_ge(q["a2_done"], h + 1)
                STT(M["M2"], M["A2"], one[:, :], M["TH"], ALU.add, ALU.mult).then_inc(q["m2_done"], 1)
                dve.wait_ge(q["conv_done"], 4 * h + 4)
                dve.wait_ge(q["ig_sig"], h + 2)
                TT(M["IX"], M["IG"], M["XC"], ALU.mult).then_inc(q["ix_done"], 1)
                dve.wait_ge(q["ix_done"], h + 1)
                dve.wait_ge(q["mult_done"], h + 1)
                TT(M["U"], M["ML"], M["IX"], ALU.mult).then_inc(q["u_done"], 1)
                dve.wait_ge(q["u_done"], h + 1)
                V.tensor_tensor_scan(M["HS"], M["AD"], M["U"], 0.0, ALU.mult, ALU.add).then_inc(q["scan_done"], 1)
                dve.wait_ge(q["scan_done"], h + 1)
                dve.wait_ge(q["gy_done"], h + 1)
                TT(M["YA"], M["HS"], M["GY"], ALU.mult).then_inc(q["ya_done"], 1)
                dve.wait_ge(q["ya_done"], 2 * h + 1)
                dve.wait_ge(q["sga_done"], h + 1)
                TT(M["YA"], M["YA"], M["SGA"], ALU.mult).then_inc(q["ya_done"], 1)
                dve.wait_ge(q["pv_done"], h + 1)
                dve.wait_ge(q["sgb_done"], h + 1)
                TT(M["YB"], bank[7][:, :], M["SGB"], ALU.mult).then_inc(q["yb_done"], 1)
                dve.wait_ge(q["ya_done"], 2 * h + 2)
                dve.wait_ge(q["yb_done"], h + 2)
                TT(tile_of(MIX, h), M["YA"], M["YB"], ALU.add).then_inc(q["mix_done"], 1)

            dve.wait_ge(unit_done, U_OUT1)
            TT(MOD[:, 16:48], bank[6][:, 16:48], v("ada_b", 16, 32), ALU.add).then_inc(mod_done, 1)
            dve.wait_ge(mod_done, 2)
            STT(G2[:, :], MOD[:, 32:40], one[:, :], v("norm2_g", 0, KD), ALU.add, ALU.mult).then_inc(prep_v, 1)
            dve.wait_ge(prep_v, 9)
            low_of_mix(8)
            residual(1, U_OUT1, 1, lambda m: MOD[:, bass.ds(m + 16, 1)], 0)
            norm(1, lambda k: G2[:, k:k + 1], 16, lambda k: MOD[:, 24 + k:25 + k])

            with dve.Fori(0, NJ1 // 2) as i:
                for jl in range(2):
                    for n, T, tap_done in ((0, CG, cg_dve), (1, CV, cv_dve)):
                        j = i * 2 + (jl + NJ1 * n)
                        dve.wait_ge(cgv_act, i * 4 + (2 * jl + n + 1))
                        for k in (1, 2):
                            STT(T[:, jl, k:S], bank[2 * jl + n][:, 0:S - k], vd("ffn_conv_w", j + (2 - k) * 48), T[:, jl, k:S],
                                ALU.mult, ALU.add).then_inc(tap_done, 1)
                            dve.wait_ge(tap_done, i * 4 + (4 + 2 * jl + k))
                    dve.wait_ge(up_act, i * 2 + (2 + jl + 1))
                    TT(TG[:, jl, :], TG[:, jl, :], CV[:, jl, :], ALU.mult).then_inc(f_tmp, 1)
                    dve.wait_ge(f_high, i * 2 + (jl + 1))
                    TT(tile_of(FL, i * 2 + jl), TG[:, jl, :], tile_of(FH, i * 2 + jl).bitcast(F32), ALU.subtract).then_inc(ff_done, 1)
            residual(2, U_DN1, 3, lambda m: MOD[:, bass.ds(m + 40, 1)], 4)
            norm(2, lambda k: v("ffn1_norm_2", k), 24)

            def ffn(u_up, before):
                with dve.Fori(0, NJ2 // 2) as i:
                    for jl in range(2):
                        dve.wait_ge(unit_done, i * 4 + (u_up + 2 * jl + 2))
                        dve.wait_ge(up_act, i * 2 + (2 + before + jl + 1))
                        TT(TG[:, jl, :], TG[:, jl, :], bank[2 * jl + 1][:, :], ALU.mult).then_inc(f_tmp, 1)
                        dve.wait_ge(f_high, i * 2 + (before + jl + 1))
                        TT(tile_of(FL, i * 2 + jl), TG[:, jl, :], tile_of(FH, i * 2 + jl).bitcast(F32), ALU.subtract).then_inc(ff_done, 1)
            ffn(U_UPA, NJ1)
            residual(3, U_DNA, 3, lambda m: 0.5, 4)
            norm(3, lambda k: v("mix_norm_2", k), 32)

            N = mixer2_tiles()
            for n in range(4):
                dve.wait_ge(r["bc_conv"], n + 1)
                for k in (1, 2, 3):
                    STT(N["BC"][:, k:S], bank[n][:, 0:S - k], v("conv_w_2", (3 - k) * 12 + 8 + n), N["BC"][:, k:S],
                        ALU.mult, ALU.add).then_inc(r["bc_tap"], 1)
                    dve.wait_ge(r["bc_tap"], 3 * n + k)
            dve.wait_ge(r["dt_ln"], 1)
            STT(N["DT"], N["DZ"], zero[:, :], N["DE"], ALU.max, ALU.add).then_inc(r["dt_sp"], 1)
            dve.wait_ge(r["dt_sp"], 1)
            V.tensor_scalar(N["LA"], N["DT"], aneg[:, :], None, ALU.mult).then_inc(r["dt_la"], 1)
            dve.wait_ge(r["dt_la"], 1)
            V.memset(SQ[:, :], 1.0).then_inc(r["dt_la"], 1)
            dve.wait_ge(r["dt_la"], 2)
            V.tensor_tensor_scan(N["CS"], SQ[:, :], N["LA"], 0.0, ALU.mult, ALU.add).then_inc(r["cs_done"], 1)
            dve.wait_ge(r["cs_done"], 1)
            clear_ss(4)

            def taps(a, b, t):
                dve.wait_ge(r["xs_conv"], 2 * t + a + 1)
                for k in (1, 2, 3):
                    STT(N["XS"][a][:, k:S], bank[b][:, 0:S - k], vd("conv_w_2", t + ((3 - k) * 12 + 4 * a)),
                        N["XS"][a][:, k:S], ALU.mult, ALU.add).then_inc(r["xs_tap"], 1)
                    dve.wait_ge(r["xs_tap"], 6 * t + 3 * a + k)

            def select(a, hh, t, reused=True):
                if reused:
                    dve.wait_ge(r["csb_done"], 4 * t + 2 * a + hh - 1)
                V.tensor_copy(N["SELH"][:, hh * P:(hh + 1) * P],
                              ident[:, bass.ds(t * 2 + (8 * a + hh), 1)].to_broadcast([P, P])).then_inc(r["sel_done"], 1)

            taps(0, 6, 0)
            select(0, 0, 0, False)
            select(0, 1, 0, False)
            dve.wait_ge(r["tr_evac"], 2)
            dve.wait_ge(r["cs_done"], 2)
            TT(N["CSL"], N["CS"], N["CSH"].bitcast(F32), ALU.subtract).then_inc(r["cs_done"], 1)

            def pair(t, is_last):
                def with_dt(a, b):
                    dve.wait_ge(r["xs_tr"], 2 * t + a + 1)
                    dtt = N["DTT"].rearrange("p (i h) -> p i h", h=16)[:, :, bass.ds(t * 2 + 8 * a, 2)]
                    TT(N["XD"][a].rearrange("p (i h c) -> p i h c", i=NT, h=2),
                       bank[b][:, :].rearrange("p (i h c) -> p i h c", i=NT, h=2),
                       dtt.unsqueeze(3).to_broadcast([P, NT, 2, 64]), ALU.mult).then_inc(r["xd_done"], 1)

                def distance(a, hh, b):
                    n = 4 * t + 2 * a + hh
                    dve.wait_ge(r["csb_done"], n + 1)
                    for i in range(NT):
                        V.tensor_scalar(N[f"ED{hh}"][:, SEG_OFF[i]:SEG_OFF[i] + SEG_W[i]], bank[b][:, i * P:S],
                                        N["CST"][:, bass.ds(t * 2 + (i * 16 + 8 * a + hh), 1)], 0.0,
                                        ALU.subtract, ALU.min).then_inc(r["dd_done"], 1)

                def times_g(a, hh):
                    dve.wait_ge(r["ed_done"], 4 * t + 2 * a + hh + 1)
                    dve.wait_ge(r["g_mask"], 4 * a + 4)
                    TT(N[f"ED{hh}"], N[f"ED{hh}"], N["GS"][:, a * TRI:(a + 1) * TRI], ALU.mult).then_inc(r["mm_done"], 1)

                def skip(a):
                    n = 2 * t + a
                    dve.wait_ge(r["y_mm"], 2 * n + 2)
                    dve.wait_ge(r["xs_silu"], n + 1)
                    STT(N["YY"], N["XS"][a], vd("d_skip_2", t + 4 * a), bank[2][:, :], ALU.mult, ALU.add).then_inc(r["y_skip"], 1)

                def gate(a):
                    n = 2 * t + a
                    dve.wait_ge(r["y_skip"], n + 3)
                    dve.wait_ge(r["z_silu"], n + 1)
                    y = tile_of(MIX, t + 4 * a)
                    TT(y, N["YY"], N["ZS"][a], ALU.mult).then_inc(r["yz_done"], 1)
                    dve.wait_ge(r["yz_done"], n + 3)
                    TT(SQ[:, :], y, y, ALU.mult).then_inc(sq_done, 1)
                    dve.wait_ge(sq_done, n + 33)
                    TT(SS[:, :], SS[:, :], SQ[:, :], ALU.add).then_inc(r["yss_done"], 1)
                    dve.wait_ge(r["yss_done"], n + 1)

                def biased_max(hh):
                    dve.wait_ge(r["s_mm"], 2 * t + hh + 1)
                    if hh == 0:
                        u = U_PAIR + 7
                        dve.wait_ge(arrived[u % RING], t * (16 * PAIR_UNITS // RING) + 16 * (u // RING + 1))
                    for i in range(NT):
                        b, c = SEG_BANK[3 - i]
                        at, w = SEG_OFF[3 - i], (i + 1) * P
                        TT(N["SC"][:, at:at + w], bank[(5, 6, 0)[b]][:, c:c + w],
                           ring[:, (U_PAIR + 7) % RING, hh * S + (NT - 1 - i) * P:(hh + 1) * S], ALU.add).then_inc(r["s_add"], 1)
                    dve.wait_ge(r["s_add"], 8 * t + 4 * hh + 4)
                    for i in range(NT):
                        at, w = SEG_OFF[3 - i], (i + 1) * P
                        V.tensor_reduce(N["mx"][:, i:i + 1], N["SC"][:, at:at + w], AX.X, ALU.max).then_inc(r["s_max"], 1)
                    dve.wait_ge(r["s_max"], 8 * t + 4 * hh + 4)
                    V.tensor_scalar(N["nmx"], N["mx"], -1.0, None, ALU.mult).then_inc(r["s_neg"], 1)

                def normalise(hh):
                    dve.wait_ge(r["s_exp"], 8 * t + 4 * hh + 4)
                    V.reciprocal(N["rsm"], N["sm"]).then_inc(r["s_rec"], 1)
                    dve.wait_ge(r["s_rec"], 2 * t + hh + 1)
                    for i in range(NT):
                        at, w = SEG_OFF[3 - i], (i + 1) * P
                        V.tensor_scalar(N["SC"][:, at:at + w], N["SC"][:, at:at + w], N["rsm"][:, i:i + 1], None,
                                        ALU.mult).then_inc(r["s_nrm"], 1)

                with_dt(0, 2)
                distance(0, 0, 3)
                distance(0, 1, 4)
                select(1, 0, t)
                select(1, 1, t)
                times_g(0, 0)
                times_g(0, 1)
                biased_max(0)
                taps(1, 7, t)
                normalise(0)
                skip(0)
                distance(1, 0, 3)
                distance(1, 1, 4)
                with_dt(1, 7)
                if not is_last:
                    select(0, 0, t + 1)
                    select(0, 1, t + 1)
                times_g(1, 0)
                times_g(1, 1)
                gate(0)
                biased_max(1)
                skip(1)
                gate(1)
                normalise(1)
                def ssd_norm(tiles):
                    for k in tiles:
                        STT(tile_of(MIX, k), tile_of(MIX, k), v("ssd_norm_2", k), bank[4][:, :], ALU.mult, ALU.mult).then_inc(r["ynorm"], 1)

                if is_last:
                    dve.wait_ge(r["yrt"], 1)
                    inverse_diagonal(r["yrc"], 1, r["ydg"])
                    dve.wait_ge(r["yrs"], 1)
                    ssd_norm(range(0, 2))
                else:
                    taps(0, 3, t + 1)
                dve.wait_ge(r["o_high"], t + 1)
                TT(tile_of(ML, t), bank[7][:, :], tile_of(MH, t).bitcast(F32), ALU.subtract).then_inc(r["o_low"], 1)
                if is_last:
                    ssd_norm(range(2, KD))

            with dve.Fori(0, 3) as t:
                pair(t, False)
            pair(3, True)
            low_of_mix(40)

            clear_ss(CLEAR[4])
            for m in range(KD):
                if m % 2:
                    dve.wait_ge(unit_done, U_OUT2 + 12 * (m + 1) // BLOCKS)
                else:
                    dve.wait_ge(r["yms"], m // 2 + 2)
                x = tile_of(XT, m)
                STT(x, bank[m % 4][:, :], one[:, :], x, ALU.mult, ALU.add).then_inc(res_done, 1)
                dve.wait_ge(res_done, 8 * 4 + m + 1)
                if m % 4 == 3:
                    TT(CG[:, m // 4, :], x, x, ALU.mult).then_inc(sq_done, 1)
                    continue
                TT(SQ[:, :], x, x, ALU.mult).then_inc(sq_done, 1)
                dve.wait_ge(sq_done, SQ_BEFORE[4] + m + 1)
                TT(SS[:, :], SS[:, :], SQ[:, :], ALU.add).then_inc(ss_done, 1)
                dve.wait_ge(ss_done, SS_BEFORE[4] + m + 1 - m // 4)
            norm(4, lambda k: v("ffn2_norm_2", k), 48)
            ffn(U_UPB, NJ1 + NJ2)
            residual(5, U_DNB, 3, lambda m: 0.5, 4)
            inverse(5)
            dve.wait_ge(rs_done, 6)
            for k in range(KD):
                STT(tile_of(XT, k), tile_of(XT, k), v("final_norm_2", k), bank[SUM_BANK[5]][:, :], ALU.mult, ALU.mult).then_inc(h_mul, 1)


def _blocks(w):
    k, m = w.shape
    return w.reshape(k // P, P, m // P, P).transpose(2, 0, 1, 3).reshape(-1, P, P)


def _units(blocks):
    pad = -len(blocks) % BLOCKS
    if pad:
        blocks = np.concatenate([blocks, np.zeros((pad, P, P), np.float32)])
    return blocks.reshape(-1, BLOCKS, P, P).transpose(0, 2, 1, 3).reshape(-1, P, UNIT)


def _down(w, nj):
    b = _blocks(w).reshape(KD, nj, P, P)
    full = np.zeros((KD, 3 * BLOCKS, P, P), np.float32)
    full[:, :nj] = b
    return _units(full.reshape(-1, P, P))


def lay_out(a):
    w = {k: np.asarray(x)[0] if k not in ("x", "c", "final_norm_2") else np.asarray(x) for k, x in a.items()}
    ada = _units(_blocks(w["ada_w"]))
    win = _units(_blocks(w["w_in"])).reshape(7, HEADS, P, UNIT)
    parts = [ada[:RING]]
    beside = ada[RING:ADA_FIRST].transpose(1, 0, 2).reshape(P, -1)
    for h in range(HEADS):
        gates = np.zeros((BLOCKS, P, P), np.float32)
        gates[0], gates[1] = w["rg_wa"][h], w["rg_wx"][h]
        of = {XR: 0, YR: 1, Q: 2, K: 3, V: 4, GA: 5, GB: 6}
        for loc in range(HEAD_UNITS):
            if loc in of:
                parts.append(win[of[loc], h:h + 1])
            elif loc == GATES:
                parts.append(_units(gates))
            else:
                m = ADA_FIRST + 4 * h + HEAD_ADA.index(loc)
                parts.append(ada[m:m + 1])
    parts.append(_units(_blocks(w["w_out"])))
    up = _units(_blocks(w["ffn_up"])).reshape(2, NJ1, P, UNIT)
    parts += [up.transpose(1, 0, 2, 3).reshape(-1, P, UNIT), _down(w["ffn_down"], NJ1)]

    def ffn2(n):
        both = np.stack([_units(_blocks(w[f"ffn{n}_w_gate_2"])), _units(_blocks(w[f"ffn{n}_w_up_2"]))], 1)
        return [both.reshape(-1, P, UNIT), _down(w[f"ffn{n}_w_down_2"], NJ2)]
    parts += ffn2(1)
    w2 = w["w_in_2"]
    z, xbc, dt, qkv = w2[:, :1024], w2[:, 1024:2560], w2[:, 2560:2576], w2[:, 2576:]
    z, xbc, qkv = (_units(_blocks(np.ascontiguousarray(y))) for y in (z, xbc, qkv))
    dtp = np.zeros((D, P), np.float32)
    dtp[:, :16] = dt
    parts += [xbc[8:12], _units(_blocks(dtp))]
    rel = np.clip(np.arange(P)[:, None] - (np.arange(S)[None, :] - 384), -256, 256) + 256
    bias = w["rel_bias_2"][:, rel]
    for t in range(4):
        b = bias[2 * t:2 * t + 2].transpose(1, 0, 2).reshape(1, P, UNIT)
        parts += [xbc[t:t + 1], z[t:t + 1], qkv[t:t + 1], qkv[4 + t:5 + t], xbc[4 + t:5 + t],
                  qkv[8 + t:9 + t], z[4 + t:5 + t], b]
    w_out = _blocks(w["w_out_2"]).reshape(KD, 12, P, P)
    parts.append(_units(np.concatenate([w_out[:, KD:], w_out[:, :KD]], 1).reshape(-1, P, P)))
    parts += ffn2(2)
    stream = np.concatenate(parts)
    assert stream.shape == (N_UNITS, P, UNIT), stream.shape

    def cols(x):
        return x.reshape(-1, P).T
    small = dict(w)
    small["d_skip_2"] = np.repeat(w["d_skip_2"], 64)
    for n in ("dt_bias_2", "a_log_2"):
        small[n] = np.concatenate([w[n], np.zeros(P - 16, np.float32)])
    vec = np.concatenate([cols(small[n]) for n, _ in VEC_SIZES], 1)
    assert vec.shape == (P, N_VEC), vec.shape
    x = w["x"][0].T.reshape(KD, P, S).transpose(1, 0, 2).reshape(P, KD * S)
    return {k: np.ascontiguousarray(y) for k, y in (("xt", x), ("vec", vec), ("ada", beside), ("stream", stream))}


def kernel(**inputs):
    import concourse.bacc as _bacc
    from concourse.bass_utils import run_bass_kernel_spmd as _run

    arrays = lay_out(inputs)
    nc = _bacc.Bacc("TRN2", target_bir_lowering=False, num_devices=1)
    args = [nc.dram_tensor("in_" + n, a.shape, F32, kind="ExternalInput").ap() for n, a in arrays.items()]
    out = nc.dram_tensor("result", (P, KD * S), F32, kind="ExternalOutput").ap()
    program(nc, *args, out)
    got = _run(nc, [{"in_" + n: a for n, a in arrays.items()}], core_ids=[0]).results[0]["result"]
    return np.ascontiguousarray(got.reshape(P, KD, S).transpose(2, 1, 0).reshape(1, S, D))
```
